# Optimizing a Trainium2 kernel written in Bass

```python
import jax, jax.numpy as jnp
from jax import lax
import numpy as np

D_MODEL = 1024
BATCH = 1
SEQ = 512
DEPTH = 2

HEAD_DIM = 64
ROPE_THETA = 10000.0
NORM_EPS = 1e-6
BLOCK = 128

A_HEADS = 6
IDX_HEADS = 8
IDX_DIM = 64
TOPK_MAX = 256

B_GROUPS = ((128, 1), (512, 4), (2048, 16))
B_HEADS_PER_GROUP = 4
B_HEADS = B_HEADS_PER_GROUP * len(B_GROUPS)

C_HEADS = 8
C_KV_HEADS = 2
C_WINDOW = 128

N_BRANCHES = 3
D_FF = 4 * D_MODEL

IN_WIDTHS = (A_HEADS * HEAD_DIM, HEAD_DIM, HEAD_DIM,
             IDX_HEADS * IDX_DIM, IDX_DIM, IDX_HEADS,
             B_HEADS * HEAD_DIM, B_HEADS * HEAD_DIM, B_HEADS * HEAD_DIM,
             C_HEADS * HEAD_DIM, C_KV_HEADS * HEAD_DIM, C_KV_HEADS * HEAD_DIM,
             N_BRANCHES * D_MODEL)
IN_WIDTH = sum(IN_WIDTHS)


def rmsnorm(x, g):
    xf = x.astype(jnp.float32)
    y = xf * lax.rsqrt(jnp.mean(xf * xf, axis=-1, keepdims=True) + NORM_EPS)
    return (y * g.astype(jnp.float32)).astype(x.dtype)

def rope(x, pos):
    half = x.shape[-1] // 2
    inv = ROPE_THETA ** (-jnp.arange(half, dtype=jnp.float32) / half)
    ang = pos.astype(jnp.float32)[..., None] * inv
    cos = jnp.cos(ang)[:, :, None, :].astype(x.dtype)
    sin = jnp.sin(ang)[:, :, None, :].astype(x.dtype)
    x1, x2 = x[..., :half], x[..., half:]
    return jnp.concatenate([x1 * cos - x2 * sin, x2 * cos + x1 * sin], axis=-1)

def split_columns(z):
    parts, off = [], 0
    for w in IN_WIDTHS:
        parts.append(z[..., off:off + w])
        off += w
    return parts

def over_query_blocks(fn, seq_len):
    starts = jnp.arange(seq_len // BLOCK, dtype=jnp.int32) * BLOCK
    out = lax.map(fn, starts)
    out = jnp.moveaxis(out, 0, 1)
    return out.reshape(out.shape[0], seq_len, *out.shape[3:])

def dsa_attention(q, k, v, iq, ik, iw):
    L = q.shape[1]
    topk = min(TOPK_MAX, L // 4)
    scale = HEAD_DIM ** -0.5
    idx_scale = IDX_DIM ** -0.5
    s_all = jnp.arange(L)

    def block(t0):
        t = t0 + jnp.arange(BLOCK)
        qb = lax.dynamic_slice_in_dim(q, t0, BLOCK, 1)
        iqb = lax.dynamic_slice_in_dim(iq, t0, BLOCK, 1)
        iwb = lax.dynamic_slice_in_dim(iw, t0, BLOCK, 1).astype(jnp.float32)
        rel = jax.nn.relu(jnp.einsum('bqhd,bsd->bqhs', iqb, ik).astype(jnp.float32) * idx_scale)
        score = jnp.einsum('bqh,bqhs->bqs', iwb, rel)
        causal = s_all[None, :] <= t[:, None]
        score = jnp.where(causal[None], score, -jnp.inf)
        _, idx = lax.top_k(score, topk)
        ks = jax.vmap(lambda kk, ii: kk[ii])(k, idx)
        vs = jax.vmap(lambda vv, ii: vv[ii])(v, idx)
        valid = idx <= t[None, :, None]
        logits = jnp.einsum('bqhd,bqkd->bqhk', qb, ks).astype(jnp.float32) * scale
        logits = jnp.where(valid[:, :, None, :], logits, -jnp.inf)
        p = jax.nn.softmax(logits, axis=-1)
        return jnp.einsum('bqhk,bqkd->bqhd', p.astype(vs.dtype), vs)

    return over_query_blocks(block, L)

def dilated_attention(q, k, v):
    L = q.shape[1]
    scale = HEAD_DIM ** -0.5
    hg = B_HEADS_PER_GROUP
    qs = [q[:, :, g * hg:(g + 1) * hg] for g in range(len(B_GROUPS))]
    kss = [k[:, :, g * hg:(g + 1) * hg] for g in range(len(B_GROUPS))]
    vss = [v[:, :, g * hg:(g + 1) * hg] for g in range(len(B_GROUPS))]

    def block(t0):
        t = t0 + jnp.arange(BLOCK)
        outs, lses = [], []
        for g, (window, dil) in enumerate(B_GROUPS):
            qb = lax.dynamic_slice_in_dim(qs[g], t0, BLOCK, 1)
            pos = t[:, None] - dil * jnp.arange(window // dil + 1)[None, :]
            valid = pos >= 0
            pos_c = jnp.maximum(pos, 0)
            kg = kss[g][:, pos_c]
            vg = vss[g][:, pos_c]
            logits = jnp.einsum('bqhd,bqkhd->bqhk', qb, kg).astype(jnp.float32) * scale
            logits = jnp.where(valid[None, :, None, :], logits, -jnp.inf)
            m = jnp.max(logits, axis=-1, keepdims=True)
            e = jnp.exp(logits - m)
            den = jnp.sum(e, axis=-1)
            o = jnp.einsum('bqhk,bqkhd->bqhd', (e / den[..., None]).astype(vg.dtype), vg)
            outs.append(o)
            lses.append(m[..., 0] + jnp.log(den))
        alpha = jax.nn.softmax(jnp.stack(lses, 0), axis=0)
        return jnp.einsum('gbqh,gbqhd->bqhd', alpha.astype(outs[0].dtype), jnp.stack(outs, 0))

    return over_query_blocks(block, L)

def sink_window_attention(q, k, v, sinks):
    Bsz, L = q.shape[0], q.shape[1]
    grp = C_HEADS // C_KV_HEADS
    scale = HEAD_DIM ** -0.5
    pad = ((0, 0), (BLOCK, 0), (0, 0), (0, 0))
    kp = jnp.pad(k, pad)
    vp = jnp.pad(v, pad)
    qg = q.reshape(Bsz, L, C_KV_HEADS, grp, HEAD_DIM)
    sink = sinks.astype(jnp.float32).reshape(C_KV_HEADS, grp)[:, :, None, None]

    def block(t0):
        t = t0 + jnp.arange(BLOCK)
        s = t0 - BLOCK + jnp.arange(2 * BLOCK)
        qb = lax.dynamic_slice_in_dim(qg, t0, BLOCK, 1)
        kb = lax.dynamic_slice_in_dim(kp, t0, 2 * BLOCK, 1)
        vb = lax.dynamic_slice_in_dim(vp, t0, 2 * BLOCK, 1)
        mask = (s[None, :] <= t[:, None]) & (s[None, :] > t[:, None] - C_WINDOW) & (s[None, :] >= 0)
        logits = jnp.einsum('bqkgd,bskd->bkgqs', qb, kb).astype(jnp.float32) * scale
        logits = jnp.where(mask, logits, -jnp.inf)
        m = jnp.maximum(jnp.max(logits, axis=-1, keepdims=True), sink)
        e = jnp.exp(logits - m)
        den = jnp.sum(e, axis=-1, keepdims=True) + jnp.exp(sink - m)
        p = (e / den).astype(vb.dtype)
        o = jnp.einsum('bkgqs,bskd->bqkgd', p, vb)
        return o.reshape(Bsz, BLOCK, C_HEADS, HEAD_DIM)

    return over_query_blocks(block, L)

def hybrid_mixer(u, pos, w_in, idx_k_norm, sinks, w_a, w_b, w_c, w_o):
    Bsz, L, _ = u.shape
    (aq, ak, av, iq, ik, iw, bq, bk, bv, cq, ck, cv, gates) = split_columns(u @ w_in)
    qa = rope(aq.reshape(Bsz, L, A_HEADS, HEAD_DIM), pos)
    ka = rope(ak[:, :, None, :], pos)[:, :, 0]
    iqr = rope(iq.reshape(Bsz, L, IDX_HEADS, IDX_DIM), pos)
    ikr = rope(rmsnorm(ik, idx_k_norm)[:, :, None, :], pos)[:, :, 0]
    o_a = dsa_attention(qa, ka, av, iqr, ikr, iw * IDX_HEADS ** -0.5)
    o_b = dilated_attention(rope(bq.reshape(Bsz, L, B_HEADS, HEAD_DIM), pos),
                            rope(bk.reshape(Bsz, L, B_HEADS, HEAD_DIM), pos),
                            bv.reshape(Bsz, L, B_HEADS, HEAD_DIM))
    o_c = sink_window_attention(rope(cq.reshape(Bsz, L, C_HEADS, HEAD_DIM), pos),
                                rope(ck.reshape(Bsz, L, C_KV_HEADS, HEAD_DIM), pos),
                                cv.reshape(Bsz, L, C_KV_HEADS, HEAD_DIM), sinks)
    g = jax.nn.sigmoid(gates.reshape(Bsz, L, N_BRANCHES, D_MODEL))
    merged = (g[:, :, 0] * (o_a.reshape(Bsz, L, -1) @ w_a)
              + g[:, :, 1] * (o_b.reshape(Bsz, L, -1) @ w_b)
              + g[:, :, 2] * (o_c.reshape(Bsz, L, -1) @ w_c))
    return merged @ w_o

def first_inputs(seed: int = 0) -> dict:
    key = jax.random.key(seed)
    ks = jax.random.split(key, 15)

    def normal(k, shape, scale):
        return jax.random.normal(k, shape, jnp.float32) * scale

    def gain(k, shape):
        return 1.0 + 0.05 * jax.random.normal(k, shape, jnp.float32)

    x = normal(ks[0], (BATCH, SEQ, D_MODEL), 1.0)
    positions = jnp.tile(jnp.arange(SEQ, dtype=jnp.int32)[None, :], (BATCH, 1))
    return {
        "x": x,
        "positions": positions,
        "attn_norm": gain(ks[1], (DEPTH, D_MODEL)),
        "w_in": normal(ks[2], (DEPTH, D_MODEL, IN_WIDTH), D_MODEL ** -0.5),
        "idx_k_norm": gain(ks[3], (DEPTH, IDX_DIM)),
        "sinks": normal(ks[4], (DEPTH, C_HEADS), 0.5),
        "w_a": normal(ks[5], (DEPTH, A_HEADS * HEAD_DIM, D_MODEL), (A_HEADS * HEAD_DIM) ** -0.5),
        "w_b": normal(ks[6], (DEPTH, B_HEADS_PER_GROUP * HEAD_DIM, D_MODEL), (B_HEADS_PER_GROUP * HEAD_DIM) ** -0.5),
        "w_c": normal(ks[7], (DEPTH, C_HEADS * HEAD_DIM, D_MODEL), (C_HEADS * HEAD_DIM) ** -0.5),
        "w_o": normal(ks[8], (DEPTH, D_MODEL, D_MODEL), D_MODEL ** -0.5),
        "mlp_norm": gain(ks[9], (DEPTH, D_MODEL)),
        "w_up": normal(ks[10], (DEPTH, D_MODEL, D_FF), D_MODEL ** -0.5),
        "w_down": normal(ks[11], (DEPTH, D_FF, D_MODEL), D_FF ** -0.5),
        "final_norm": gain(ks[12], (D_MODEL,)),
    }

def first_block(x, positions, attn_norm, w_in, idx_k_norm, sinks, w_a, w_b, w_c, w_o,
              mlp_norm, w_up, w_down, final_norm):
    h = x
    for l in range(DEPTH):
        u = rmsnorm(h, attn_norm[l])
        h = h + hybrid_mixer(u, positions, w_in[l], idx_k_norm[l], sinks[l],
                             w_a[l], w_b[l], w_c[l], w_o[l])
        u = rmsnorm(h, mlp_norm[l])
        h = h + jnp.square(jax.nn.relu(u @ w_up[l])) @ w_down[l]
    return rmsnorm(h, final_norm)


CTX_LEN = 256
GRID_W = 64

FOURIER_WIDTH = D_MODEL // 4
N_FOURIER_HEADS = 4
FOURIER_HEAD_DIM = FOURIER_WIDTH // N_FOURIER_HEADS

V_HEAD_DIM = 64
QK_NOPE_DIM = 64
QK_ROPE_DIM = 32
QK_HEAD_DIM = QK_NOPE_DIM + QK_ROPE_DIM
N_MLA_HEADS = (D_MODEL - FOURIER_WIDTH) // V_HEAD_DIM
MLA_WIDTH = N_MLA_HEADS * V_HEAD_DIM
Q_LORA_RANK = 384
KV_LORA_RANK = 128

MIX_WIDTH = FOURIER_WIDTH + MLA_WIDTH
IN_PROJ_WIDTH = FOURIER_WIDTH + Q_LORA_RANK + KV_LORA_RANK + QK_ROPE_DIM

D_FF_2 = 2816
CONV_WIDTH = 3

Q_BLOCK = 128
SOFTMAX_SCALE = QK_HEAD_DIM ** -0.5
N_MOD = 6


def rms_norm(x, g):
    xf = x.astype(jnp.float32)
    y = xf * lax.rsqrt(jnp.mean(xf * xf, axis=-1, keepdims=True) + NORM_EPS)
    return (y * g.astype(jnp.float32)).astype(x.dtype)

def modulate(h, shift, scale):
    return h * (1 + scale) + shift

def axial_rope_tables(rows, dtype):
    row_ids = jnp.broadcast_to(jnp.arange(rows)[:, None], (rows, GRID_W)).reshape(-1).astype(jnp.float32)
    col_ids = jnp.broadcast_to(jnp.arange(GRID_W)[None, :], (rows, GRID_W)).reshape(-1).astype(jnp.float32)
    n_freq = QK_ROPE_DIM // 4
    inv_freq = ROPE_THETA ** (-jnp.arange(n_freq, dtype=jnp.float32) / n_freq)
    ang = jnp.concatenate([row_ids[:, None] * inv_freq, col_ids[:, None] * inv_freq], axis=-1)
    return jnp.cos(ang).astype(dtype), jnp.sin(ang).astype(dtype)

def apply_rope(x, cos, sin):
    x1, x2 = jnp.split(x, 2, axis=-1)
    return jnp.concatenate([x1 * cos - x2 * sin, x2 * cos + x1 * sin], axis=-1)

def fourier_mix(u, w_f, b_f):
    b, n, _ = u.shape
    uh = u.reshape(b, n, N_FOURIER_HEADS, FOURIER_HEAD_DIM).astype(jnp.float32)
    f = jnp.fft.fft2(uh, axes=(1, 3), norm="ortho").real
    f = f.reshape(b, n, FOURIER_WIDTH).astype(u.dtype)
    return f @ w_f + b_f

def mla_q(c_q, g_q, w_q_b, cos, sin):
    b, n, _ = c_q.shape
    q = (rms_norm(c_q, g_q) @ w_q_b).reshape(b, n, N_MLA_HEADS, QK_HEAD_DIM)
    q_nope, q_rope = q[..., :QK_NOPE_DIM], q[..., QK_NOPE_DIM:]
    if cos is not None:
        q_rope = apply_rope(q_rope, cos[:, None, :], sin[:, None, :])
    return q_nope, q_rope

def mla_kv(c_kv, k_rope, g_kv, w_kv_b, cos, sin):
    b, n, _ = c_kv.shape
    kv = (rms_norm(c_kv, g_kv) @ w_kv_b).reshape(b, n, N_MLA_HEADS, QK_NOPE_DIM + V_HEAD_DIM)
    k_nope, v = kv[..., :QK_NOPE_DIM], kv[..., QK_NOPE_DIM:]
    if cos is not None:
        k_rope = apply_rope(k_rope, cos, sin)
    return k_nope, k_rope, v

def mla_attend(q_nope, q_rope, k_nope, k_rope, v):
    s = jnp.einsum('bqhd,bkhd->bhqk', q_nope, k_nope) + jnp.einsum('bqhr,bkr->bhqk', q_rope, k_rope)
    p = jax.nn.softmax(s.astype(jnp.float32) * SOFTMAX_SCALE, axis=-1).astype(v.dtype)
    return jnp.einsum('bhqk,bkhd->bqhd', p, v)

def blocked_attention(q_nope, q_rope, k_nope, k_rope, v):
    b, n, h, _ = q_nope.shape
    nb = n // Q_BLOCK
    qn = q_nope.reshape(b, nb, Q_BLOCK, h, QK_NOPE_DIM).transpose(1, 0, 2, 3, 4)
    qr = q_rope.reshape(b, nb, Q_BLOCK, h, QK_ROPE_DIM).transpose(1, 0, 2, 3, 4)
    out = lax.map(lambda blk: mla_attend(blk[0], blk[1], k_nope, k_rope, v), (qn, qr))
    return out.transpose(1, 0, 2, 3, 4).reshape(b, n, h * V_HEAD_DIM)

def split_in_proj(p):
    f_in = p[..., :FOURIER_WIDTH]
    c_q = p[..., FOURIER_WIDTH:FOURIER_WIDTH + Q_LORA_RANK]
    c_kv = p[..., FOURIER_WIDTH + Q_LORA_RANK:FOURIER_WIDTH + Q_LORA_RANK + KV_LORA_RANK]
    k_rope = p[..., FOURIER_WIDTH + Q_LORA_RANK + KV_LORA_RANK:]
    return f_in, c_q, c_kv, k_rope

def conv_ffn(h, w_up, w_dw, b_dw, w_down):
    u = h @ w_up
    u = lax.conv_general_dilated(u, w_dw[:, None, :], window_strides=(1,),
                                 padding=((CONV_WIDTH // 2, CONV_WIDTH // 2),),
                                 dimension_numbers=('NWC', 'WIO', 'NWC'),
                                 feature_group_count=2 * D_FF_2) + b_dw
    gate, val = jnp.split(u, 2, axis=-1)
    return (jax.nn.silu(gate) * val) @ w_down

def second_inputs(seed: int = 0) -> dict:
    key = jax.random.key(seed)
    ks = jax.random.split(key, 24)
    f32 = jnp.float32

    def nrm(k, shape, scale):
        return jax.random.normal(k, shape, f32) * scale

    def gain(k, shape):
        return 1.0 + 0.02 * jax.random.normal(k, shape, f32)

    L, D = DEPTH, D_MODEL
    return {
        "x": jax.random.normal(ks[0], (BATCH, SEQ, D), f32),
        "c": jax.random.normal(ks[1], (BATCH, D), f32),
        "ctx": jax.random.normal(ks[2], (BATCH, CTX_LEN, D), f32),
        "c_ctx": jax.random.normal(ks[3], (D,), f32),
        "w_ada": nrm(ks[4], (L, D, N_MOD * D), 0.5 * D ** -0.5),
        "b_ada": nrm(ks[5], (L, N_MOD * D), 0.02),
        "g_mix": gain(ks[6], (L, D)),
        "w_in": nrm(ks[7], (L, D, IN_PROJ_WIDTH), D ** -0.5),
        "w_fourier": nrm(ks[8], (L, FOURIER_WIDTH, FOURIER_WIDTH), FOURIER_WIDTH ** -0.5),
        "b_fourier": nrm(ks[9], (L, FOURIER_WIDTH), 0.02),
        "g_q_a": gain(ks[10], (L, Q_LORA_RANK)),
        "w_q_b": nrm(ks[11], (L, Q_LORA_RANK, N_MLA_HEADS * QK_HEAD_DIM), Q_LORA_RANK ** -0.5),
        "g_kv_a": gain(ks[12], (L, KV_LORA_RANK)),
        "w_kv_b": nrm(ks[13], (L, KV_LORA_RANK, N_MLA_HEADS * (QK_NOPE_DIM + V_HEAD_DIM)), KV_LORA_RANK ** -0.5),
        "w_out": nrm(ks[14], (L, MIX_WIDTH, D), MIX_WIDTH ** -0.5),
        "g_ffn": gain(ks[15], (L, D)),
        "w_up": nrm(ks[16], (L, D, 2 * D_FF_2), D ** -0.5),
        "w_dw": nrm(ks[17], (L, CONV_WIDTH, 2 * D_FF_2), CONV_WIDTH ** -0.5),
        "b_dw": nrm(ks[18], (L, 2 * D_FF_2), 0.02),
        "w_down": nrm(ks[19], (L, D_FF_2, D), D_FF_2 ** -0.5),
        "g_final": gain(ks[20], (D,)),
    }

def second_block(x, c, ctx, c_ctx, w_ada, b_ada, g_mix, w_in, w_fourier, b_fourier,
              g_q_a, w_q_b, g_kv_a, w_kv_b, w_out, g_ffn, w_up, w_dw, b_dw, w_down, g_final):
    b, n_lat, _ = x.shape
    ROWS = n_lat // GRID_W
    cos, sin = axial_rope_tables(ROWS, x.dtype)
    silu_c = jax.nn.silu(c)
    silu_cc = jax.nn.silu(c_ctx)

    for l in range(DEPTH):
        last = l == DEPTH - 1
        mod_lat = (silu_c @ w_ada[l] + b_ada[l])[:, None, :]
        mod_ctx = silu_cc @ w_ada[l] + b_ada[l]
        sh1, sc1, gt1, sh2, sc2, gt2 = jnp.split(mod_lat, N_MOD, axis=-1)
        csh1, csc1, cgt1, csh2, csc2, cgt2 = jnp.split(mod_ctx, N_MOD, axis=-1)

        h = modulate(rms_norm(x, g_mix[l]), sh1, sc1)
        hc = modulate(rms_norm(ctx, g_mix[l]), csh1, csc1)
        f_in, c_q, c_kv, k_rope_raw = split_in_proj(h @ w_in[l])
        f_in_c, c_q_c, c_kv_c, k_rope_raw_c = split_in_proj(hc @ w_in[l])

        kn_c, kr_c, v_c = mla_kv(c_kv_c, k_rope_raw_c, g_kv_a[l], w_kv_b[l], None, None)
        kn_l, kr_l, v_l = mla_kv(c_kv, k_rope_raw, g_kv_a[l], w_kv_b[l], cos, sin)
        qn_l, qr_l = mla_q(c_q, g_q_a[l], w_q_b[l], cos, sin)

        k_nope_all = jnp.concatenate([kn_l, kn_c], axis=1)
        k_rope_all = jnp.concatenate([kr_l, kr_c], axis=1)
        v_all = jnp.concatenate([v_l, v_c], axis=1)
        att_l = blocked_attention(qn_l, qr_l, k_nope_all, k_rope_all, v_all)
        four_l = fourier_mix(f_in, w_fourier[l], b_fourier[l])
        mix_l = jnp.concatenate([four_l, att_l], axis=-1) @ w_out[l]
        x = x + gt1 * mix_l

        x = x + gt2 * conv_ffn(modulate(rms_norm(x, g_ffn[l]), sh2, sc2),
                               w_up[l], w_dw[l], b_dw[l], w_down[l])

        if not last:
            qn_c, qr_c = mla_q(c_q_c, g_q_a[l], w_q_b[l], None, None)
            att_c = mla_attend(qn_c, qr_c, kn_c, kr_c, v_c).reshape(b, -1, MLA_WIDTH)
            four_c = fourier_mix(f_in_c, w_fourier[l], b_fourier[l])
            mix_c = jnp.concatenate([four_c, att_c], axis=-1) @ w_out[l]
            ctx = ctx + cgt1 * mix_c
            ctx = ctx + cgt2 * conv_ffn(modulate(rms_norm(ctx, g_ffn[l]), csh2, csc2),
                                        w_up[l], w_dw[l], b_dw[l], w_down[l])

    return rms_norm(x, g_final)


def setup_inputs(seed=0):
    out = dict(first_inputs(seed))
    for name, value in second_inputs(seed + 1).items():
        if name != "x":
            out[name + "_2"] = value
    return out


def reference(
    x, positions, attn_norm, w_in, idx_k_norm, sinks, w_a, w_b, w_c, w_o, mlp_norm, w_up,
    w_down, final_norm, c_2, ctx_2, c_ctx_2, w_ada_2, b_ada_2, g_mix_2, w_in_2, w_fourier_2,
    b_fourier_2, g_q_a_2, w_q_b_2, g_kv_a_2, w_kv_b_2, w_out_2, g_ffn_2, w_up_2, w_dw_2, b_dw_2,
    w_down_2, g_final_2,
):
    x = first_block(
        x, positions, attn_norm, w_in, idx_k_norm, sinks, w_a, w_b, w_c, w_o, mlp_norm, w_up,
        w_down, final_norm,
    )
    return second_block(
        x, c_2, ctx_2, c_ctx_2, w_ada_2, b_ada_2, g_mix_2, w_in_2, w_fourier_2, b_fourier_2,
        g_q_a_2, w_q_b_2, g_kv_a_2, w_kv_b_2, w_out_2, g_ffn_2, w_up_2, w_dw_2, b_dw_2,
        w_down_2, g_final_2,
    )


_drawn_inputs = setup_inputs


def setup_inputs(seed=0):
    import zlib

    import numpy as np

    out = dict(_drawn_inputs(seed))
    spreads = {}
    factors = {'idx_k_norm': 3.43,
     'sinks': 8.0,
     'ctx_2': 3.958,
     'g_mix_2': 8.0,
     'b_fourier_2': 8.0,
     'g_q_a_2': 8.0,
     'g_kv_a_2': 8.0,
     'g_ffn_2': 6.681,
     'b_dw_2': 6.765,
     'g_final_2': 2.822}
    for name, (base, spread) in spreads.items():
        noise = np.random.default_rng([zlib.crc32(name.encode()), seed]).standard_normal(out[name].shape)
        drawn = base * np.exp(spread * noise) if base else spread * noise
        out[name] = __import__('jax').numpy.asarray(drawn.astype(out[name].dtype))
    for name, factor in factors.items():
        out[name] = (out[name] * factor).astype(out[name].dtype)
    return out
```

```python
from contextlib import ExitStack

import numpy as np

import concourse.bass as bass
from concourse import mybir

P = 128
F32 = mybir.dt.float32
F32R = mybir.dt.float32r
I32 = mybir.dt.int32
ACT = mybir.ActivationFunctionType
ALU = mybir.AluOpType
AX = mybir.AxisListType

D = 1024
KT = D // P
T = 512
QB = T // P
DEPTH = 2
HD = 64
EPS = 1e-6
NEG = -1e30
TAKEN = -3e38
TOPK = 128
SLAB = 2048
TWO_PI = 2.0 * np.pi
ROUND = 1.5 * 2.0 ** 23

A_HEADS, IDX_HEADS, B_HPG, C_HEADS = 6, 8, 4, 8
COL_AQ = 0
COL_AK = COL_AQ + A_HEADS * HD
COL_IQ = COL_AK + 2 * HD
COL_IK = COL_IQ + IDX_HEADS * HD
COL_BQ = COL_IK + HD + IDX_HEADS
COL_BV = COL_BQ + 2 * 3 * B_HPG * HD
COL_CQ = COL_BV + 3 * B_HPG * HD
COL_CK = COL_CQ + C_HEADS * HD
COL_CV = COL_CK + 2 * HD
COL_G = COL_CV + 2 * HD
D_FF = 4 * D

SL_A, SL_B, SL_BV, SL_C, SL_ADA, SL_MERGE, SL_WO, SL_MLP, SLABS1 = 0, 5, 11, 14, 18, 42, 62, 66, 98
ADA_SLABS = SL_MERGE - SL_ADA
TL_A, TL_B, TL_BV, TL_C, TL_MERGE, TL_WO, TL_MLP, TILES1 = 0, 17, 29, 41, 50, 98, 106, 170
FR_A, FR_B, FR_BV, FR_C, FR_MERGE, FR_WO, FR_MLP, FREES1 = 0, 17, 29, 41, 50, 74, 82, 148
RP_A, RP_B, RP_IK, RP_C, ROPES1 = 0, 8, 20, 21, 26
IT_IDX = 0
IT_A = IT_IDX + (QB - 1) * IDX_HEADS
IT_B = IT_A + QB * A_HEADS
IT_C = IT_B + QB * B_HPG
ITEMS1 = IT_C + QB * C_HEADS
SX_A, SX_B, SX_C, SOFTS1 = 0, QB * A_HEADS, QB * (A_HEADS + B_HPG), QB * (A_HEADS + B_HPG + C_HEADS)
GROUPS1 = 3 * QB
NORMS1 = 2

M_CAUSAL = 0
M_C = M_CAUSAL + 512
M_B0 = M_C + 256
M_B1 = M_B0 + 256
M_B2 = M_B1 + 512
MASKS = M_B2 + 512


def shape_constants():
    q = np.arange(P)[:, None]
    s = np.arange(P)[None, :]
    ok = lambda m: np.where(m, 0.0, NEG).astype(np.float32)
    causal = ok(s <= q)
    free = np.zeros((P, 3 * P), np.float32)
    parts = [free, causal, ok(s > q), causal, ok(s >= q), causal]
    for dilation in (4, 16):
        near = (q - s) % dilation == 0
        parts += [ok(near)] * 3 + [ok(near & (s <= q))]
    masks = np.concatenate(parts, axis=1)
    half = HD // 2
    inv = (np.float32(10000.0) ** (-np.arange(half, dtype=np.float32) / np.float32(half))).astype(np.float32)
    inv = np.tile(inv, 4)[:, None]
    sign = np.where((np.arange(P) // half) % 2 == 0, -1.0, 1.0).astype(np.float32)[:, None]
    ident = np.eye(P, dtype=np.float32)
    ones = np.ones((P, P), np.float32)
    return {"c_masks": masks, "c_ident": np.concatenate([ident, ones, inv, sign], axis=1)}

TC = 256
TA = T + TC
KH, QH, RH, VH = 12, 96, 32, 64
HG = 4
FQ, FKV = 384, 128
FF2 = 2816
SM = QH ** -0.5
S2_WIN, S2_HG, S2_FOUR, S2_WOUT, S2_FFN, SLABS2 = 0, 4, 10, 12, 16, 50
FFN_CHUNKS = ((0, 8, 16), (8, 8, 28), (16, 6, 40))
TILE_BASE2 = DEPTH * TILES1
FREE_OFF = DEPTH * (TILES1 - FREES1)
SLAB_BASE2 = DEPTH * SLABS1
SLABS_ALL = DEPTH * (SLABS1 + SLABS2)


def tiles2(l):
    sides = 2 if l == 0 else 1
    counts = [("win", 14 if l == 0 else 9), ("hg", 3 * (24 if l == 0 else 20)), ("four", 2 * sides),
              ("wout", 8 * sides)]
    for c, (_, pairs, _) in enumerate(FFN_CHUNKS):
        counts += [(f"up{c}", 2 * pairs * sides), (f"down{c}", 8 * sides)]
    base = TILE_BASE2 if l == 0 else tiles2(0)["end"]
    out = {}
    for name, n in counts:
        out[name] = base
        base += n
    out["end"] = base
    return out


def slab2(l, c, i=0, step=0):
    return slab_of(SLAB_BASE2 + l * SLABS2 + c, 0, 0, i, step)


def pieces(l, both=None):
    lat, con = (0, T, 0), (1, TC, T)
    return (lat, con) if (l == 0 if both is None else both) else (lat,)


def norms2():
    k, n, out = (DEPTH * NORMS1 + 1) * KT, DEPTH * NORMS1 + 1, {}
    for l in range(DEPTH):
        for name, kt, piece in [(f"mix{l}0", KT, 1), (f"mix{l}1", KT, 1), (f"q{l}0", 3, 1)] + (
                [("q01", 3, 1)] if l == 0 else []) + [(f"kv{l}0", 1, 1), (f"kv{l}1", 1, 1), (f"ffn{l}0", KT, 1)] + (
                [("ffn01", KT, 1)] if l == 0 else []):
            out[name] = (k, n)
            k += kt
            n += piece
    out["final"] = (k, n)
    return out


NORMS2 = norms2()
X_OFF = KT
GL_BASE = {0: 0, 1: 44}


def items2(l):
    return [(qb, j, 0) for qb in range(QB) for j in range(HG)] + (
        [(qb, j, 1) for qb in range(TC // P) for j in range(HG)] if l == 0 else [])


def item_base2(l):
    return 0 if l == 0 else 3 * len(items2(0))


def group_base2(l):
    return item_base2(l) // HG


C2 = {}
_at = 0
for _name, _n in (("b_ada", 2 * 96), ("g_mix", 32), ("g_ffn", 32), ("g_final", 8), ("b_f", 4), ("g_q", 6),
                  ("g_kv", 2), ("w_dw", 2 * 3 * 44), ("b_dw", 2 * 44)):
    C2[_name] = _at
    _at += _n
SMALL2 = _at


def shape_constants_2():
    n_freq = RH // 4
    inv = (np.float32(10000.0) ** (-np.arange(n_freq, dtype=np.float32) / np.float32(n_freq))).astype(np.float32)
    t = np.arange(T)
    rows, cols = (t // 64).astype(np.float32), (t % 64).astype(np.float32)
    ang = np.concatenate([rows[:, None] * inv, cols[:, None] * inv], axis=1).astype(np.float32)
    cos, sin = np.cos(ang.astype(np.float64)).T, np.sin(ang.astype(np.float64)).T
    table = np.zeros((P, T))
    table[64:96] = np.concatenate([cos, cos])
    table[96:128] = np.concatenate([-sin, sin])
    table = table.astype(np.float32)
    ropes = np.stack([table * np.float32(SM), table], axis=1)

    def dft(n, reps=1):
        a = 2.0 * np.pi * ((np.arange(n)[:, None] * np.arange(n)[None, :]) % n) / n
        return np.cos(a), np.sin(a)
    c64, s64 = dft(64)
    two = lambda a: np.kron(np.eye(2), a)
    chan = np.concatenate([two(c64), two(s64)], axis=1).astype(np.float32)
    pos = []
    for n in (T, TC):
        c, s_ = dft(n)
        scale = 1.0 / np.sqrt(n * 64.0)
        both = np.stack([c * scale, -s_ * scale], axis=1)
        pos.append(both.reshape(n // P, P, 2, n).transpose(1, 0, 2, 3).reshape(P, -1).astype(np.float32))
    return {"c_ropes": ropes.reshape(P, 2 * T), "c_dft": np.concatenate([chan, *pos], axis=1)}


class Names:
    pass


def place(nc, at, name, shape, dt=F32):
    return nc.alloc_sbuf_tensor_at(name, shape, dt, offset=at), (at + 4 * int(np.prod(shape[1:])) + 31) // 32 * 32


def slab_of(c, l=0, per_layer=0, i=0, step=0):
    return l * per_layer + c + i * step, c % 2, l * (per_layer // 2) + c // 2 + i * (step // 2)


def two_stacks(nc, io, out):
    m, s = Names(), Names()
    with ExitStack() as ctx:
        at = 16512
        m.hT, at = place(nc, at, "hT", [P, KT, T])
        m.wst, at = place(nc, at, "wst", [P, 2, SLAB])
        m.whi, at = place(nc, at, "whi", [P, 2, SLAB], F32R)
        m.wlo, at = place(nc, at, "wlo", [P, 2, SLAB], F32R)
        m.xh, at = place(nc, at, "xh", [P, KT, T], F32R)
        m.xl, at = place(nc, at, "xl", [P, KT, T], F32R)
        m.cst, at = place(nc, at, "cst", [P, 258])
        m.sm1, at = place(nc, at, "sm1", [P, 74])
        m.cs, at = place(nc, at, "cs", [P, KT, 2])
        m.mods, at = place(nc, at, "mods", [P, DEPTH, 6 * KT * 2])
        region = at
        m.cosT, at = place(nc, region, "cosT", [P, T])
        m.sinT, at = place(nc, at, "sinT", [P, T])
        m.masks, at = place(nc, at, "masks", [P, MASKS])
        a_area = at
        m.AQ, at = place(nc, at, "AQ", [P, 3, T])
        m.AK, at = place(nc, at, "AK", [P, T])
        m.IQ, at = place(nc, at, "IQ", [P, 4, T])
        m.IK, at = place(nc, at, "IK", [P, T])
        m.VA, at = place(nc, at, "VA", [P, QB, HD])
        m.IW, at = place(nc, at, "IW", [P, QB, IDX_HEADS])
        m.CQ, at = place(nc, at, "CQ", [P, 4, T])
        m.CK, at = place(nc, at, "CK", [P, T])
        m.VC, at = place(nc, at, "VC", [P, QB, 2 * HD])
        ma_area = at
        m.MA, at = place(nc, at, "MA", [P, 1152])
        m.ikraw, _ = place(nc, ma_area, "ikraw", [P, T])
        m.iknorm, _ = place(nc, ma_area + 2048, "iknorm", [P, T])
        m.OB, _ = place(nc, ma_area, "OB", [P, QB, 4 * HD])
        m.OC, _ = place(nc, a_area, "OC", [P, QB, 8 * HD])
        m.OA, _ = place(nc, a_area + 8192, "OA", [P, QB, 6 * HD])
        m.mh, _ = place(nc, a_area, "mh", [P, KT, T], F32R)
        m.ml, _ = place(nc, a_area + 16384, "ml", [P, KT, T], F32R)
        b_area = at
        assert a_area + 32768 <= b_area
        m.BQK, at = place(nc, at, "BQK", [P, 12, T])
        m.VB, at = place(nc, at, "VB", [P, QB, 12 * HD])
        m.oh, _ = place(nc, b_area, "oh", [P, 9, T], F32R)
        m.ol, _ = place(nc, b_area + 18432, "ol", [P, 9, T], F32R)
        m.uh, _ = place(nc, b_area, "uh", [P, KT, T], F32R)
        m.ul, _ = place(nc, b_area + 16384, "ul", [P, KT, T], F32R)
        work = at
        m.S, at = place(nc, at, "S", [P, 2, 1296])
        m.PT, at = place(nc, at, "PT", [P, 2, 1280])
        m.qs, at = place(nc, at, "qs", [P, 2, 3, P])
        m.den, at = place(nc, at, "den", [P, 2, 12])
        m.rden, at = place(nc, at, "rden", [P, 12])
        m.nmax, at = place(nc, at, "nmax", [P, 2])
        m.top8, at = place(nc, at, "top8", [P, 8])
        assert at <= 229344, at
        m.xs, _ = place(nc, work, "xs", [P, 2, T])
        m.xc, _ = place(nc, work + 4096, "xc", [P, T])
        m.R, _ = place(nc, work, "R", [P, 2, T])
        m.rows, _ = place(nc, work + 4096, "rows", [P, 2, 256])
        m.sg, _ = place(nc, work, "sg", [P, 6, T])
        m.mt, _ = place(nc, work + 12288, "mt", [P, 2, T])
        m.mtmp, _ = place(nc, work + 16384, "mtmp", [P, T])
        m.ur, _ = place(nc, work, "ur", [P, 2, T])
        m.us, _ = place(nc, work + 4096, "us", [P, 2, T])
        m.of, _ = place(nc, work + 8192, "of", [P, 2, T])
        m.sq, _ = place(nc, work + 10368, "sq", [P, 2, T])
        m.xn, _ = place(nc, work + 14464, "xn", [P, 2, T])
        m.rstd, _ = place(nc, work + 18560, "rstd", [P, T])
        m.posi, _ = place(nc, work, "posi", [P, T], I32)
        m.ang, _ = place(nc, work + 2048, "ang", [P, T])
        m.turns, _ = place(nc, work + 4096, "turns", [P, T])
        m.red, _ = place(nc, work + 6144, "red", [P, T])
        m.cT, at = place(nc, region, "cT", [P, KT, TC])
        m.xch, at = place(nc, at, "xch", [P, KT, TC], F32R)
        m.xcl, at = place(nc, at, "xcl", [P, KT, TC], F32R)
        m.sm2, at = place(nc, at, "sm2", [P, SMALL2])
        m.mod, at = place(nc, at, "mod", [P, 6, KT, 2])
        m.G, at = place(nc, at, "G", [P, 2, KT, 2])
        m.ropes, at = place(nc, at, "ropes", [P, 2, T])
        base2 = at
        m.fT, at = place(nc, at, "fT", [P, 2, TA])
        o_area = at
        m.O2, at = place(nc, at, "O2", [P, 6, KH * VH])
        m.cqr, _ = place(nc, o_area, "cqr", [P, 3, TA])
        m.ckvr, _ = place(nc, o_area + 9216, "ckvr", [P, TA])
        m.krr, _ = place(nc, o_area + 12288, "krr", [P, 2, TA])
        m.f2h, _ = place(nc, o_area, "f2h", [P, 2, TA], F32R)
        m.f2l, _ = place(nc, o_area + 6144, "f2l", [P, 2, TA], F32R)
        c_area = at
        m.cqh, at = place(nc, at, "cqh", [P, 3, TA], F32R)
        m.cql, at = place(nc, at, "cql", [P, 3, TA], F32R)
        m.ckvh, at = place(nc, at, "ckvh", [P, TA], F32R)
        m.ckvl, at = place(nc, at, "ckvl", [P, TA], F32R)
        m.dft, _ = place(nc, c_area, "dft", [P, 2 * P + QB * 2 * T + 2 * 2 * TC])
        w2_area = at
        m.P2, at = place(nc, at, "P2", [P, 2, TA])
        m.PT2, at = place(nc, at, "PT2", [P, 2, TA])
        m.qs2, at = place(nc, at, "qs2", [P, 2, P])
        m.rt, at = place(nc, at, "rt", [P, 2, T])
        m.den2, at = place(nc, at, "den2", [P, 2, HG])
        m.rden2, at = place(nc, at, "rden2", [P, HG])
        m.nmax2, at = place(nc, at, "nmax2", [P, 2])
        assert at <= 229344, at
        m.AB, _ = place(nc, w2_area, "AB", [P, QB, 2, 2 * P])
        m.f2, _ = place(nc, w2_area + 8192, "f2", [P, 2, T])
        x_area = 16512 + 4 * (KT * T + 6 * SLAB)
        m.Q4, _ = place(nc, x_area, "Q4", [P, HG, TA])
        m.K4, _ = place(nc, x_area + 12288, "K4", [P, HG, TA])
        m.V4, _ = place(nc, x_area + 24576, "V4", [P, 6, HG * VH])
        m.gh, at = place(nc, base2, "gh", [P, KT, TA], F32R)
        m.gl, at = place(nc, at, "gl", [P, KT, TA], F32R)
        m.cg, at = place(nc, at, "cg", [P, T])
        m.cv, at = place(nc, at, "cv", [P, T])
        m.sgl, at = place(nc, at, "sgl", [P, T])
        m.gu, at = place(nc, at, "gu", [P, T])
        m.ot2, at = place(nc, at, "ot2", [P, 2, T])
        assert at <= 229344, at
        n_area = w2_area
        m.sq2, _ = place(nc, n_area, "sq2", [P, 2, T])
        m.xn2, _ = place(nc, n_area + 4096, "xn2", [P, 2, T])
        m.rstd2, _ = place(nc, n_area + 8192, "rstd2", [P, T])

        psum = ctx.enter_context(nc.psum_tensor("psum", [P, 8 * 512], F32))
        ps = [psum[:, 512 * b:512 * (b + 1)] for b in range(8)]

        ident, ones = m.cst[:, 0:P], m.cst[:, P:2 * P]
        inv, sign = m.cst[:, 256:257], m.cst[:, 257:258]

        def sem(name):
            return ctx.enter_context(nc.semaphore(name))

        s.consts_in, s.pos_in, s.h_in, s.out_done = (sem("consts_in"), sem("pos_in"), sem("h_in"), sem("out_done"))
        s.hi_ready, s.lo_ready = (sem("hi_ready"), sem("lo_ready"))
        s.acc_ready = sem("acc_ready")
        s.acc_free = sem("acc_free")
        s.gate_free = sem("gate_free")
        s.swap_ready, s.rope_done = (sem("swap_ready"), sem("rope_done"))
        s.sq_ready, s.sq_used = (sem("sq_ready"), sem("sq_used"))
        s.var_ready, s.std_ready = (sem("var_ready"), sem("std_ready"))
        s.xn_ready, s.xh_ready, s.x_ready = (sem("xn_ready"), sem("xh_ready"), sem("x_ready"))
        s.ik_sq, s.ik_stat, s.ik_var, s.ik_std, s.ik_norm = (sem("ik_sq"), sem("ik_stat"), sem("ik_var"), sem("ik_std"), sem("ik_norm"))
        s.q_staged = sem("q_staged")
        s.s_done, s.s_free = (sem("s_done"), sem("s_free"))
        s.max_ready, s.exp_ready = (sem("max_ready"), sem("exp_ready"))
        s.t_done, s.t_copied, s.pv_done = (sem("t_done"), sem("t_copied"), sem("pv_done"))
        s.o_ready = sem("o_ready")
        s.ot_done, s.of_ready, s.oh_ready, s.ol_ready = (sem("ot_done"), sem("of_ready"), sem("oh_ready"), sem("ol_ready"))
        s.sig_ready, s.mt_ready, s.mh_ready, s.m_ready = (sem("sig_ready"), sem("mt_ready"), sem("mh_ready"), sem("m_ready"))
        s.h_ready = sem("h_ready")
        s.relu_ready, s.us_ready, s.uh_ready = (sem("relu_ready"), sem("us_ready"), sem("uh_ready"))
        s.angles, s.tables = (sem("angles"), sem("tables"))
        s.ada_turned, s.row_copied = sem("ada_turned"), sem("row_copied")
        s.cs_ready, s.ada_used, s.mods_ready = sem("cs_ready"), sem("ada_used"), sem("mods_ready")
        s.sm2_in, s.ctx_in, s.dft_in = (sem("sm2_in"), sem("ctx_in"), sem("dft_in"))
        s.mod_ready = sem("mod_ready")
        s.kr_ready, s.k4_ready, s.q4_part = (sem("kr_ready"), sem("k4_ready"), sem("q4_part"))
        s.q2_staged, s.s2_done, s.max2_ready, s.exp2_ready, s.t2_done = (sem("q2_staged"), sem("s2_done"), sem("max2_ready"), sem("exp2_ready"), sem("t2_done"))
        s.t2_copied, s.pv2_done, s.o2_ready = (sem("t2_copied"), sem("pv2_done"), sem("o2_ready"))
        s.ot2_done, s.ot2_copied, s.oth_ready, s.mixed = (sem("ot2_done"), sem("ot2_copied"), sem("oth_ready"), sem("mixed"))
        s.ab_done, s.ab_copied, s.f2_done, s.f2_copied, s.f2h_ready = (sem("ab_done"), sem("ab_copied"), sem("f2_done"), sem("f2_copied"), sem("f2h_ready"))
        s.f2_split = sem("f2_split")
        s.mid_ready, s.silu_ready, s.gu_ready, s.gh_ready, s.gl_ready = (sem("mid_ready"), sem("silu_ready"), sem("gu_ready"), sem("gh_ready"), sem("gl_ready"))
        s.final_ready = sem("final_ready")
        s.loaded = [ctx.enter_context(nc.semaphore(f"loaded{i}")) for i in range(2)]
        s.held = ctx.enter_context(nc.semaphore("held"))
        block = ctx.enter_context(nc.Block())

        def hold(engine, sem, value):
            engine.wait_ge(sem, value)
            engine.sem_inc(s.held, 1)

        @block.sync
        def _(sp):
            sp.dma_start(m.posi[:, :], io["pos"]).then_inc(s.pos_in, 16)
            sp.dma_start(m.cst[:, :], io["c_ident"]).then_inc(s.consts_in, 16)
            sp.dma_start(m.sm1[:, :], io["small_1"]).then_inc(s.consts_in, 16)
            sp.dma_start(m.hT[:, :, :], io["x_t"]).then_inc(s.h_in, 16)
            sp.dma_start(m.masks[:, :], io["c_masks"]).then_inc(s.consts_in, 16)
            with sp.Fori(0, SLABS_ALL // 2) as i:
                for slot in range(2):
                    sp.wait_ge(s.hi_ready, 2 * i + slot + 1)
                    sp.wait_ge(s.lo_ready, 2 * i + slot + 1)
                    sp.dma_start(m.wst[:, slot, :],
                                 io["weights"][bass.ds(2 * i + slot, 1)].rearrange("a p n -> p (a n)")
                                 ).then_inc(s.loaded[slot], 16)
            sp.wait_ge(s.final_ready, 1)
            sp.dma_start(out, m.hT[:, :, :]).then_inc(s.out_done, 16)
            sp.wait_ge(s.out_done, 16)

        @block.gpsimd
        def _(pool):
            def stage(item, parity, g, tile_ap, row0, qb):
                if g == 0:
                    pool.wait_ge(s.s_done, item + 1)
                return nc.gpsimd.tensor_copy(
                    m.qs[row0:row0 + HD, parity, g, :],
                    tile_ap[row0:row0 + HD, qb * P:(qb + 1) * P])

            def pick(buf, i):
                return buf[:, bass.ds(i, 1), :].rearrange("p a n -> p (a n)")

            nc.gpsimd.memset(m.qs[:, :, :, :], 0.0)
            pool.drain()
            with pool.Fori(0, DEPTH) as l:
                item0 = l * ITEMS1
                hold(pool, s.rope_done, l * ROPES1 + ROPES1 + 2)
                for qb in range(1, QB):
                    with pool.Fori(0, IDX_HEADS // 2) as i:
                        for par in range(2):
                            item = item0 + IT_IDX + (qb - 1) * IDX_HEADS + 2 * i + par
                            stage(item, par, 0, pick(m.IQ, i), par * HD, qb).then_inc(s.q_staged, 1)
                for qb in range(QB):
                    with pool.Fori(0, A_HEADS // 2) as i:
                        for par in range(2):
                            item = item0 + IT_A + qb * A_HEADS + 2 * i + par
                            stage(item, par, 0, pick(m.AQ, i), par * HD, qb).then_inc(s.q_staged, 1)
                for qb in range(QB):
                    with pool.Fori(0, B_HPG // 2) as i:
                        for par in range(2):
                            item = item0 + IT_B + qb * B_HPG + 2 * i + par
                            for g in range(3):
                                last = stage(item, par, g, pick(m.BQK, 2 * g + i), par * HD, qb)
                            last.then_inc(s.q_staged, 1)
                for qb in range(QB):
                    with pool.Fori(0, C_HEADS // 2) as i:
                        for par in range(2):
                            item = item0 + IT_C + qb * C_HEADS + 2 * i + par
                            stage(item, par, 0, pick(m.CQ, i), par * HD, qb).then_inc(s.q_staged, 1)
            for l in range(DEPTH):
                with pool.Fori(0, 3) as hg:
                    hold(pool, s.acc_free, tiles2(l)["hg"] - FREE_OFF + (24 if l == 0 else 20) * (hg + 1) + 4)
                    for n, (qb, j, side) in enumerate(items2(l)):
                        item = item_base2(l) + len(items2(l)) * hg + n
                        hold(pool, s.s2_done, item + 1)
                        c = side * T + qb * P
                        nc.gpsimd.tensor_copy(m.qs2[0:QH, n % 2, :], m.Q4[0:QH, j, c:c + P]).then_inc(s.q2_staged, 1)

        @block.tensor
        def _(pe):
            def slab_split(slab):
                pe.wait_ge(s.hi_ready, slab + 3)
                pe.wait_ge(s.lo_ready, slab + 3)

            def columns_tile(bank, slot, kts, col, rh, rl, k0=0, late=()):
                for n, k in enumerate(kts):
                    for k_late, sem_, value in late:
                        if k == k_late:
                            pe.wait_ge(sem_, value)
                    w_hi = m.whi[:, slot, k * 256 + col:k * 256 + col + P]
                    w_lo = m.wlo[:, slot, k * 256 + col:k * 256 + col + P]
                    pe.matmul(ps[bank][:, :], w_hi, rh[:, k + k0, :], start=n == 0, stop=False)
                    pe.matmul(ps[bank][:, :], w_hi, rl[:, k + k0, :], start=False, stop=False)
                    last = pe.matmul(ps[bank][:, :], w_lo, rh[:, k + k0, :], start=False,
                                     stop=n == len(kts) - 1)
                return last

            def tokens_tile(bank, slot, block_, col, n):
                for k in range(KT):
                    x_hi = m.xh[:, k, block_ * P:(block_ + 1) * P]
                    x_lo = m.xl[:, k, block_ * P:(block_ + 1) * P]
                    w_hi = m.whi[:, slot, k * 256 + col:k * 256 + col + n]
                    w_lo = m.wlo[:, slot, k * 256 + col:k * 256 + col + n]
                    pe.matmul(ps[bank][:, 0:n], x_hi, w_hi, start=k == 0, stop=False)
                    pe.matmul(ps[bank][:, 0:n], x_hi, w_lo, start=False, stop=False)
                    last = pe.matmul(ps[bank][:, 0:n], x_lo, w_hi, start=False, stop=k == KT - 1)
                return last

            def norm_sums(norm):
                for k in range(KT):
                    pe.wait_ge(s.sq_ready, norm * KT + k + 1)
                    pe.matmul(ps[4][:, :], ones, m.sq[:, k % 2, :], start=k == 0, stop=k == KT - 1
                              ).then_inc(s.sq_used, 1)

            def attention(item0, soft0, group, pairs, segs_of, v_of, o_of):
                def logits(i, par):
                    pe.wait_ge(s.q_staged, item0 + 2 * i + par + 1)
                    pe.wait_ge(s.s_free, item0 + 2 * i + par + 2)
                    for bank, c0, n, g, keys in segs_of(par, i):
                        last = pe.matmul(ps[bank][:, 0:n], m.qs[:, par, g, :], keys, start=True, stop=True)
                    last.then_inc(s.s_done, 1)

                def turn(i, par):
                    n = soft0 + 2 * i + par
                    pe.wait_ge(s.exp_ready, n + 1)
                    pe.wait_ge(s.t_copied, n + 1)
                    blocks = [c0 + P * b for _, c0, w, _, _ in segs_of(par, i) for b in range(w // P)]
                    for b, c in enumerate(blocks):
                        last = pe.transpose(ps[3 + b // 4][:, (b % 4) * P:(b % 4 + 1) * P],
                                            m.S[:, par, c:c + P], ident)
                    last.then_inc(s.t_done, 1)

                def weighted(i, par):
                    n = soft0 + 2 * i + par
                    pe.wait_ge(s.t_copied, n + 2)
                    vs = v_of(par, i)
                    for b, v in enumerate(vs):
                        last = pe.matmul(o_of(par, i), m.PT[:, par, b * P:(b + 1) * P], v,
                                         start=b == 0, stop=b == len(vs) - 1)
                    last.then_inc(s.pv_done, 1)

                def body(i, first, last):
                    logits(i, 1)
                    turn(i, 0)
                    if not first:
                        weighted(i - 1, 1)
                    if not last:
                        logits(i + 1, 0)
                    turn(i, 1)
                    weighted(i, 0)

                logits(0, 0)
                body(0, True, pairs == 1)
                if pairs > 2:
                    with pe.Fori(1, pairs - 1) as i:
                        body(i, False, False)
                body(pairs - 1, False, True)
                weighted(pairs - 1, 1)

            def kslice(buf, i, n):
                return buf[:, bass.ds(i, 1), 0:n].rearrange("p a n -> p (a n)")

            def vslice(buf, blk, c):
                return buf[:, blk, bass.ds(c, HD)]

            pe.wait_ge(s.consts_in, 48)
            pe.sem_inc(s.sq_used, 2)
            pe.sem_inc(s.s_done, 2)
            pe.sem_inc(s.t_done, 2)
            pe.sem_inc(s.pv_done, 2)
            with pe.Fori(0, DEPTH) as l:
                slab0, tile0, free0 = l * SLABS1, l * TILES1, l * FREES1

                def done(mm):
                    mm.then_inc(s.acc_ready, 1)

                def bank_free(v):
                    pe.wait_ge(s.acc_free, free0 + v + 1)

                norm_sums(l * NORMS1)
                v = FR_A
                for sl in range(5):
                    slab_split(slab0 + SL_A + sl)
                    for t in range(1 if sl == 4 else 2):
                        bank_free(v)
                        late = [(k, s.x_ready, l * NORMS1 * KT + k + 1) for k in range(KT)] if v == FR_A else ()
                        done(columns_tile(v % 4, (SL_A + sl) % 2, range(KT), t * P, m.xh, m.xl, late=late))
                        v += 1
                    if sl in (1, 4):
                        col, n = (P + HD, HD) if sl == 1 else (HD, IDX_HEADS)
                        for b in range(QB):
                            bank_free(v)
                            done(tokens_tile(v % 4, (SL_A + sl) % 2, b, col, n))
                            v += 1
                with pe.Fori(0, 3) as i:
                    for sl in range(2):
                        slab_split(slab0 + SL_B + 2 * i + sl)
                        for t in range(2):
                            bank_free(FR_B + 4 * i + 2 * sl + t)
                            done(columns_tile((FR_B + 2 * sl + t) % 4, (SL_B + sl) % 2, range(KT), t * P,
                                              m.xh, m.xl))
                hold(pe, s.ik_sq, l + 1)
                pe.matmul(ps[4][0:HD, :], m.cst[0:HD, P:P + HD], m.iknorm[0:HD, :], start=True, stop=True
                          ).then_inc(s.ik_stat, 1)
                for sl in range(3):
                    slab_split(slab0 + SL_BV + sl)
                    for b in range(QB):
                        v = FR_BV + 4 * sl + b
                        bank_free(v)
                        done(tokens_tile(v % 4, (SL_BV + sl) % 2, b, 0, 256))
                for sl in range(2):
                    slab_split(slab0 + SL_C + sl)
                    for t in range(2):
                        v = FR_C + 2 * sl + t
                        bank_free(v)
                        done(columns_tile(v % 4, (SL_C + sl) % 2, range(KT), t * P, m.xh, m.xl))
                slab_split(slab0 + SL_C + 2)
                v = FR_C + 4
                bank_free(v)
                done(columns_tile(v % 4, (SL_C + 2) % 2, range(KT), 0, m.xh, m.xl))
                slab_split(slab0 + SL_C + 3)
                for b in range(QB):
                    v = FR_C + 5 + b
                    bank_free(v)
                    done(tokens_tile(v % 4, (SL_C + 3) % 2, b, 0, P))
                pe.wait_ge(s.rope_done, l * ROPES1 + ROPES1 + 2)
                hold(pe, s.acc_free, free0 + FR_C + 9 + 4)
                for qb in range(1, QB):
                    with pe.Fori(0, IDX_HEADS // 2) as i:
                        for par in range(2):
                            item = l * ITEMS1 + IT_IDX + (qb - 1) * IDX_HEADS + 2 * i + par
                            pe.wait_ge(s.q_staged, item + 1)
                            pe.wait_ge(s.s_free, item + 1)
                            n = (qb + 1) * P
                            pe.matmul(ps[par][:, 0:n], m.qs[:, par, 0, :], m.IK[:, 0:n], start=True, stop=True
                                      ).then_inc(s.s_done, 1)
                def rows_of(i, slot):
                    pe.wait_ge(s.loaded[slot], 16 * ((l * SLABS1 + SL_ADA) // 2 + i + 1))
                    for k in range(KT):
                        last = pe.matmul(ps[5 + slot][0:2, 0:256], m.cs[:, k, :], m.wst[:, slot, k * 256:(k + 1) * 256],
                                         start=k == 0, stop=k == KT - 1)
                    last.then_inc(s.ada_used, 1)

                def columns_of(i, slot):
                    pe.wait_ge(s.row_copied, l * ADA_SLABS + 2 * i + slot + 1)
                    for t in range(2):
                        last = pe.matmul(ps[7][:, bass.ds(8 * i + 4 * slot + 2 * t, 2)],
                                         m.rows[0:2, slot, t * P:(t + 1) * P], m.cst[0:2, 0:2], start=True, stop=True)
                    last.then_inc(s.ada_turned, 1)

                pe.wait_ge(s.cs_ready, 1)
                hold(pe, s.gate_free, l * 24 + 4)
                rows_of(0, 0)
                with pe.Fori(0, ADA_SLABS // 2 - 1) as i:
                    rows_of(i, 1)
                    columns_of(i, 0)
                    rows_of(i + 1, 0)
                    columns_of(i, 1)
                rows_of(ADA_SLABS // 2 - 1, 1)
                columns_of(ADA_SLABS // 2 - 1, 0)
                columns_of(ADA_SLABS // 2 - 1, 1)
                for branch in range(3):
                    for qb in range(QB):
                        group = branch * QB + qb
                        n = (qb + 1) * P
                        near = (0, P) if qb == 0 else ((qb - 1) * P, 2 * P)
                        ob = 6 + group % 2
                        if branch == 0:
                            item0, soft0, pairs = IT_A + qb * A_HEADS, SX_A + qb * A_HEADS, A_HEADS // 2
                            segs = lambda par, i, n=n: [(par, 0, n, 0, m.AK[:, 0:n])]
                            vs = lambda par, i, qb=qb: [m.VA[:, b, :] for b in range(qb + 1)]
                            oc = lambda par, i: (2 * i + par) * HD
                        elif branch == 1:
                            item0, soft0, pairs = IT_B + qb * B_HPG, SX_B + qb * B_HPG, B_HPG // 2

                            def segs(par, i, n=n, near=near):
                                k0, w = near
                                return [(0, 0, w, 0, m.BQK[:, bass.ds(6 + i, 1), k0:k0 + w].rearrange("p a n -> p (a n)")),
                                        (1, w, n, 1, kslice(m.BQK, 8 + i, n)),
                                        (2, w + n, n, 2, kslice(m.BQK, 10 + i, n))]

                            def vs(par, i, qb=qb, near=near):
                                k0, w = near
                                head = lambda g: (g * B_HPG + 2 * i + par) * HD
                                return ([vslice(m.VB, k0 // P + b, head(0)) for b in range(w // P)]
                                        + [vslice(m.VB, b, head(1)) for b in range(qb + 1)]
                                        + [vslice(m.VB, b, head(2)) for b in range(qb + 1)])
                            oc = lambda par, i: (2 * i + par) * HD
                        else:
                            item0, soft0, pairs = IT_C + qb * C_HEADS, SX_C + qb * C_HEADS, C_HEADS // 2
                            segs = lambda par, i, near=near: [(par, 0, near[1], 0, m.CK[:, near[0]:near[0] + near[1]])]
                            vs = lambda par, i, near=near: [m.VC[:, near[0] // P + b, par * HD:(par + 1) * HD]
                                                            for b in range(near[1] // P)]
                            oc = lambda par, i: (4 * par + i) * HD
                        pe.wait_ge(s.o_ready, l * GROUPS1 + group + 1)
                        attention(l * ITEMS1 + item0, l * SOFTS1 + soft0, group, pairs, segs, vs,
                                  lambda par, i, oc=oc, ob=ob: ps[ob][:, bass.ds(oc(par, i), HD)])
                pe.wait_ge(s.o_ready, (l + 1) * GROUPS1 + 2)
                for j in range(9):
                    src, c = (m.OA, j) if j < 3 else (m.OB, j - 3) if j < 5 else (m.OC, j - 5)
                    pe.wait_ge(s.of_ready, l * 9 + j + 1)
                    for b in range(QB):
                        last = pe.transpose(ps[4 + j % 2][:, b * P:(b + 1) * P], src[:, b, c * P:(c + 1) * P], ident)
                    last.then_inc(s.ot_done, 1)
                hold(pe, s.ol_ready, (l + 1) * 9)
                with pe.Fori(0, 2) as jp:
                    for half in range(2):
                        for g in range(3):
                            c = SL_MERGE + 5 * half + g
                            slab_split(slab0 + c + 10 * jp)
                            for t in range(2):
                                u = 6 * half + 2 * g + t
                                pe.wait_ge(s.gate_free, l * 24 + 12 * jp + u + 1)
                                done(columns_tile(4 + u % 4, c % 2, range(KT), t * P, m.xh, m.xl))
                        c = SL_MERGE + 5 * half + 3
                        slab_split(slab0 + c + 10 * jp)
                        for b, (kts, k0) in enumerate((((0, 1, 2), 0), ((3, 4), 0), ((0, 1, 2, 3), 5))):
                            if b == 2:
                                c += 1
                                slab_split(slab0 + c + 10 * jp)
                            for t in range(2):
                                v = FR_MERGE + 6 * half + 2 * b + t
                                bank_free(v + 12 * jp)
                                done(columns_tile(v % 4, c % 2, kts, t * P, m.oh, m.ol, k0))
                hold(pe, s.m_ready, (l + 1) * KT)
                with pe.Fori(0, 2) as i:
                    for sl in range(2):
                        slab_split(slab0 + SL_WO + 2 * i + sl)
                        for t in range(2):
                            v = FR_WO + 2 * sl + t
                            bank_free(v + 4 * i)
                            done(columns_tile(v % 4, (SL_WO + sl) % 2, range(KT), t * P, m.mh, m.ml))
                norm_sums(l * NORMS1 + 1)
                with pe.Fori(0, 4) as q:
                    for down in range(2):
                        xa, xb = (m.uh, m.ul) if down else (m.xh, m.xl)
                        with pe.Fori(0, 2) as i:
                            for sl in range(2):
                                if down:
                                    pe.wait_ge(s.acc_free, free0 + FR_MLP + 16 * q + 7 + 4)
                                    late = [(KT - 1, s.acc_free, free0 + FR_MLP + 16 * q + 8 + 4)]
                                else:
                                    late = [(k, s.x_ready, (l * NORMS1 + 1) * KT + k + 2) for k in range(0, KT, 2)]
                                slab_split(slab0 + SL_MLP + 8 * q + 4 * down + 2 * i + sl)
                                for t in range(2):
                                    v = FR_MLP + 8 * down + 2 * sl + t
                                    bank_free(v + 16 * q + 4 * i)
                                    done(columns_tile(v % 4, (SL_MLP + sl) % 2, range(KT), t * P, xa, xb,
                                                      late=late if t == 0 else ()))
            norm_sums(DEPTH * NORMS1)
            def done2(mm, skip=0):
                mm.then_inc(s.acc_ready, 1 + skip)

            def bank2(tile, i=0):
                pe.wait_ge(s.acc_free, tile - FREE_OFF + 1 + i)
                return tile % 4

            def columns2(bank, slot, kts, col, step, rh, rl, n, k0=0, late=()):
                for a, k in enumerate(kts):
                    for k_late, sem_, value in late:
                        if k == k_late:
                            pe.wait_ge(sem_, value)
                    w_hi = m.whi[:, slot, k * step + col:k * step + col + P]
                    w_lo = m.wlo[:, slot, k * step + col:k * step + col + P]
                    h, t = rh(k + k0), rl(k + k0)
                    pe.matmul(ps[bank][:, 0:n], w_hi, h, start=a == 0, stop=False)
                    pe.matmul(ps[bank][:, 0:n], w_hi, t, start=False, stop=False)
                    last = pe.matmul(ps[bank][:, 0:n], w_lo, h, start=False, stop=a == len(kts) - 1)
                return last

            def sums2(name, kt, n):
                k0 = NORMS2[name][0]
                for k in range(kt):
                    pe.wait_ge(s.sq_ready, k0 + k + 1)
                    pe.matmul(ps[4][:, 0:n], ones, m.sq2[:, (k0 + k) % 2, 0:n], start=k == 0, stop=k == kt - 1
                              ).then_inc(s.sq_used, 1)

            def x_of(side):
                return ((lambda k: m.xch[:, k, :], lambda k: m.xcl[:, k, :]) if side else
                        (lambda k: m.xh[:, k, :], lambda k: m.xl[:, k, :]))

            pe.sem_inc(s.s2_done, 2)
            pe.sem_inc(s.t2_done, 2)
            pe.sem_inc(s.pv2_done, 2)
            for l in range(DEPTH):
                tl = tiles2(l)
                lat_con = pieces(l)

                def slabw(c, i=0, step=0):
                    number, slot, _ = slab2(l, c, i, step)
                    slab_split(number)
                    return slot

                for side, n, _ in pieces(l, True):
                    sums2(f"mix{l}{side}", KT, n)
                t = tl["win"]
                for c in range(7):
                    if c % 2 == 0:
                        slot = slabw(S2_WIN + c // 2)
                    for side, n, _ in pieces(l, l == 0 or c >= 5):
                        b = bank2(t)
                        x0 = NORMS2[f"mix{l}{side}"][0] - X_OFF
                        late = [(k, s.x_ready, x0 + k + 1) for k in range(KT)] if c == 0 or c == 5 else ()
                        done2(columns2(b, slot, range(KT), (c % 2) * P, 256, *x_of(side), n, late=late))
                        t += 1
                for side, n, _ in lat_con:
                    sums2(f"q{l}{side}", 3, n)
                for side, n, _ in pieces(l, True):
                    sums2(f"kv{l}{side}", 1, n)
                hold(pe, s.x_ready, NORMS2[f"kv{l}1"][0] + 1 - X_OFF)
                items = items2(l)
                with pe.Fori(0, 3) as hg:
                    per = 24 if l == 0 else 20
                    tile = tl["hg"]
                    slot = slabw(S2_HG, hg, 2)
                    for j in range(HG):
                        for side, n, c0 in lat_con:
                            b = bank2(tile, per * hg)
                            done2(columns2(b, slot, range(3), j * P, 512, lambda k: m.cqh[:, k, c0:c0 + n],
                                           lambda k: m.cql[:, k, c0:c0 + n], n))
                            tile += 1
                    slot = slabw(S2_HG + 1, hg, 2)
                    for j in range(HG):
                        for side, n, c0 in pieces(l, True):
                            b = bank2(tile, per * hg)
                            done2(columns2(b, slot, range(1), j * P, 512, lambda k: m.ckvh[:, c0:c0 + n],
                                           lambda k: m.ckvl[:, c0:c0 + n], n))
                            tile += 1
                    for blk in range(6):
                        b = bank2(tile, per * hg)
                        o = ps[b][:, 0:HG * VH]
                        wv = [w[:, slot, 0:512].rearrange("p (h d) -> p h d", h=HG)[:, :, VH:2 * VH]
                              for w in (m.whi, m.wlo)]
                        xa, xb = (x[:, blk * P:(blk + 1) * P] for x in (m.ckvh, m.ckvl))
                        pe.matmul(o, xa, wv[0], start=True, stop=False)
                        pe.matmul(o, xa, wv[1], start=False, stop=False)
                        last = pe.matmul(o, xb, wv[0], start=False, stop=True)
                        done2(last, 2 if blk == 5 else 0)
                        tile += 1
                    pe.wait_ge(s.acc_free, tl["hg"] - FREE_OFF + per * (hg + 1) + 4)

                    def logits(n):
                        qb, j, side = items[n]
                        item = item_base2(l) + len(items) * hg + n
                        pe.wait_ge(s.q2_staged, item + 1)
                        pe.wait_ge(s.exp2_ready, item + 1)
                        for c, w in (((0, 512), (512, 256)) if side == 0 else ((0, 256),)):
                            last = pe.matmul(ps[2 * (n % 2) + c // 512][:, 0:w], m.qs2[0:QH, n % 2, :],
                                             m.K4[0:QH, j, side * T + c:side * T + c + w], start=True, stop=True)
                        last.then_inc(s.s2_done, 1)

                    def turn(n):
                        item = item_base2(l) + len(items) * hg + n
                        pe.wait_ge(s.exp2_ready, item + 3)
                        pe.wait_ge(s.t2_copied, item + 1)
                        for b in range(6 if items[n][2] == 0 else 2):
                            last = pe.transpose(ps[4 + b // 4][:, (b % 4) * P:(b % 4 + 1) * P],
                                                m.P2[:, n % 2, b * P:(b + 1) * P], ident)
                        last.then_inc(s.t2_done, 1)

                    def weighted(n):
                        qb, j, side = items[n]
                        item = item_base2(l) + len(items) * hg + n
                        pe.wait_ge(s.t2_copied, item + 2)
                        if j == 0:
                            pe.wait_ge(s.o2_ready, group_base2(l) + len(items) // HG * hg + n // HG + 1)
                        blocks = range(6) if side == 0 else range(4, 6)
                        for b, blk in enumerate(blocks):
                            last = pe.matmul(ps[6 + n // HG % 2][:, j * VH:(j + 1) * VH],
                                             m.PT2[:, n % 2, b * P:(b + 1) * P], m.V4[:, blk, j * VH:(j + 1) * VH],
                                             start=b == 0, stop=b == len(blocks) - 1)
                        last.then_inc(s.pv2_done, 1)

                    logits(0)
                    for n in range(len(items)):
                        if n + 1 < len(items):
                            logits(n + 1)
                        turn(n)
                        if n:
                            weighted(n - 1)
                    weighted(len(items) - 1)
                hold(pe, s.o2_ready, group_base2(l) + 3 * len(items) // HG + 2)
                n = 12 * l
                for j in range(6):
                    for side, w, _ in lat_con:
                        pe.wait_ge(s.ot2_copied, n + 1)
                        for b in range(w // P):
                            last = pe.transpose(ps[6 + n % 2][:, b * P:(b + 1) * P],
                                                m.O2[:, 4 * side + b, j * P:(j + 1) * P], ident)
                        last.then_inc(s.ot2_done, 1)
                        n += 1
                pe.wait_ge(s.dft_in, 16 * (l + 1))
                pe.wait_ge(s.mixed, 12 if l == 0 else 22)
                n = 0 if l == 0 else 12
                for side, w, c0 in lat_con:
                    if side == 1:
                        pe.wait_ge(s.f2_copied, 2)
                    for b in range(w // P):
                        for c in range(2):
                            bank = 4 + n % 2
                            pe.wait_ge(s.ab_copied, n + 1)
                            pe.matmul(ps[bank][:, 0:2 * P], m.fT[:, c, c0 + b * P:c0 + (b + 1) * P], m.dft[:, 0:2 * P],
                                      start=True, stop=True).then_inc(s.ab_done, 1)
                            n += 1
                    pe.wait_ge(s.ab_copied, n + 2)
                    for c in range(2):
                        nb, off = w // P, 2 * P + side * QB * 2 * T
                        for b in range(nb):
                            for h in range(2):
                                last = pe.matmul(ps[6 + c][:, 0:w], m.AB[:, b, c, h * P:(h + 1) * P], m.dft[:, off + (2 * b + h) * w:off + (2 * b + h + 1) * w],
                                                 start=b == 0 and h == 0, stop=b == nb - 1 and h == 1)
                        last.then_inc(s.f2_done, 1)
                hold(pe, s.f2_split, 4 if l == 0 else 6)
                t = tl["four"]
                for c in range(2):
                    slot = slabw(S2_FOUR + c)
                    for side, n, c0 in lat_con:
                        b = bank2(t)
                        done2(columns2(b, slot, range(2), 0, 256, lambda k: m.f2h[:, k, c0:c0 + n],
                                       lambda k: m.f2l[:, k, c0:c0 + n], n))
                        t += 1
                pe.wait_ge(s.mixed, 16 if l == 0 else 24)
                t = tl["wout"]
                for sl in range(4):
                    slot = slabw(S2_WOUT + sl)
                    for h in range(2):
                        for side, n, _ in lat_con:
                            b = bank2(t)
                            done2(columns2(b, slot, range(KT), h * P, 256, *x_of(side), n))
                            t += 1
                for side, n, _ in lat_con:
                    sums2(f"ffn{l}{side}", KT, n)
                for c, (_, pairs, first) in enumerate(FFN_CHUNKS):
                    ns = len(lat_con)
                    with pe.Fori(0, pairs // 2) as i:
                        for sl in range(2):
                            slot = slabw(first + sl, i, 2)
                            for side, n, _ in lat_con:
                                for g in range(2):
                                    t = tl[f"up{c}"] + sl * 2 * ns + 2 * side + g
                                    b = bank2(t, 4 * ns * i)
                                    x0 = NORMS2[f"ffn{l}{side}"][0] - X_OFF
                                    late = [(k, s.x_ready, x0 + k + 2) for k in range(0, KT, 2)]
                                    done2(columns2(b, slot, range(KT), g * P, 256, *x_of(side), n,
                                                   late=late if g == 0 and sl == 0 and c == 0 else ()))
                    hold(pe, s.gl_ready, GL_BASE[l] + (8 * c + pairs - 1) * ns)
                    with pe.Fori(0, 2) as i:
                        for sl in range(2):
                            slot = slabw(first + pairs + sl, i, 2)
                            for g in range(2):
                                for side, n, c0 in lat_con:
                                    t = tl[f"down{c}"] + sl * 2 * ns + g * ns + side
                                    b = bank2(t, 4 * ns * i)
                                    done2(columns2(b, slot, range(pairs), g * P, 256,
                                                   lambda k: m.gh[:, k, c0:c0 + n], lambda k: m.gl[:, k, c0:c0 + n], n,
                                                   late=[(pairs - 1, s.gl_ready, GL_BASE[l] + (8 * c + pairs) * ns)]))
            sums2("final", KT, T)

        @block.scalar
        def _(act):
            def split(slab, slot, turn, tiles):
                act.wait_ge(s.loaded[slot], 16 * (turn + 1))
                if tiles is not None:
                    act.wait_ge(s.acc_ready, tiles)
                act.activation(m.whi[:, slot, :], m.wst[:, slot, :], ACT.Copy).then_inc(s.hi_ready, 1)

            def swap_halves(rope, tile_count, src, rows=P):
                if tile_count is not None:
                    act.wait_ge(s.acc_ready, tile_count)
                act.wait_ge(s.rope_done, rope[0] + 1)
                for a in range(0, rows, 64):
                    act.activation(m.xs[a:a + 32, rope[1], :], src[a + 32:a + 64, :], ACT.Copy)
                    last = act.activation(m.xs[a + 32:a + 64, rope[1], :], src[a:a + 32, :], ACT.Copy)
                last.then_inc(s.swap_ready, 1)

            def norm(n):
                act.wait_ge(s.var_ready, n + 1)
                act.activation(m.rstd[:, :], m.rstd[:, :], ACT.Sqrt).then_inc(s.std_ready, 1)

            def norm_heads(n):
                with act.Fori(0, KT // 2) as kk:
                    for par in range(2):
                        act.wait_ge(s.xn_ready, n * KT + 2 * kk + par + 1)
                        act.activation(m.xh[:, bass.ds(2 * kk + par, 1), :].rearrange("p a n -> p (a n)"),
                                       m.xn[:, par, :], ACT.Copy).then_inc(s.xh_ready, 1)

            def attention(soft0, group, group0, pairs, scale, den_col, blocks):
                act.wait_ge(s.o_ready, group0 + group + 1)
                with act.Fori(0, pairs) as i:
                    for par in range(2):
                        n = soft0 + 2 * i + par
                        act.wait_ge(s.max_ready, n + 1)
                        act.activation(m.S[:, par, 0:blocks[0]], m.S[:, par, 0:blocks[0]], ACT.Exp,
                                       bias=m.nmax[:, par:par + 1], scale=scale,
                                       accum_out=m.den[:, group % 2, bass.ds(den_col(par, i), 1)]
                                       ).then_inc(s.exp_ready, 1)
                        act.wait_ge(s.t_done, n + 3)
                        act.wait_ge(s.pv_done, n + 1)
                        nb = blocks[1]
                        for b in range(0, nb, 4):
                            w = min(4, nb - b) * P
                            last = act.activation(m.PT[:, par, b * P:b * P + w], ps[3 + b // 4][:, 0:w], ACT.Copy)
                        last.then_inc(s.t_copied, 1)

            def mlp_slab(l, c, q, i):
                return l * SLABS1 + c + 8 * q + 2 * i, c % 2, l * (SLABS1 // 2) + c // 2 + 4 * q + i

            act.sem_inc(s.hi_ready, 2)
            act.sem_inc(s.gate_free, 4)
            act.sem_inc(s.of_ready, 2)
            act.sem_inc(s.t_copied, 1)
            act.sem_inc(s.mh_ready, 1)
            for slot in range(2):
                split(slot, slot, 0, None)
            act.wait_ge(s.consts_in, 48)
            act.activation(m.cs[:, :, :], m.sm1[:, 58:74].rearrange("p (k s) -> p k s", s=2), ACT.Silu
                           ).then_inc(s.cs_ready, 1)
            act.wait_ge(s.angles, 1)
            act.activation(m.cosT[:, :], m.red[:, :], ACT.Sin).then_inc(s.tables, 1)
            act.wait_ge(s.angles, 2)
            act.activation(m.sinT[:, :], m.ang[:, :], ACT.Sin).then_inc(s.tables, 1)
            with act.Fori(0, DEPTH) as l:
                tile0, rope0 = l * TILES1, l * ROPES1

                def next_split(c, tiles, i=0, step=0):
                    split(*slab_of(c + 2, l, SLABS1, i, step), tile0 + tiles)

                norm(l * NORMS1)
                norm_heads(l * NORMS1)
                r = RP_A
                for sl, tiles, count in ((0, (0, 1), 2), (1, (2, 3), 8), (2, (8, 9), 10), (3, (10, 11), 12), (4, (), 17)):
                    for t in tiles:
                        swap_halves((rope0 + r, r % 2), tile0 + t + 1, ps[(FR_A + t) % 4])
                        r += 1
                    next_split(SL_A + sl, count)
                with act.Fori(0, 3) as i:
                    for sl in range(2):
                        for t in range(2):
                            j = 2 * sl + t
                            swap_halves((rope0 + RP_B + 4 * i + j, (RP_B + j) % 2), tile0 + TL_B + 4 * i + j + 1,
                                        ps[(FR_B + j) % 4])
                        next_split(SL_B + sl, TL_B + 2 * sl + 2 + 4 * i, i, 2)
                act.wait_ge(s.ik_var, l + 1)
                act.activation(m.rstd[0:HD, :], m.rstd[0:HD, :], ACT.Sqrt).then_inc(s.ik_std, 1)
                act.wait_ge(s.ik_norm, l + 1)
                swap_halves((rope0 + RP_IK, RP_IK % 2), None, m.iknorm, HD)
                for sl in range(3):
                    next_split(SL_BV + sl, TL_BV + 4 * sl + 4)
                for t in range(4):
                    r = RP_C + t
                    swap_halves((rope0 + r, r % 2), tile0 + TL_C + t + 1, ps[(FR_C + t) % 4])
                    if t % 2:
                        next_split(SL_C + t // 2, TL_C + t + 1)
                swap_halves((rope0 + RP_C + 4, (RP_C + 4) % 2), tile0 + TL_C + 5, ps[(FR_C + 4) % 4])
                with act.Fori(0, ADA_SLABS // 2) as i:
                    for slot in range(2):
                        act.wait_ge(s.ada_used, l * ADA_SLABS + 2 * i + slot + 1)
                        act.sem_inc(s.hi_ready, 1)
                        act.sem_inc(s.lo_ready, 1)
                        act.activation(m.rows[0:2, slot, :], ps[5 + slot][0:2, 0:256], ACT.Copy
                                       ).then_inc(s.row_copied, 1)
                for sl in range(2):
                    split(*slab_of(SL_MERGE + sl, l, SLABS1), tile0 + TL_C + 9)
                for branch in range(3):
                    for qb in range(QB):
                        n = (qb + 1) * P
                        near = P if qb == 0 else 2 * P
                        group = branch * QB + qb
                        if branch == 0:
                            args = (SX_A + qb * A_HEADS, A_HEADS // 2, lambda par, i: 2 * i + par, (n, qb + 1))
                        elif branch == 1:
                            args = (SX_B + qb * B_HPG, B_HPG // 2, lambda par, i: 2 * i + par,
                                    (near + 2 * n, (near + 2 * n) // P))
                        else:
                            args = (SX_C + qb * C_HEADS, C_HEADS // 2, lambda par, i: 4 * par + i,
                                    (near + 1, near // P))
                        attention(l * SOFTS1 + args[0], group, l * GROUPS1, args[1], 1.0, args[2], args[3])
                for j in range(9):
                    act.wait_ge(s.ot_done, l * 9 + j + 1)
                    act.wait_ge(s.ol_ready, l * 9 + j - 1) if j >= 2 else None
                    act.activation(m.of[:, j % 2, :], ps[4 + j % 2][:, :], ACT.Copy).then_inc(s.of_ready, 1)
                    act.drain()
                    act.activation(m.oh[:, j, :], m.of[:, j % 2, :], ACT.Copy).then_inc(s.oh_ready, 1)
                with act.Fori(0, 2) as jp:
                    for half in range(2):
                        t0 = TL_MERGE + 12 * half
                        for g in range(3):
                            for t in range(2):
                                u = 6 * half + 2 * g + t
                                act.wait_ge(s.acc_ready, tile0 + t0 + 24 * 0 + 2 * g + t + 1 + 24 * jp)
                                if g == 0 and t == 0:
                                    act.wait_ge(s.mt_ready, l * 8 + 4 * jp + 2 * half + 1)
                                act.activation(m.sg[:, 2 * g + t, :], ps[4 + u % 4][:, :], ACT.Sigmoid
                                               ).then_inc(s.gate_free, 1)
                            next_split(SL_MERGE + 5 * half + g, t0 + 2 * g + 2 + 24 * jp, jp, 10)
                        next_split(SL_MERGE + 5 * half + 3, t0 + 10 + 24 * jp, jp, 10)
                        next_split(SL_MERGE + 5 * half + 4, t0 + 12 + 24 * jp, jp, 10)
                        for t in range(2):
                            act.wait_ge(s.mt_ready, l * 8 + 4 * jp + 2 * half + t + 2)
                            act.activation(m.mh[:, bass.ds(4 * jp + 2 * half + t, 1), :].rearrange("p a n -> p (a n)"),
                                           m.mt[:, t, :], ACT.Copy).then_inc(s.mh_ready, 1)
                with act.Fori(0, 2) as i:
                    for sl in range(2):
                        next_split(SL_WO + sl, TL_WO + 2 * sl + 2 + 4 * i, i, 2)
                norm(l * NORMS1 + 1)
                norm_heads(l * NORMS1 + 1)
                with act.Fori(0, 4) as q:
                    with act.Fori(0, 2) as i:
                        for sl in range(2):
                            for t in range(2):
                                n = l * 32 + 8 * q + 4 * i + 2 * sl + t
                                act.wait_ge(s.acc_ready, tile0 + TL_MLP + 16 * q + 4 * i + 2 * sl + t + 1)
                                act.wait_ge(s.us_ready, n + 1)
                                act.activation(m.ur[:, t, :], ps[(FR_MLP + 2 * sl + t) % 4][:, :], ACT.Relu
                                               ).then_inc(s.relu_ready, 1)
                                act.wait_ge(s.us_ready, n + 3)
                                act.activation(m.uh[:, bass.ds(4 * i + 2 * sl + t, 1), :].rearrange("p a n -> p (a n)"),
                                               m.us[:, t, :], ACT.Copy).then_inc(s.uh_ready, 1)
                            split(*mlp_slab(l, SL_MLP + sl + 2, q, i), tile0 + TL_MLP + 2 * sl + 2 + 16 * q + 4 * i)
                    with act.Fori(0, 2) as i:
                        for sl in range(2):
                            c = SL_MLP + 4 + sl + 2
                            tiles = tile0 + TL_MLP + 8 + 2 * sl + 2 + 16 * q + 4 * i
                            split(*mlp_slab(l, c, q, i), tiles)
            norm(DEPTH * NORMS1)
            def norm2(name):
                n0, n = NORMS2[name][1], T if name[-1] == "0" or name == "final" else TC
                act.wait_ge(s.var_ready, n0 + 1)
                act.activation(m.rstd2[:, 0:n], m.rstd2[:, 0:n], ACT.Sqrt).then_inc(s.std_ready, 1)

            def heads2(name, kt, n, dst, shift=None):
                k0 = NORMS2[name][0]
                for k in range(kt):
                    act.wait_ge(s.xn_ready, k0 + k + 1 - X_OFF)
                    src = m.xn2[:, (k0 + k) % 2, 0:n]
                    if shift is None:
                        ins = act.activation(dst(k), src, ACT.Copy)
                    else:
                        ins = act.activation(dst(k), src, ACT.Identity, bias=shift(k))
                    ins.then_inc(s.xh_ready, 1)

            def x_dst(side):
                return (lambda k: m.xch[:, k, :]) if side else (lambda k: m.xh[:, k, :])

            act.wait_ge(s.h_ready, KT)
            act.dma_start(m.sm2[:, :], io["small_2"]).then_inc(s.sm2_in, 16)
            act.dma_start(m.cT[:, :, :], io["ctx_t"]).then_inc(s.ctx_in, 16)
            act.dma_start(m.ropes[:, :, :].rearrange("p a n -> p (a n)"), io["c_ropes"]).then_inc(s.ctx_in, 16)
            act.wait_ge(s.sm2_in, 16)
            act.sem_inc(s.exp2_ready, 2)
            act.sem_inc(s.ot2_copied, 2)
            act.sem_inc(s.ab_copied, 2)
            for l in range(DEPTH):
                tl = tiles2(l)
                lat_con = pieces(l)
                ns = len(lat_con)

                def next2(c, tiles, i=0, step=0):
                    if l == DEPTH - 1 and isinstance(i, int) and c + 2 >= SLABS2:
                        return
                    split(*slab2(l, c + 2, i, step), tiles)

                act.wait_ge(s.mod_ready, l + 1)
                for side, n, _ in pieces(l, True):
                    norm2(f"mix{l}{side}")
                    heads2(f"mix{l}{side}", KT, n, x_dst(side), lambda k, side=side: m.mod[:, 0, k, side:side + 1])
                t = tl["win"]
                for sl in range(4):
                    for c in range(2 * sl, min(2 * sl + 2, 7)):
                        t += len(pieces(l, l == 0 or c >= 5))
                    next2(S2_WIN + sl, t)
                for side, n, c0 in lat_con:
                    norm2(f"q{l}{side}")
                    heads2(f"q{l}{side}", 3, n, lambda k, c0=c0, n=n: m.cqh[:, k, c0:c0 + n])
                for side, n, c0 in pieces(l, True):
                    norm2(f"kv{l}{side}")
                    heads2(f"kv{l}{side}", 1, n, lambda k, c0=c0, n=n: m.ckvh[:, c0:c0 + n])
                act.wait_ge(s.kr_ready, l + 1)
                for j in range(HG):
                    last = act.activation(m.K4[64:96, j, :], m.krr[64:96, 0, :], ACT.Copy)
                last.then_inc(s.k4_ready, 1)
                items = items2(l)
                per = 24 if l == 0 else 20
                with act.Fori(0, 3) as hg:
                    tile = tl["hg"] + per * hg
                    for j in range(HG):
                        act.wait_ge(s.acc_ready, tile + j * ns + 1)
                        act.activation(m.Q4[0:64, j, 0:T], ps[(tl["hg"] + j * ns) % 4][0:64, :], ACT.Copy, scale=SM
                                       ).then_inc(s.q4_part, 1)
                    next2(S2_HG, tile + HG * ns, hg, 2)
                    next2(S2_HG + 1, tile + per, hg, 2)
                    for n, (qb, j, side) in enumerate(items):
                        item = item_base2(l) + len(items) * hg + n
                        w = TA if side == 0 else TC
                        if j == 0:
                            act.wait_ge(s.o2_ready, group_base2(l) + len(items) // HG * hg + n // HG + 1)
                        act.wait_ge(s.t2_done, item + 1)
                        act.wait_ge(s.max2_ready, item + 1)
                        act.activation(m.P2[:, n % 2, 0:w], psum[:, 1024 * (n % 2):1024 * (n % 2) + w], ACT.Exp,
                                       bias=m.nmax2[:, n % 2:n % 2 + 1],
                                       accum_out=m.den2[:, n // HG % 2, j:j + 1]).then_inc(s.exp2_ready, 1)
                act.wait_ge(s.o2_ready, group_base2(l) + 3 * len(items) // HG + 2)
                act.dma_start(m.dft[:, :], io["c_dft"]).then_inc(s.dft_in, 16)
                n = 12 * l
                for j in range(6):
                    for side, w, _ in lat_con:
                        act.wait_ge(s.ot2_done, n + 1)
                        if n - 12 * l >= 2:
                            act.wait_ge(s.mixed, n - 1 + 4 * l)
                        act.activation(m.ot2[:, n % 2, 0:w], ps[6 + n % 2][:, 0:w], ACT.Copy).then_inc(s.ot2_copied, 1)
                        act.drain()
                        act.activation(x_dst(side)(2 + j), m.ot2[:, n % 2, 0:w], ACT.Copy).then_inc(s.oth_ready, 1)
                        n += 1
                n, f = (0, 0) if l == 0 else (12, 4)
                for side, w, c0 in lat_con:
                    for b in range(w // P):
                        for c in range(2):
                            act.wait_ge(s.ab_done, n + 1)
                            act.activation(m.AB[:, b, c, :], ps[4 + n % 2][:, 0:2 * P], ACT.Copy).then_inc(s.ab_copied, 1)
                            n += 1
                    for c in range(2):
                        act.wait_ge(s.f2_done, f + 1)
                        if side:
                            act.wait_ge(s.f2_split, f - 1)
                        act.activation(m.f2[:, c, 0:w], ps[6 + c][:, 0:w], ACT.Copy).then_inc(s.f2_copied, 1)
                        act.drain()
                        act.activation(m.f2h[:, c, c0:c0 + w], m.f2[:, c, 0:w], ACT.Copy).then_inc(s.f2h_ready, 1)
                        f += 1
                t = tl["four"]
                for c in range(2):
                    for side, n, _ in lat_con:
                        act.wait_ge(s.acc_ready, t + 1)
                        bf = m.sm2[:, C2["b_f"] + 2 * l + c:C2["b_f"] + 2 * l + c + 1]
                        act.activation(x_dst(side)(c), ps[t % 4][:, 0:n], ACT.Identity, bias=bf).then_inc(s.oth_ready, 1)
                        t += 1
                    next2(S2_FOUR + c, t)
                for sl in range(4):
                    next2(S2_WOUT + sl, tl["wout"] + (sl + 1) * 2 * ns)
                for side, n, _ in lat_con:
                    norm2(f"ffn{l}{side}")
                    heads2(f"ffn{l}{side}", KT, n, x_dst(side), lambda k, side=side: m.mod[:, 3, k, side:side + 1])
                for c, (pair0, pairs, first) in enumerate(FFN_CHUNKS):
                    with act.Fori(0, pairs // 2) as i:
                        for sl in range(2):
                            for side, n, c0 in lat_con:
                                u = 2 * i + sl
                                for g, buf in ((0, m.cg), (1, m.cv)):
                                    col = 44 * 3 * l + 44 + 22 * g + pair0 + u
                                    bcol = 44 * l + 22 * g + pair0 + u
                                    t = tl[f"up{c}"] + sl * 2 * ns + 2 * side + g
                                    act.wait_ge(s.acc_ready, t + 1 + 4 * ns * i)
                                    hold(act, s.gu_ready, GL_BASE[l] + (8 * c + u) * ns + side + 1)
                                    act.activation(buf[:, 0:n], ps[t % 4][:, 0:n], ACT.Identity,
                                                   bias=m.sm2[:, bass.ds(C2["b_dw"] + bcol, 1)],
                                                   scale=m.sm2[:, bass.ds(C2["w_dw"] + col, 1)]).then_inc(s.mid_ready, 1)
                                if side == ns - 1:
                                    next2(first + sl, tl[f"up{c}"] + (sl + 1) * 2 * ns + 4 * ns * i, i, 2)
                                at = GL_BASE[l] + (8 * c + u) * ns + side
                                act.wait_ge(s.acc_free, tl[f"up{c}"] + sl * 2 * ns + 2 * side + 5 - FREE_OFF + 4 * ns * i)
                                act.activation(m.sgl[:, 0:n], m.cg[:, 0:n], ACT.Silu).then_inc(s.silu_ready, 1)
                                hold(act, s.gu_ready, at + 2)
                                act.activation(m.gh[:, bass.ds(u, 1), c0:c0 + n].rearrange("p a n -> p (a n)"),
                                               m.gu[:, 0:n], ACT.Copy).then_inc(s.gh_ready, 1)
                    down = first + pairs
                    for sl in range(4):
                        next2(down + sl, tl[f"down{c}"] + (sl + 1) * 2 * ns)
            norm2("final")

        @block.vector
        def _(dve):
            STT, TT, TS = nc.vector.scalar_tensor_tensor, nc.vector.tensor_tensor, nc.vector.tensor_scalar

            def split(slab, slot):
                dve.wait_ge(s.hi_ready, slab + 3)
                TT(m.wlo[:, slot, :], m.wst[:, slot, :], m.whi[:, slot, :].bitcast(F32), ALU.subtract
                   ).then_inc(s.lo_ready, 1)

            def rotate(rope, src, dests, rows=P, frees=None):
                dve.drain()
                dve.wait_ge(s.swap_ready, rope[0] + 1)
                xs = m.xs[0:rows, rope[1], :]
                ins = TT(m.xc[0:rows, :], src[0:rows, :], m.cosT[0:rows, :], ALU.mult)
                if frees:
                    ins.then_inc(s.acc_free, frees)
                TT(xs, xs, m.sinT[0:rows, :], ALU.mult)
                dve.drain()
                for r0, r1, dst in dests:
                    ins = TT(dst, m.xc[r0:r1, :], m.xs[r0:r1, rope[1], :], ALU.add)
                ins.then_inc(s.rope_done, 1)

            def col(buf, i):
                return buf[:, bass.ds(i, 1), :].rearrange("p a n -> p (a n)")

            def norm(n, gain, split_it):
                with dve.Fori(0, KT // 2) as kk:
                    for par in range(2):
                        dve.wait_ge(s.sq_used, n * KT + 2 * kk + par + 1)
                        h = col(m.hT, 2 * kk + par)
                        TT(m.sq[:, par, :], h, h, ALU.mult).then_inc(s.sq_ready, 1)
                dve.wait_ge(s.sq_used, (n + 1) * KT + 2)
                TS(m.rstd[:, :], ps[4][:, :], 1.0 / D, EPS, ALU.mult, ALU.add).then_inc(s.var_ready, 1)
                dve.wait_ge(s.std_ready, n + 1)
                nc.vector.reciprocal(m.rstd[:, :], m.rstd[:, :])
                dve.drain()
                def normed(k, dst):
                    return STT(dst, m.hT[:, k, :], m.sm1[:, bass.ds(gain + k, 1)], m.rstd[:, :], ALU.mult, ALU.mult)

                for k in range(KT):
                    if not split_it:
                        ins = normed(k, m.hT[:, k, :])
                        continue
                    if k == 0:
                        normed(0, m.xn[:, 0, :]).then_inc(s.xn_ready, 1)
                    if k + 1 < KT:
                        if k:
                            hold(dve, s.x_ready, n * KT + k)
                        normed(k + 1, m.xn[:, (k + 1) % 2, :]).then_inc(s.xn_ready, 1)
                    dve.wait_ge(s.xh_ready, n * KT + k + 1)
                    ins = TT(m.xl[:, k, :], m.xn[:, k % 2, :], m.xh[:, k, :].bitcast(F32), ALU.subtract)
                    ins.then_inc(s.x_ready, 1)
                if not split_it:
                    dve.drain()
                return ins

            def attention(item0, soft0, group, group0, pairs, segs, width, scale, heads, dst, sink=None):
                with dve.Fori(0, pairs) as i:
                    for par in range(2):
                        n = soft0 + 2 * i + par
                        dve.wait_ge(s.t_done, n + 1)
                        dve.wait_ge(s.s_done, item0 + 2 * i + par + 3)
                        for bank, c0, w, mask in segs(par):
                            ins = STT(m.S[:, par, c0:c0 + w], ps[bank][:, 0:w], scale, mask, ALU.mult, ALU.add)
                        ins.then_inc(s.s_free, 1)
                        if sink is not None:
                            nc.vector.tensor_copy(m.S[:, par, width - 1:width], sink(par, i))
                        dve.drain()
                        nc.vector.tensor_reduce(m.nmax[:, par:par + 1], m.S[:, par, 0:width], AX.X, ALU.max,
                                                negate=True).then_inc(s.max_ready, 1)
                dve.wait_ge(s.pv_done, soft0 + 2 * pairs + 2)
                nc.vector.reciprocal(m.rden[:, 0:heads], m.den[:, group % 2, 0:heads])
                dve.drain()
                TT(dst.rearrange("p (h d) -> p h d", d=HD),
                   ps[6 + group % 2][:, 0:heads * HD].rearrange("p (h d) -> p h d", d=HD),
                   m.rden[:, 0:heads].unsqueeze(2).broadcast_to([P, heads, HD]), ALU.mult).then_inc(s.o_ready, 1)

            dve.sem_inc(s.lo_ready, 2)
            dve.sem_inc(s.acc_free, 4)
            dve.sem_inc(s.rope_done, 2)
            dve.sem_inc(s.us_ready, 2)
            dve.sem_inc(s.o_ready, 2)
            dve.sem_inc(s.s_free, 2)
            dve.sem_inc(s.mt_ready, 1)
            dve.sem_inc(s.t2_copied, 1)
            dve.sem_inc(s.gu_ready, 1)
            dve.wait_ge(s.pos_in, 16)
            dve.wait_ge(s.consts_in, 48)
            c1 = 6.28125
            c2 = float(np.float32(np.round((TWO_PI - c1) * 2 ** 19) / 2 ** 19))
            c3 = float(np.float32(TWO_PI - c1 - c2))
            nc.vector.tensor_copy(m.ang[:, :], m.posi[:, :])
            dve.drain()
            TS(m.ang[:, :], m.ang[:, :], inv, None, ALU.mult)
            for which, dst in ((0, m.red), (1, m.ang)):
                dve.drain()
                TS(m.turns[:, :], m.ang[:, :], 1.0 / TWO_PI, 0.25 if which == 0 else 0.0, ALU.mult, ALU.add)
                dve.drain()
                TS(m.turns[:, :], m.turns[:, :], ROUND, -ROUND, ALU.add, ALU.add)
                dve.drain()
                STT(dst[:, :], m.turns[:, :], -c1, m.ang[:, :], ALU.mult, ALU.add)
                dve.drain()
                STT(dst[:, :], m.turns[:, :], -c2, dst[:, :], ALU.mult, ALU.add)
                dve.drain()
                STT(dst[:, :], m.turns[:, :], -c3, dst[:, :], ALU.mult, ALU.add)
                dve.drain()
                if which == 0:
                    TS(dst[:, :], dst[:, :], float(np.pi / 2), None, ALU.add)
                    dve.drain()
                TS(dst[:, :], dst[:, :], 3.1415925, -3.1415925, ALU.min, ALU.max).then_inc(s.angles, 1)
            dve.wait_ge(s.tables, 2)
            TS(m.sinT[:, :], m.sinT[:, :], sign, None, ALU.mult)
            dve.wait_ge(s.h_in, 16)
            split(0, 0)
            split(1, 1)
            with dve.Fori(0, DEPTH) as l:
                slab0, tile0, rope0 = l * SLABS1, l * TILES1, l * ROPES1
                norm(l * NORMS1, l * 8, True)

                def next_split(c, i=0, step=0):
                    split(slab0 + c + 2 + i * step, c % 2)

                def whole(ap):
                    return [(0, P, ap)]

                r = RP_A
                for sl in range(5):
                    if sl < 4:
                        for t in range(2):
                            tile = (0, 1, 2, 3, 8, 9, 10, 11)[r]
                            src = ps[(FR_A + tile) % 4]
                            if tile < 3:
                                dst = whole(m.AQ[:, tile, :])
                            elif tile == 3:
                                dst = [(0, HD, m.AK[0:HD, :]), (0, HD, m.AK[HD:P, :])]
                            else:
                                dst = whole(m.IQ[:, tile - 8, :])
                            rotate((rope0 + r, r % 2), src, dst, frees=1)
                            r += 1
                    if sl == 1:
                        for b in range(QB):
                            dve.wait_ge(s.acc_ready, tile0 + 4 + b + 1)
                            nc.vector.tensor_copy(m.VA[:, b, :], ps[(FR_A + 4 + b) % 4][:, 0:HD]
                                                  ).then_inc(s.acc_free, 1)
                    if sl == 4:
                        dve.wait_ge(s.acc_ready, tile0 + 13)
                        nc.vector.tensor_copy(m.ikraw[0:HD, :], ps[(FR_A + 12) % 4][0:HD, :]).then_inc(s.acc_free, 1)
                        dve.drain()
                        TT(m.iknorm[0:HD, :], m.ikraw[0:HD, :], m.ikraw[0:HD, :], ALU.mult).then_inc(s.ik_sq, 1)
                        for b in range(QB):
                            dve.wait_ge(s.acc_ready, tile0 + 13 + b + 1)
                            TS(m.IW[:, b, :], ps[(FR_A + 13 + b) % 4][:, 0:IDX_HEADS],
                               float(np.float32(IDX_HEADS ** -0.5)), None, ALU.mult).then_inc(s.acc_free, 1)
                    next_split(SL_A + sl)
                with dve.Fori(0, 3) as i:
                    for sl in range(2):
                        for t in range(2):
                            j = 2 * sl + t
                            rotate((rope0 + RP_B + 4 * i + j, (RP_B + j) % 2), ps[(FR_B + j) % 4],
                                   whole(col(m.BQK, 4 * i + j)), frees=1)
                        next_split(SL_B + sl, i, 2)
                dve.wait_ge(s.ik_stat, l + 1)
                TS(m.rstd[0:HD, :], ps[4][0:HD, :], 1.0 / HD, EPS, ALU.mult, ALU.add).then_inc(s.ik_var, 1)
                dve.wait_ge(s.ik_std, l + 1)
                nc.vector.reciprocal(m.rstd[0:HD, :], m.rstd[0:HD, :])
                dve.drain()
                STT(m.iknorm[0:HD, :], m.ikraw[0:HD, :], m.sm1[0:HD, bass.ds(40 + l, 1)], m.rstd[0:HD, :],
                    ALU.mult, ALU.mult).then_inc(s.ik_norm, 1)
                rotate((rope0 + RP_IK, RP_IK % 2), m.iknorm, [(0, HD, m.IK[0:HD, :]), (0, HD, m.IK[HD:P, :])], HD)
                for sl in range(3):
                    for b in range(QB):
                        t = 4 * sl + b
                        dve.wait_ge(s.acc_ready, tile0 + TL_BV + t + 1)
                        nc.vector.tensor_copy(m.VB[:, b, sl * 256:(sl + 1) * 256], ps[(FR_BV + t) % 4][:, 0:256]
                                              ).then_inc(s.acc_free, 1)
                    next_split(SL_BV + sl)
                for t in range(4):
                    r = RP_C + t
                    rotate((rope0 + r, r % 2), ps[(FR_C + t) % 4], whole(m.CQ[:, t, :]), frees=1)
                    if t % 2:
                        next_split(SL_C + t // 2)
                rotate((rope0 + RP_C + 4, (RP_C + 4) % 2), ps[(FR_C + 4) % 4], whole(m.CK[:, :]), frees=1)
                for b in range(QB):
                    dve.wait_ge(s.acc_ready, tile0 + TL_C + 5 + b + 1)
                    nc.vector.tensor_copy(m.VC[:, b, :], ps[(FR_C + 5 + b) % 4][:, 0:P]).then_inc(s.acc_free, 1)
                offs = {1: 0, 2: 256, 3: 640}
                for qb in range(1, QB):
                    n = (qb + 1) * P
                    acc = m.MA[:, offs[qb]:offs[qb] + n]
                    nc.vector.tensor_copy(acc, m.masks[:, M_CAUSAL + 512 - n:M_CAUSAL + 512])
                    with dve.Fori(0, IDX_HEADS // 2) as i:
                        for par in range(2):
                            item = l * ITEMS1 + IT_IDX + (qb - 1) * IDX_HEADS + 2 * i + par
                            dve.wait_ge(s.s_done, item + 3)
                            TS(m.R[:, par, 0:n], ps[par][:, 0:n], float(HD ** -0.5), 0.0, ALU.mult, ALU.max
                               ).then_inc(s.s_free, 1)
                            dve.drain()
                            STT(acc, m.R[:, par, 0:n], m.IW[:, qb, bass.ds(2 * i + par, 1)], acc,
                                ALU.mult, ALU.add)
                for qb in range(1, QB):
                    n = (qb + 1) * P
                    acc = m.MA[:, offs[qb]:offs[qb] + n]
                    dve.drain()
                    with dve.Fori(0, TOPK // 8) as _i:
                        nc.vector.max(m.top8[:, :], acc)
                        dve.drain()
                        nc.vector.match_replace(acc, m.top8[:, :], acc, TAKEN)
                        dve.drain()
                    TS(acc, acc, 0.5 * TAKEN, NEG, ALU.is_gt, ALU.mult)
                hold(dve, s.ada_turned, (l + 1) * ADA_SLABS)
                nc.vector.tensor_copy(m.mods[:, bass.ds(l, 1), :].rearrange("p a n -> p (a n)"),
                                      ps[7][:, 0:6 * KT * 2]).then_inc(s.mods_ready, 1)
                for sl in range(2):
                    split(slab0 + SL_MERGE + sl, sl)
                SC = HD ** -0.5
                for branch in range(3):
                    for qb in range(QB):
                        group = branch * QB + qb
                        n = (qb + 1) * P
                        near = P if qb == 0 else 2 * P
                        common = (group, l * GROUPS1)
                        mk = lambda base, size, w: m.masks[:, base + size - w:base + size]
                        if branch == 0:
                            mask = mk(M_CAUSAL, 512, n) if qb == 0 else m.MA[:, offs[qb]:offs[qb] + n]
                            attention(l * ITEMS1 + IT_A + qb * A_HEADS, l * SOFTS1 + SX_A + qb * A_HEADS, *common,
                                      A_HEADS // 2, lambda par: [(par, 0, n, mask)], n, SC, A_HEADS,
                                      m.OA[:, qb, :])
                        elif branch == 1:
                            segs = lambda par: [(0, 0, near, mk(M_B0, 256, near)), (1, near, n, mk(M_B1, 512, n)),
                                                (2, near + n, n, mk(M_B2, 512, n))]
                            attention(l * ITEMS1 + IT_B + qb * B_HPG, l * SOFTS1 + SX_B + qb * B_HPG, *common,
                                      B_HPG // 2, segs, near + 2 * n, SC, B_HPG, m.OB[:, qb, :])
                        else:
                            attention(l * ITEMS1 + IT_C + qb * C_HEADS, l * SOFTS1 + SX_C + qb * C_HEADS, *common,
                                      C_HEADS // 2, lambda par: [(par, 0, near, mk(M_C, 256, near))], near + 1, SC,
                                      C_HEADS, m.OC[:, qb, :],
                                      lambda par, i: m.sm1[:, bass.ds(42 + l * 8 + 4 * par + i, 1)])
                for j in range(9):
                    dve.wait_ge(s.oh_ready, l * 9 + j + 1)
                    TT(m.ol[:, j, :], m.of[:, j % 2, :], m.oh[:, j, :].bitcast(F32), ALU.subtract
                       ).then_inc(s.ol_ready, 1)
                with dve.Fori(0, 2) as jp:
                    for half in range(2):
                        for g in range(3):
                            next_split(SL_MERGE + 5 * half + g, jp, 10)
                        for b in range(3):
                            for t in range(2):
                                v = FR_MERGE + 6 * half + 2 * b + t
                                dve.drain()
                                dve.wait_ge(s.acc_ready, tile0 + TL_MERGE + 12 * half + 6 + 2 * b + t + 1 + 24 * jp)
                                if b == 0 and t == 0:
                                    dve.wait_ge(s.gate_free, l * 24 + 12 * jp + 6 * half + 6 + 4)
                                if b == 0:
                                    dve.wait_ge(s.mh_ready, l * 8 + 4 * jp + 2 * half + 1)
                                    TT(m.mt[:, t, :], ps[v % 4][:, :], m.sg[:, t, :], ALU.mult).then_inc(s.acc_free, 1)
                                    continue
                                TT(m.mtmp[:, :], ps[v % 4][:, :], m.sg[:, 2 * b + t, :], ALU.mult
                                   ).then_inc(s.acc_free, 1)
                                dve.drain()
                                ins = TT(m.mt[:, t, :], m.mt[:, t, :], m.mtmp[:, :], ALU.add)
                                if b == 2:
                                    ins.then_inc(s.mt_ready, 1)
                            if b == 1:
                                next_split(SL_MERGE + 5 * half + 3, jp, 10)
                        next_split(SL_MERGE + 5 * half + 4, jp, 10)
                        for t in range(2):
                            k = 4 * jp + 2 * half + t
                            dve.wait_ge(s.mh_ready, l * 8 + k + 2)
                            TT(col(m.ml, k), m.mt[:, t, :], col(m.mh, k).bitcast(F32), ALU.subtract
                               ).then_inc(s.m_ready, 1)
                with dve.Fori(0, 2) as i:
                    for sl in range(2):
                        for t in range(2):
                            j = 2 * sl + t
                            dve.wait_ge(s.acc_ready, tile0 + TL_WO + 4 * i + j + 1)
                            h = col(m.hT, 4 * i + j)
                            TT(h, h, ps[(FR_WO + j) % 4][:, :], ALU.add).then_inc(s.acc_free, 1)
                        next_split(SL_WO + sl, i, 2)
                dve.drain()
                norm(l * NORMS1 + 1, 16 + l * 8, True)
                with dve.Fori(0, 4) as q:
                    with dve.Fori(0, 2) as i:
                        for sl in range(2):
                            for t in range(2):
                                n = l * 32 + 8 * q + 4 * i + 2 * sl + t
                                dve.wait_ge(s.relu_ready, n + 1)
                                TT(m.us[:, t, :], m.ur[:, t, :], m.ur[:, t, :], ALU.mult).then_inc(s.us_ready, 1)
                                dve.wait_ge(s.uh_ready, n + 1)
                                k = 4 * i + 2 * sl + t
                                TT(col(m.ul, k), m.us[:, t, :], col(m.uh, k).bitcast(F32), ALU.subtract
                                   ).then_inc(s.acc_free, 1)
                            next_split(SL_MLP + sl, 8 * q + 2 * i, 1)
                    with dve.Fori(0, 2) as i:
                        for sl in range(2):
                            for t in range(2):
                                j = 2 * sl + t
                                dve.wait_ge(s.acc_ready, tile0 + TL_MLP + 8 + 16 * q + 4 * i + j + 1)
                                h = col(m.hT, 4 * i + j)
                                TT(h, h, ps[(FR_MLP + j) % 4][:, :], ALU.add).then_inc(s.acc_free, 1)
                            next_split(SL_MLP + 4 + sl, 8 * q + 2 * i, 1)
                dve.drain()
                dve.sem_inc(s.acc_free, 2)
            norm(DEPTH * NORMS1, 32, False)
            dve.sem_inc(s.h_ready, KT)
            def norm2(name, kt, n, src, gain, shift=None, dst=None, width=D):
                k0, n0 = NORMS2[name]
                for k in range(kt):
                    dve.wait_ge(s.sq_used, k0 + k + 1)
                    h = src(k)
                    TT(m.sq2[:, (k0 + k) % 2, 0:n], h, h, ALU.mult).then_inc(s.sq_ready, 1)
                dve.wait_ge(s.sq_used, k0 + kt + 2)
                TS(m.rstd2[:, 0:n], ps[4][:, 0:n], 1.0 / width, EPS, ALU.mult, ALU.add).then_inc(s.var_ready, 1)
                dve.wait_ge(s.std_ready, n0 + 1)
                nc.vector.reciprocal(m.rstd2[:, 0:n], m.rstd2[:, 0:n])
                dve.drain()
                def normed(k):
                    xn = m.xn2[:, (k0 + k) % 2, 0:n]
                    STT(xn, src(k), gain(k), m.rstd2[:, 0:n], ALU.mult, ALU.mult).then_inc(s.xn_ready, 1)

                for k in range(kt):
                    if dst is None:
                        last = STT(src(k), src(k), gain(k), m.rstd2[:, 0:n], ALU.mult, ALU.mult)
                        continue
                    if k == 0:
                        normed(0)
                    if k + 1 < kt:
                        if k:
                            dve.wait_ge(s.x_ready, k0 + k - X_OFF)
                        normed(k + 1)
                    head, tail = dst
                    xn = m.xn2[:, (k0 + k) % 2, 0:n]
                    dve.wait_ge(s.xh_ready, k0 + k + 1 - X_OFF)
                    if shift is None:
                        last = TT(tail(k), xn, head(k).bitcast(F32), ALU.subtract)
                    else:
                        last = STT(tail(k), xn, shift(k), head(k).bitcast(F32), ALU.add, ALU.subtract)
                    last.then_inc(s.x_ready, 1)
                return last

            def x_pair(side):
                a, b = (m.xch, m.xcl) if side else (m.xh, m.xl)
                return (lambda k: a[:, k, :]), (lambda k: b[:, k, :])

            dve.sem_inc(s.o2_ready, 2)
            dve.wait_ge(s.sm2_in, 16)
            dve.wait_ge(s.ctx_in, 32)
            for l in range(DEPTH):
                tl = tiles2(l)
                lat_con = pieces(l)
                ns = len(lat_con)

                def next2(c, i=0, step=0):
                    if l == DEPTH - 1 and isinstance(i, int) and c + 2 >= SLABS2:
                        return
                    number, slot, _ = slab2(l, c + 2, i, step)
                    split(number, slot)

                def ready(tile):
                    dve.wait_ge(s.acc_ready, tile + 1)

                mod = m.mod[:, :, :, :].rearrange("p a k s -> p (a k s)")
                TT(mod, m.mods[:, l, :], m.sm2[:, C2["b_ada"] + 96 * l:C2["b_ada"] + 96 * (l + 1)], ALU.add)
                dve.drain()
                for a, (part, name) in enumerate(((1, "g_mix"), (4, "g_ffn"))):
                    g = m.sm2[:, C2[name] + 16 * l:C2[name] + 16 * l + 16].rearrange("p (k s) -> p k s", s=2)
                    ins = STT(m.G[:, a, :, :], m.mod[:, part, :, :], 1.0, g, ALU.add, ALU.mult)
                ins.then_inc(s.mod_ready, 1)
                dve.drain()

                def residual(side):
                    return (lambda k: m.cT[:, k, :]) if side else (lambda k: m.hT[:, k, :])

                def modulated(which, name, sides):
                    for side, n, _ in sides:
                        norm2(f"{name}{l}{side}", KT, n, residual(side),
                              lambda k: m.G[:, which, k, side:side + 1],
                              lambda k: m.mod[:, 3 * which, k, side:side + 1], x_pair(side))

                modulated(0, "mix", pieces(l, True))
                t = tl["win"]
                for c in range(7):
                    for side, n, c0 in pieces(l, l == 0 or c >= 5):
                        ready(t)
                        bank = ps[t % 4]
                        if c < 6:
                            dst = m.fT[:, c, c0:c0 + n] if c < 2 else (
                                m.cqr[:, c - 2, c0:c0 + n] if c < 5 else m.ckvr[:, c0:c0 + n])
                            nc.vector.tensor_copy(dst, bank[:, 0:n]).then_inc(s.acc_free, 1)
                        elif side == 0:
                            TT(m.krr[64:96, 0, 0:T], bank[64:96, :], m.ropes[64:96, 1, :], ALU.mult)
                            TT(m.krr[64:96, 1, 0:T], bank[96:128, :], m.ropes[96:128, 1, :], ALU.mult
                               ).then_inc(s.acc_free, 1)
                            dve.drain()
                            TT(m.krr[64:96, 0, 0:T], m.krr[64:96, 0, 0:T], m.krr[64:96, 1, 0:T], ALU.add)
                        else:
                            nc.vector.tensor_copy(m.krr[64:96, 0, T:TA], bank[64:96, 0:n]).then_inc(s.acc_free, 1)
                            dve.drain()
                            dve.sem_inc(s.kr_ready, 1)
                        t += 1
                    if c % 2 == 1 or c == 6:
                        next2(S2_WIN + c // 2)
                for side, n, c0 in lat_con:
                    norm2(f"q{l}{side}", 3, n, lambda k: m.cqr[:, k, c0:c0 + n],
                          lambda k: m.sm2[:, C2["g_q"] + 3 * l + k:C2["g_q"] + 3 * l + k + 1], None,
                          ((lambda k: m.cqh[:, k, c0:c0 + n]), (lambda k: m.cql[:, k, c0:c0 + n])), FQ)
                for side, n, c0 in pieces(l, True):
                    norm2(f"kv{l}{side}", 1, n, lambda k: m.ckvr[:, c0:c0 + n],
                          lambda k: m.sm2[:, C2["g_kv"] + l:C2["g_kv"] + l + 1], None,
                          ((lambda k: m.ckvh[:, c0:c0 + n]), (lambda k: m.ckvl[:, c0:c0 + n])), FKV)
                items = items2(l)
                per = 24 if l == 0 else 20
                with dve.Fori(0, 3) as hg:
                    tile = tl["hg"]
                    for j in range(HG):
                        for side, n, c0 in lat_con:
                            bank = ps[tile % 4]
                            if side == 0:
                                dve.drain()
                            ready(tile + per * hg)
                            if side == 0:
                                TT(m.rt[64:96, 0, :], bank[64:96, :], m.ropes[64:96, 0, :], ALU.mult)
                                TT(m.rt[64:96, 1, :], bank[96:128, :], m.ropes[96:128, 0, :], ALU.mult)
                                dve.drain()
                                dve.wait_ge(s.q4_part, 4 * (3 * l + hg) + j + 1)
                                TT(m.Q4[64:96, j, 0:T], m.rt[64:96, 0, :], m.rt[64:96, 1, :], ALU.add
                                   ).then_inc(s.acc_free, 1)
                            else:
                                TS(m.Q4[0:QH, j, T:TA], bank[0:QH, 0:n], SM, None, ALU.mult).then_inc(s.acc_free, 1)
                            tile += 1
                    next2(S2_HG, hg, 2)
                    for j in range(HG):
                        for side, n, c0 in pieces(l, True):
                            ready(tile + per * hg)
                            nc.vector.tensor_copy(m.K4[0:64, j, c0:c0 + n], ps[tile % 4][0:64, 0:n]
                                                  ).then_inc(s.acc_free, 1)
                            tile += 1
                    for blk in range(6):
                        ready(tile + per * hg)
                        nc.vector.tensor_copy(m.V4[:, blk, :], ps[tile % 4][:, 0:HG * VH]
                                              ).then_inc(s.acc_free, 3 if blk == 5 else 1)
                        tile += 1
                    next2(S2_HG + 1, hg, 2)

                    def item(n):
                        return item_base2(l) + len(items) * hg + n

                    def maximum(n):
                        w = TA if items[n][2] == 0 else TC
                        dve.wait_ge(s.s2_done, item(n) + 3)
                        nc.vector.tensor_reduce(m.nmax2[:, n % 2:n % 2 + 1], psum[:, 1024 * (n % 2):1024 * (n % 2) + w],
                                                AX.X, ALU.max, negate=True).then_inc(s.max2_ready, 1)

                    def copied(n):
                        w = TA if items[n][2] == 0 else TC
                        dve.wait_ge(s.pv2_done, item(n) + 1)
                        dve.wait_ge(s.t2_done, item(n) + 3)
                        nc.vector.tensor_copy(m.PT2[:, n % 2, 0:w], psum[:, 2048:2048 + w]).then_inc(s.t2_copied, 1)

                    def normalized(n):
                        qb, _, side = items[n]
                        par = n // HG % 2
                        dve.drain()
                        dve.wait_ge(s.pv2_done, item(n) + 3)
                        nc.vector.reciprocal(m.rden2[:, :], m.den2[:, par, :])
                        dve.drain()
                        TT(m.O2[:, 4 * side + qb, bass.ds(hg * (HG * VH), HG * VH)].rearrange("p (h d) -> p h d", d=VH),
                           ps[6 + par][:, 0:HG * VH].rearrange("p (h d) -> p h d", d=VH),
                           m.rden2[:, :].unsqueeze(2).broadcast_to([P, HG, VH]), ALU.mult).then_inc(s.o2_ready, 1)

                    maximum(0)
                    for n in range(len(items)):
                        if n + 1 < len(items):
                            maximum(n + 1)
                        copied(n)
                        if n > HG - 1 and n % HG == 0:
                            normalized(n - 1)
                    normalized(len(items) - 1)
                n, at_ = 12 * l, 16 * l
                for j in range(6):
                    for side, w, _ in lat_con:
                        head, tail = x_pair(side)
                        dve.wait_ge(s.oth_ready, at_ + 1)
                        TT(tail(2 + j), m.ot2[:, n % 2, 0:w], head(2 + j).bitcast(F32), ALU.subtract
                           ).then_inc(s.mixed, 1)
                        n += 1
                        at_ += 1
                f = 4 * l
                for side, w, c0 in lat_con:
                    for c in range(2):
                        dve.wait_ge(s.f2h_ready, f + 1)
                        TT(m.f2l[:, c, c0:c0 + w], m.f2[:, c, 0:w], m.f2h[:, c, c0:c0 + w].bitcast(F32), ALU.subtract
                           ).then_inc(s.f2_split, 1)
                        f += 1
                t = tl["four"]
                for c in range(2):
                    bf = m.sm2[:, C2["b_f"] + 2 * l + c:C2["b_f"] + 2 * l + c + 1]
                    for side, n, _ in lat_con:
                        head, tail = x_pair(side)
                        dve.wait_ge(s.oth_ready, at_ + 1)
                        STT(tail(c), ps[t % 4][:, 0:n], bf, head(c).bitcast(F32), ALU.add, ALU.subtract
                            ).then_inc(s.acc_free, 1)
                        t += 1
                        at_ += 1
                    next2(S2_FOUR + c)
                dve.drain()
                dve.sem_inc(s.mixed, 2 * ns)

                def gated_residual(t, gate, col, side, n, i=0):
                    if isinstance(col, int):
                        h, g = residual(side)(col), m.mod[:, gate, col, side:side + 1]
                    else:
                        buf = m.cT if side else m.hT
                        h = buf[:, bass.ds(col, 1), :].rearrange("p a n -> p (a n)")
                        g = mod[:, bass.ds(16 * gate + 2 * col + side, 1)]
                    STT(h, ps[t % 4][:, 0:n], g, h, ALU.mult, ALU.add).then_inc(s.acc_free, 1)

                t = tl["wout"]
                for sl in range(4):
                    for h in range(2):
                        for side, n, _ in lat_con:
                            ready(t)
                            gated_residual(t, 2, 2 * sl + h, side, n)
                            t += 1
                    next2(S2_WOUT + sl)
                dve.drain()
                modulated(1, "ffn", lat_con)
                for c, (pair0, pairs, first) in enumerate(FFN_CHUNKS):
                    with dve.Fori(0, pairs // 2) as i:
                        for sl in range(2):
                            for side, n, c0 in lat_con:
                                u = 2 * i + sl
                                at_ = GL_BASE[l] + (8 * c + u) * ns + side
                                for g, buf in ((0, m.cg), (1, m.cv)):
                                    t = tl[f"up{c}"] + sl * 2 * ns + 2 * side + g
                                    bank = ps[t % 4]
                                    tap = lambda k: m.sm2[:, bass.ds(C2["w_dw"] + 132 * l + 44 * k + 22 * g + pair0 + u, 1)]
                                    dve.wait_ge(s.mid_ready, 2 * at_ + g + 1)
                                    STT(buf[:, 1:n], bank[:, 0:n - 1], tap(0), buf[:, 1:n], ALU.mult, ALU.add)
                                    dve.drain()
                                    STT(buf[:, 0:n - 1], bank[:, 1:n], tap(2), buf[:, 0:n - 1], ALU.mult, ALU.add
                                        ).then_inc(s.acc_free, 1)
                                if side == ns - 1:
                                    next2(first + sl, i, 2)
                                dve.drain()
                                dve.wait_ge(s.silu_ready, at_ + 1)
                                TT(m.gu[:, 0:n], m.sgl[:, 0:n], m.cv[:, 0:n], ALU.mult).then_inc(s.gu_ready, 1)
                                dve.wait_ge(s.gh_ready, at_ + 1)
                                TT(m.gl[:, bass.ds(u, 1), c0:c0 + n].rearrange("p a n -> p (a n)"), m.gu[:, 0:n],
                                   m.gh[:, bass.ds(u, 1), c0:c0 + n].rearrange("p a n -> p (a n)").bitcast(F32),
                                   ALU.subtract).then_inc(s.gl_ready, 1)
                    for sl in range(4):
                        for g in range(2):
                            for side, n, c0 in lat_con:
                                t = tl[f"down{c}"] + sl * 2 * ns + g * ns + side
                                ready(t)
                                gated_residual(t, 5, 2 * sl + g, side, n)
                        next2(first + pairs + sl)
                dve.drain()
            last = norm2("final", KT, T, lambda k: m.hT[:, k, :],
                         lambda k: m.sm2[:, C2["g_final"] + k:C2["g_final"] + k + 1])
            last.then_inc(s.final_ready, 1)



def _slab(w):
    kt, n = w.shape[0] // P, w.shape[1]
    out = np.zeros((P, KT, 256), w.dtype)
    out[:, :kt, :n] = w.reshape(kt, P, n).transpose(1, 0, 2)
    return out.reshape(P, SLAB)


def _columns(v):
    return v.reshape(-1, P).T


def _features(x):
    return np.ascontiguousarray(x.T.reshape(-1, P, x.shape[0]).transpose(1, 0, 2))


def _stream_1(w_in, w_a, w_b, w_c, w_o, w_up, w_down, w_ada):
    slabs = []
    for l in range(DEPTH):
        w = w_in[l]
        slabs += [_slab(w[:, c:c + 256]) for c in range(0, 1280, 256)]
        slabs += [_slab(w[:, c:c + 256]) for c in range(COL_BQ, COL_BV + 768, 256)]
        cq = w[:, COL_CQ:COL_CK].reshape(D, 2, 4, HD).transpose(0, 2, 1, 3).reshape(D, 8 * HD)
        slabs += [_slab(cq[:, 0:256]), _slab(cq[:, 256:512]),
                  _slab(w[:, COL_CK:COL_CK + P]), _slab(w[:, COL_CV:COL_CV + P])]
        slabs += [_slab(w_ada[l][:, c:c + 256]) for c in range(0, 6 * D, 256)]
        for c in range(0, D, 256):
            slabs += [_slab(w[:, COL_G + g * D + c:COL_G + g * D + c + 256]) for g in range(3)]
            slabs += [_slab(np.concatenate([w_a[l][:, c:c + 256], w_b[l][:, c:c + 256]])), _slab(w_c[l][:, c:c + 256])]
        slabs += [_slab(w_o[l][:, c:c + 256]) for c in range(0, D, 256)]
        for q in range(0, D_FF, D):
            slabs += [_slab(w_up[l][:, q + c:q + c + 256]) for c in range(0, D, 256)]
            slabs += [_slab(w_down[l][q:q + D, c:c + 256]) for c in range(0, D, 256)]
    return slabs


def _arrays_1(x, positions, attn_norm, w_in, idx_k_norm, sinks, w_a, w_b, w_c, w_o, mlp_norm, w_up, w_down,
              final_norm, c, c_ctx):
    small = np.zeros((P, 74), np.float32)
    small[:, 0:16] = _columns(attn_norm)
    small[:, 16:32] = _columns(mlp_norm)
    small[:, 32:40] = _columns(final_norm)
    small[:HD, 40:42] = idx_k_norm.T
    small[:, 42:58] = sinks.reshape(1, -1)
    small[:, 58:74] = np.stack([_columns(c), _columns(c_ctx)], axis=2).reshape(P, 16)
    return {
        "x_t": _features(x[0]), "pos": np.ascontiguousarray(np.broadcast_to(positions[0], (P, T))),
        "small_1": small, **shape_constants(),
    }


def _stream_2(w_in, w_fourier, w_q_b, w_kv_b, w_out, w_up, w_down):
    slabs = []
    for l in range(DEPTH):
        w = w_in[l]
        kr = np.zeros((D, P), w.dtype)
        kr[:, 64:96] = w[:, 768:800]
        kr[:, 96:112], kr[:, 112:128] = w[:, 784:800], w[:, 768:784]
        slabs += [_slab(w[:, c:c + 256]) for c in (0, 256, 512)] + [_slab(kr)]
        q = w_q_b[l].reshape(FQ, KH, QH)
        q = np.concatenate([q, q[:, :, 80:96], q[:, :, 64:80]], axis=2)
        kv = w_kv_b[l].reshape(FKV, KH, P)
        for h in range(0, KH, HG):
            a = np.zeros((P, SLAB), w.dtype)
            a[:, :3 * 512] = q[:, h:h + HG].reshape(3, P, 512).transpose(1, 0, 2).reshape(P, 3 * 512)
            b = np.zeros((P, SLAB), w.dtype)
            b[:, :512] = kv[:, h:h + HG].reshape(P, 512)
            slabs += [a, b]
        slabs += [_slab(w_fourier[l][:, c:c + P]) for c in (0, P)]
        slabs += [_slab(w_out[l][:, c:c + 256]) for c in range(0, D, 256)]
        for pair0, pairs, _ in FFN_CHUNKS:
            for u in range(pair0, pair0 + pairs):
                slabs.append(_slab(np.concatenate([w_up[l][:, u * P:(u + 1) * P],
                                                   w_up[l][:, FF2 + u * P:FF2 + (u + 1) * P]], axis=1)))
            rows = w_down[l][pair0 * P:(pair0 + pairs) * P]
            slabs += [_slab(rows[:, c:c + 256]) for c in range(0, D, 256)]
    return slabs


def _arrays_2(ctx, b_ada, g_mix, b_fourier, g_q_a, g_kv_a, g_ffn, w_dw, b_dw, g_final):
    twice = lambda v: np.repeat(_columns(v), 2, axis=1)
    parts = {
        "b_ada": twice(b_ada), "g_mix": twice(g_mix), "g_ffn": twice(g_ffn), "g_final": _columns(g_final),
        "b_f": _columns(b_fourier), "g_q": _columns(g_q_a), "g_kv": _columns(g_kv_a), "w_dw": _columns(w_dw),
        "b_dw": _columns(b_dw),
    }
    small = np.concatenate([parts[name] for name in C2], axis=1)
    assert small.shape[1] == SMALL2
    return {"small_2": small, "ctx_t": _features(ctx[0]), **shape_constants_2()}


def kernel(**inputs):
    import concourse.bacc as bacc
    from concourse.bass_utils import run_bass_kernel_spmd

    a = {k: np.asarray(v) for k, v in inputs.items()}
    arrays = _arrays_1(*[a[k] for k in ("x", "positions", "attn_norm", "w_in", "idx_k_norm", "sinks", "w_a", "w_b",
                                        "w_c", "w_o", "mlp_norm", "w_up", "w_down", "final_norm", "c_2",
                                        "c_ctx_2")])
    arrays.update(_arrays_2(*[a[k + "_2"] for k in ("ctx", "b_ada", "g_mix", "b_fourier", "g_q_a",
                                                    "g_kv_a", "g_ffn", "w_dw", "b_dw", "g_final")]))
    slabs = _stream_1(*[a[k] for k in ("w_in", "w_a", "w_b", "w_c", "w_o", "w_up", "w_down", "w_ada_2")])
    slabs += _stream_2(*[a[k + "_2"] for k in ("w_in", "w_fourier", "w_q_b", "w_kv_b", "w_out", "w_up",
                                               "w_down")])
    assert len(slabs) == SLABS_ALL
    arrays["weights"] = np.stack(slabs)
    nc = bacc.Bacc("TRN2", target_bir_lowering=False, num_devices=1)
    io = {}
    for name, v in arrays.items():
        io[name] = nc.dram_tensor(name, v.shape, mybir.dt.from_np(v.dtype), kind="ExternalInput").ap()
    out = nc.dram_tensor("out", (P, KT, T), F32, kind="ExternalOutput").ap()
    two_stacks(nc, io, out)
    r = run_bass_kernel_spmd(nc, [arrays], core_ids=[0])
    return np.ascontiguousarray(r.results[0]["out"].transpose(2, 1, 0)).reshape(1, T, D)
```

```python
from contextlib import ExitStack

import numpy as np

import concourse.bass as bass
from concourse import mybir

P = 128
F32 = mybir.dt.float32
F32R = mybir.dt.float32r
I32 = mybir.dt.int32
ACT = mybir.ActivationFunctionType
ALU = mybir.AluOpType
AX = mybir.AxisListType

D = 1024
KT = D // P
T = 512
QB = T // P
DEPTH = 2
HD = 64
EPS = 1e-6
NEG = -1e30
TAKEN = -3e38
TOPK = 128
SLAB = 2048
TWO_PI = 2.0 * np.pi
ROUND = 1.5 * 2.0 ** 23

A_HEADS, IDX_HEADS, B_HPG, C_HEADS = 6, 8, 4, 8
COL_AQ = 0
COL_AK = COL_AQ + A_HEADS * HD
COL_IQ = COL_AK + 2 * HD
COL_IK = COL_IQ + IDX_HEADS * HD
COL_BQ = COL_IK + HD + IDX_HEADS
COL_BV = COL_BQ + 2 * 3 * B_HPG * HD
COL_CQ = COL_BV + 3 * B_HPG * HD
COL_CK = COL_CQ + C_HEADS * HD
COL_CV = COL_CK + 2 * HD
COL_G = COL_CV + 2 * HD
D_FF = 4 * D

SL_A, SL_B, SL_BV, SL_C, SL_ADA, SL_MERGE, SL_WO, SL_MLP, SLABS1 = 0, 5, 11, 14, 18, 42, 62, 66, 98
ADA_SLABS = SL_MERGE - SL_ADA
TL_A, TL_B, TL_BV, TL_C, TL_MERGE, TL_WO, TL_MLP, TILES1 = 0, 17, 29, 41, 50, 98, 106, 170
FR_A, FR_B, FR_BV, FR_C, FR_MERGE, FR_WO, FR_MLP, FREES1 = 0, 17, 29, 41, 50, 74, 82, 148
RP_A, RP_B, RP_IK, RP_C, ROPES1 = 0, 8, 20, 21, 26
IT_IDX = 0
IT_A = IT_IDX + (QB - 1) * IDX_HEADS
IT_B = IT_A + QB * A_HEADS
IT_C = IT_B + QB * B_HPG
ITEMS1 = IT_C + QB * C_HEADS
SX_A, SX_B, SX_C, SOFTS1 = 0, QB * A_HEADS, QB * (A_HEADS + B_HPG), QB * (A_HEADS + B_HPG + C_HEADS)
GROUPS1 = 3 * QB
NORMS1 = 2

M_CAUSAL = 0
M_C = M_CAUSAL + 512
M_B0 = M_C + 256
M_B1 = M_B0 + 256
M_B2 = M_B1 + 512
MASKS = M_B2 + 512


def shape_constants():
    q = np.arange(P)[:, None]
    s = np.arange(P)[None, :]
    ok = lambda m: np.where(m, 0.0, NEG).astype(np.float32)
    causal = ok(s <= q)
    free = np.zeros((P, 3 * P), np.float32)
    parts = [free, causal, ok(s > q), causal, ok(s >= q), causal]
    for dilation in (4, 16):
        near = (q - s) % dilation == 0
        parts += [ok(near)] * 3 + [ok(near & (s <= q))]
    masks = np.concatenate(parts, axis=1)
    half = HD // 2
    inv = (np.float32(10000.0) ** (-np.arange(half, dtype=np.float32) / np.float32(half))).astype(np.float32)
    inv = np.tile(inv, 4)[:, None]
    sign = np.where((np.arange(P) // half) % 2 == 0, -1.0, 1.0).astype(np.float32)[:, None]
    ident = np.eye(P, dtype=np.float32)
    ones = np.ones((P, P), np.float32)
    return {"c_masks": masks, "c_ident": np.concatenate([ident, ones, inv, sign], axis=1)}

TC = 256
TA = T + TC
KH, QH, RH, VH = 12, 96, 32, 64
HG = 4
FQ, FKV = 384, 128
FF2 = 2816
SM = QH ** -0.5
S2_WIN, S2_HG, S2_FOUR, S2_WOUT, S2_FFN, SLABS2 = 0, 4, 10, 12, 16, 50
FFN_CHUNKS = ((0, 8, 16), (8, 8, 28), (16, 6, 40))
TILE_BASE2 = DEPTH * TILES1
FREE_OFF = DEPTH * (TILES1 - FREES1)
SLAB_BASE2 = DEPTH * SLABS1
SLABS_ALL = DEPTH * (SLABS1 + SLABS2)


def tiles2(l):
    sides = 2 if l == 0 else 1
    counts = [("win", 14 if l == 0 else 9), ("hg", 3 * (24 if l == 0 else 20)), ("four", 2 * sides),
              ("wout", 8 * sides)]
    for c, (_, pairs, _) in enumerate(FFN_CHUNKS):
        counts += [(f"up{c}", 2 * pairs * sides), (f"down{c}", 8 * sides)]
    base = TILE_BASE2 if l == 0 else tiles2(0)["end"]
    out = {}
    for name, n in counts:
        out[name] = base
        base += n
    out["end"] = base
    return out


def slab2(l, c, i=0, step=0):
    return slab_of(SLAB_BASE2 + l * SLABS2 + c, 0, 0, i, step)


def pieces(l, both=None):
    lat, con = (0, T, 0), (1, TC, T)
    return (lat, con) if (l == 0 if both is None else both) else (lat,)


def win_steps(l):
    t, out = tiles2(l)["win"], []
    order = {0: (0, 1), 1: (2, 3), 2: (4, 5), 3: (6,)}
    both = lambda c: l == 0 or c in (3, 6)
    for side, n, c0 in pieces(l, True):
        out.append(("norm", f"mix{l}{side}", KT, n, c0))
        if side == 0:
            out.append(("slab", 0))
        out += [("tile", c, side, n, c0) for c in order[0] if side == 0 or both(c)]
    out += [("split", 0), ("slab", 1)]
    out += [("tile", c, side, n, c0) for side, n, c0 in pieces(l, True) for c in order[1] if side == 0 or both(c)]
    out += [("split", 1)]
    for side, n, c0 in pieces(l):
        out.append(("norm", f"q{l}{side}", 3, n, c0))
        if side == 0:
            out.append(("slab", 2))
        out += [("tile", c, side, n, c0) for c in order[2]]
    out.append(("split", 2))
    for side, n, c0 in pieces(l, True):
        out.append(("norm", f"kv{l}{side}", 1, n, c0))
        if side == 0:
            out.append(("slab", 3))
        out.append(("tile", 6, side, n, c0))
    out.append(("split", 3))
    numbered = []
    for step in out:
        if step[0] == "tile":
            step = ("tile", t) + step[1:]
            t += 1
        numbered.append(step)
    return numbered


def summed(name):
    return name[:3] == "ffn" or name in ("mix10", "mix11", "final")


def norms2():
    k, n, out = (DEPTH * NORMS1 + 1) * KT, DEPTH * NORMS1 + 1, {}
    for l in range(DEPTH):
        for name, kt, piece in [(f"mix{l}0", KT, 1), (f"mix{l}1", KT, 1), (f"q{l}0", 3, 1)] + (
                [("q01", 3, 1)] if l == 0 else []) + [(f"kv{l}0", 1, 1), (f"kv{l}1", 1, 1), (f"ffn{l}0", KT, 1)] + (
                [("ffn01", KT, 1)] if l == 0 else []):
            out[name] = (k, n)
            k += kt
            n += piece
    out["final"] = (k, n)
    return out


NORMS2 = norms2()
X_OFF = KT
GL_BASE = {0: 0, 1: 44}


def items2(l):
    return [(qb, j, 0) for qb in range(QB) for j in range(HG)] + (
        [(qb, j, 1) for qb in range(TC // P) for j in range(HG)] if l == 0 else [])


def item_base2(l):
    return 0 if l == 0 else 3 * len(items2(0))


def group_base2(l):
    return item_base2(l) // HG


C2 = {}
_at = 0
for _name, _n in (("b_ada", 2 * 96), ("g_mix", 32), ("g_ffn", 32), ("g_final", 8), ("b_f", 4), ("g_q", 6),
                  ("g_kv", 2), ("w_dw", 2 * 3 * 44), ("b_dw", 2 * 44)):
    C2[_name] = _at
    _at += _n
SMALL2 = _at


def shape_constants_2():
    n_freq = RH // 4
    inv = (np.float32(10000.0) ** (-np.arange(n_freq, dtype=np.float32) / np.float32(n_freq))).astype(np.float32)
    t = np.arange(T)
    rows, cols = (t // 64).astype(np.float32), (t % 64).astype(np.float32)
    ang = np.concatenate([rows[:, None] * inv, cols[:, None] * inv], axis=1).astype(np.float32)
    cos, sin = np.cos(ang.astype(np.float64)).T, np.sin(ang.astype(np.float64)).T
    table = np.zeros((P, T))
    table[64:96] = np.concatenate([cos, cos])
    table[96:128] = np.concatenate([-sin, sin])
    table = table.astype(np.float32)
    ropes = np.stack([table * np.float32(SM), table], axis=1)

    def dft(n, reps=1):
        a = 2.0 * np.pi * ((np.arange(n)[:, None] * np.arange(n)[None, :]) % n) / n
        return np.cos(a), np.sin(a)
    c64, s64 = dft(64)
    two = lambda a: np.kron(np.eye(2), a)
    chan = np.concatenate([two(c64), two(s64)], axis=1).astype(np.float32)
    pos = []
    for n in (T, TC):
        c, s_ = dft(n)
        scale = 1.0 / np.sqrt(n * 64.0)
        both = np.stack([c * scale, -s_ * scale], axis=1)
        pos.append(both.reshape(n // P, P, 2, n).transpose(1, 0, 2, 3).reshape(P, -1).astype(np.float32))
    return {"c_ropes": ropes.reshape(P, 2 * T), "c_dft": np.concatenate([chan, *pos], axis=1)}


class Names:
    pass


def place(nc, at, name, shape, dt=F32):
    return nc.alloc_sbuf_tensor_at(name, shape, dt, offset=at), (at + 4 * int(np.prod(shape[1:])) + 31) // 32 * 32


def slab_of(c, l=0, per_layer=0, i=0, step=0):
    return l * per_layer + c + i * step, c % 2, l * (per_layer // 2) + c // 2 + i * (step // 2)


def two_stacks(nc, io, out):
    m, s = Names(), Names()
    with ExitStack() as ctx:
        at = 16512
        m.hT, at = place(nc, at, "hT", [P, KT, T])
        m.wst, at = place(nc, at, "wst", [P, 2, SLAB])
        m.whi, at = place(nc, at, "whi", [P, 2, SLAB], F32R)
        m.wlo, at = place(nc, at, "wlo", [P, 2, SLAB], F32R)
        m.xh, at = place(nc, at, "xh", [P, KT, T], F32R)
        m.xl, at = place(nc, at, "xl", [P, KT, T], F32R)
        m.cst, at = place(nc, at, "cst", [P, 258])
        m.sm1, at = place(nc, at, "sm1", [P, 74])
        m.nsink, at = place(nc, at, "nsink", [P, 2 * C_HEADS])
        m.cs, at = place(nc, at, "cs", [P, KT, 2])
        m.mods, at = place(nc, at, "mods", [P, DEPTH, 6 * KT * 2])
        region = at
        m.cosT, at = place(nc, region, "cosT", [P, T])
        m.sinT, at = place(nc, at, "sinT", [P, T])
        m.masks, at = place(nc, at, "masks", [P, MASKS])
        a_area = at
        m.AQ, at = place(nc, at, "AQ", [P, 3, T])
        m.AK, at = place(nc, at, "AK", [P, T])
        m.IQ, at = place(nc, at, "IQ", [P, 4, T])
        m.IK, at = place(nc, at, "IK", [P, T])
        m.VA, at = place(nc, at, "VA", [P, QB, HD])
        m.IW, at = place(nc, at, "IW", [P, QB, IDX_HEADS])
        m.CQ, at = place(nc, at, "CQ", [P, 4, T])
        m.CK, at = place(nc, at, "CK", [P, T])
        m.VC, at = place(nc, at, "VC", [P, QB, 2 * HD])
        ma_area = at
        m.MA, at = place(nc, at, "MA", [P, 1152])
        m.ikraw, _ = place(nc, ma_area, "ikraw", [P, T])
        m.iknorm, _ = place(nc, ma_area + 2048, "iknorm", [P, T])
        m.OB, _ = place(nc, ma_area, "OB", [P, QB, 4 * HD])
        m.OC, _ = place(nc, a_area, "OC", [P, QB, 8 * HD])
        m.OA, _ = place(nc, a_area + 8192, "OA", [P, QB, 6 * HD])
        m.mh, _ = place(nc, a_area, "mh", [P, KT, T], F32R)
        m.ml, _ = place(nc, a_area + 16384, "ml", [P, KT, T], F32R)
        b_area = at
        assert a_area + 32768 <= b_area
        m.BQK, at = place(nc, at, "BQK", [P, 12, T])
        m.VB, at = place(nc, at, "VB", [P, QB, 12 * HD])
        m.oh, _ = place(nc, b_area, "oh", [P, 9, T], F32R)
        m.ol, _ = place(nc, b_area + 18432, "ol", [P, 9, T], F32R)
        m.uh, _ = place(nc, b_area, "uh", [P, KT, T], F32R)
        m.ul, _ = place(nc, b_area + 16384, "ul", [P, KT, T], F32R)
        work = at
        m.S, at = place(nc, at, "S", [P, 2, 1296])
        m.PT, at = place(nc, at, "PT", [P, 2, 1280])
        m.qs, at = place(nc, at, "qs", [P, 2, 3, P])
        m.den, at = place(nc, at, "den", [P, 2, 12])
        m.rden, at = place(nc, at, "rden", [P, 12])
        m.nmax, at = place(nc, at, "nmax", [P, 2])
        m.top8, at = place(nc, at, "top8", [P, 8])
        assert at <= 229344, at
        m.xs, _ = place(nc, work, "xs", [P, 2, T])
        m.xc, _ = place(nc, work + 4096, "xc", [P, T])
        m.R, _ = place(nc, work, "R", [P, 2, T])
        m.rows, _ = place(nc, work + 4096, "rows", [P, 2, 256])
        m.sg, _ = place(nc, work, "sg", [P, 6, T])
        m.mt, _ = place(nc, work + 12288, "mt", [P, 2, T])
        m.mtmp, _ = place(nc, work + 16384, "mtmp", [P, T])
        m.ur, _ = place(nc, work, "ur", [P, 2, T])
        m.us, _ = place(nc, work + 4096, "us", [P, 2, T])
        m.of, _ = place(nc, work + 8192, "of", [P, 2, T])
        m.sq, _ = place(nc, work + 10368, "sq", [P, 2, T])
        m.vT, _ = place(nc, work + 10368, "vT", [P, 2, T])
        m.xn, _ = place(nc, work + 14464, "xn", [P, 2, T])
        m.rstd, _ = place(nc, work + 18560, "rstd", [P, T])
        m.posi, _ = place(nc, work, "posi", [P, T], I32)
        m.ang, _ = place(nc, work + 2048, "ang", [P, T])
        m.turns, _ = place(nc, work + 4096, "turns", [P, T])
        m.red, _ = place(nc, work + 6144, "red", [P, T])
        m.cT, at = place(nc, region, "cT", [P, KT, TC])
        m.xch, at = place(nc, at, "xch", [P, KT, TC], F32R)
        m.xcl, at = place(nc, at, "xcl", [P, KT, TC], F32R)
        m.sm2, at = place(nc, at, "sm2", [P, SMALL2])
        m.mod, at = place(nc, at, "mod", [P, 6, KT, 2])
        m.G, at = place(nc, at, "G", [P, 2, KT, 2])
        m.ropes, at = place(nc, at, "ropes", [P, 2, T])
        base2 = at
        m.fT, at = place(nc, at, "fT", [P, 2, TA])
        o_area = at
        m.O2, at = place(nc, at, "O2", [P, 6, KH * VH])
        m.cqr, _ = place(nc, o_area, "cqr", [P, 3, TA])
        m.ckvr, _ = place(nc, o_area + 9216, "ckvr", [P, TA])
        m.krr, _ = place(nc, o_area + 12288, "krr", [P, 2, TA])
        m.f2h, _ = place(nc, o_area, "f2h", [P, 2, TA], F32R)
        m.f2l, _ = place(nc, o_area + 6144, "f2l", [P, 2, TA], F32R)
        c_area = at
        m.cqh, at = place(nc, at, "cqh", [P, 3, TA], F32R)
        m.cql, at = place(nc, at, "cql", [P, 3, TA], F32R)
        m.ckvh, at = place(nc, at, "ckvh", [P, TA], F32R)
        m.ckvl, at = place(nc, at, "ckvl", [P, TA], F32R)
        m.dft, _ = place(nc, c_area, "dft", [P, 2 * P + QB * 2 * T + 2 * 2 * TC])
        w2_area = at
        m.P2, at = place(nc, at, "P2", [P, 2, TA])
        m.PT2, at = place(nc, at, "PT2", [P, 2, TA])
        m.qs2, at = place(nc, at, "qs2", [P, 2, P])
        m.rt, at = place(nc, at, "rt", [P, 2, T])
        m.den2, at = place(nc, at, "den2", [P, 2, HG])
        m.rden2, at = place(nc, at, "rden2", [P, HG])
        m.nmax2, at = place(nc, at, "nmax2", [P, 2])
        assert at <= 229344, at
        m.AB, _ = place(nc, w2_area, "AB", [P, QB, 2, 2 * P])
        m.f2, _ = place(nc, w2_area + 8192, "f2", [P, 2, T])
        x_area = 16512 + 4 * (KT * T + 6 * SLAB)
        m.Q4, _ = place(nc, x_area, "Q4", [P, HG, TA])
        m.K4, _ = place(nc, x_area + 12288, "K4", [P, HG, TA])
        m.V4, _ = place(nc, x_area + 24576, "V4", [P, 6, HG * VH])
        m.gh, at = place(nc, base2, "gh", [P, KT, TA], F32R)
        m.gl, at = place(nc, at, "gl", [P, KT, TA], F32R)
        m.cg, at = place(nc, at, "cg", [P, T])
        m.cv, at = place(nc, at, "cv", [P, T])
        m.sgl, at = place(nc, at, "sgl", [P, T])
        m.gu, at = place(nc, at, "gu", [P, T])
        m.ot2, at = place(nc, at, "ot2", [P, 2, T])
        assert at <= 229344, at
        n_area = w2_area
        m.sq2, _ = place(nc, n_area, "sq2", [P, 2, T])
        m.sum2, _ = place(nc, n_area + 12288, "sum2", [P, TA])
        m.xn2, _ = place(nc, n_area + 4096, "xn2", [P, 2, T])
        m.rstd2, _ = place(nc, n_area + 8192, "rstd2", [P, T])

        psum = ctx.enter_context(nc.psum_tensor("psum", [P, 8 * 512], F32))
        ps = [psum[:, 512 * b:512 * (b + 1)] for b in range(8)]

        ident, ones = m.cst[:, 0:P], m.cst[:, P:2 * P]
        inv, sign = m.cst[:, 256:257], m.cst[:, 257:258]

        def sem(name):
            return ctx.enter_context(nc.semaphore(name))

        s.consts_in, s.pos_in = sem("consts_in"), sem("pos_in")
        s.h_in, s.out_done = sem("h_in"), sem("out_done")
        s.hi_ready, s.lo_ready = sem("hi_ready"), sem("lo_ready")
        s.acc_ready = sem("acc_ready")
        s.acc_free = sem("acc_free")
        s.gate_free = sem("gate_free")
        s.swap_ready, s.rope_done = sem("swap_ready"), sem("rope_done")
        s.sq_ready, s.sq_used = sem("sq_ready"), sem("sq_used")
        s.var_ready, s.std_ready = sem("var_ready"), sem("std_ready")
        s.xn_ready, s.xh_ready = sem("xn_ready"), sem("xh_ready")
        s.x_ready = sem("x_ready")
        s.ik_sq, s.ik_stat = sem("ik_sq"), sem("ik_stat")
        s.ik_var, s.ik_std = sem("ik_var"), sem("ik_std")
        s.ik_norm = sem("ik_norm")
        s.q_staged = sem("q_staged")
        s.s_done, s.s_free = sem("s_done"), sem("s_free")
        s.max_ready, s.exp_ready = sem("max_ready"), sem("exp_ready")
        s.t_done, s.t_copied = sem("t_done"), sem("t_copied")
        s.pv_done = sem("pv_done")
        s.o_ready = sem("o_ready")
        s.ot_done, s.of_ready = sem("ot_done"), sem("of_ready")
        s.oh_ready, s.ol_ready = sem("oh_ready"), sem("ol_ready")
        s.mt_ready, s.mh_ready, s.m_ready = sem("mt_ready"), sem("mh_ready"), sem("m_ready")
        s.relu_ready, s.us_ready = sem("relu_ready"), sem("us_ready")
        s.uh_ready = sem("uh_ready")
        s.angles, s.tables = sem("angles"), sem("tables")
        s.ada_turned, s.row_copied = sem("ada_turned"), sem("row_copied")
        s.cs_ready, s.ada_used = sem("cs_ready"), sem("ada_used")
        s.vt_ready = sem("vt_ready")
        s.part_free = sem("part_free")
        s.masks_in = sem("masks_in")
        s.r_ready, s.r_used = sem("r_ready"), sem("r_used")
        s.h_squared = sem("h_squared")
        s.sm2_in, s.ctx_in = sem("sm2_in"), sem("ctx_in")
        s.dft_in = sem("dft_in")
        s.t2_tail = sem("t2_tail")
        s.mod_ready = sem("mod_ready")
        s.kr_ready, s.q4_part = sem("kr_ready"), sem("q4_part")
        s.q2_staged, s.s2_done = sem("q2_staged"), sem("s2_done")
        s.max2_ready, s.exp2_ready = sem("max2_ready"), sem("exp2_ready")
        s.t2_done = sem("t2_done")
        s.t2_copied, s.pv2_done = sem("t2_copied"), sem("pv2_done")
        s.o2_ready = sem("o2_ready")
        s.ot2_done, s.ot2_copied = sem("ot2_done"), sem("ot2_copied")
        s.oth_ready, s.mixed = sem("oth_ready"), sem("mixed")
        s.ab_done, s.ab_copied = sem("ab_done"), sem("ab_copied")
        s.f2_done, s.f2_copied = sem("f2_done"), sem("f2_copied")
        s.f2h_ready = sem("f2h_ready")
        s.f2_split = sem("f2_split")
        s.mid_ready, s.silu_ready = sem("mid_ready"), sem("silu_ready")
        s.gu_ready, s.gh_ready = sem("gu_ready"), sem("gh_ready")
        s.gl_ready = sem("gl_ready")
        s.final_ready = sem("final_ready")
        s.loaded = [ctx.enter_context(nc.semaphore(f"loaded{i}")) for i in range(2)]
        s.held = ctx.enter_context(nc.semaphore("held"))
        block = ctx.enter_context(nc.Block())

        def hold(engine, sem, value):
            engine.wait_ge(sem, value)
            engine.sem_inc(s.held, 1)

        @block.sync
        def _(sp):
            sp.dma_start(m.posi[:, :], io["pos"]).then_inc(s.pos_in, 16)
            sp.dma_start(m.cst[:, :], io["c_ident"]).then_inc(s.consts_in, 16)
            sp.dma_start(m.sm1[:, :], io["small_1"]).then_inc(s.consts_in, 16)
            for slot in range(2):
                sp.dma_start(m.wst[:, slot, :], io["weights"][slot]).then_inc(s.loaded[slot], 16)
            sp.dma_start(m.hT[:, :, :], io["x_t"]).then_inc(s.h_in, 16)
            sp.dma_start(m.masks[:, :], io["c_masks"]).then_inc(s.masks_in, 16)
            with sp.Fori(1, SLABS_ALL // 2) as i:
                for slot in range(2):
                    sp.wait_ge(s.hi_ready, 2 * i + slot + 1)
                    sp.wait_ge(s.lo_ready, 2 * i + slot + 1)
                    sp.dma_start(m.wst[:, slot, :],
                                 io["weights"][bass.ds(2 * i + slot, 1)].rearrange("a p n -> p (a n)")
                                 ).then_inc(s.loaded[slot], 16)
            sp.wait_ge(s.final_ready, 1)
            sp.dma_start(out, m.hT[:, :, :]).then_inc(s.out_done, 16)
            sp.wait_ge(s.out_done, 16)

        @block.gpsimd
        def _(pool):
            def stage(item, parity, g, tile_ap, row0, qb):
                if g == 0:
                    pool.wait_ge(s.s_done, item + 1)
                return nc.gpsimd.tensor_copy(
                    m.qs[row0:row0 + HD, parity, g, :],
                    tile_ap[row0:row0 + HD, qb * P:(qb + 1) * P])

            def pick(buf, i):
                return buf[:, bass.ds(i, 1), :].rearrange("p a n -> p (a n)")

            nc.gpsimd.memset(m.qs[:, :, :, :], 0.0)
            pool.drain()
            with pool.Fori(0, DEPTH) as l:
                item0 = l * ITEMS1
                hold(pool, s.rope_done, l * ROPES1 + ROPES1 + 2)
                for qb in range(1, QB):
                    with pool.Fori(0, IDX_HEADS // 2) as i:
                        for par in range(2):
                            item = item0 + IT_IDX + (qb - 1) * IDX_HEADS + 2 * i + par
                            stage(item, par, 0, pick(m.IQ, i), par * HD, qb).then_inc(s.q_staged, 1)
                for qb in range(QB):
                    with pool.Fori(0, A_HEADS // 2) as i:
                        for par in range(2):
                            item = item0 + IT_A + qb * A_HEADS + 2 * i + par
                            stage(item, par, 0, pick(m.AQ, i), par * HD, qb).then_inc(s.q_staged, 1)
                for qb in range(QB):
                    with pool.Fori(0, B_HPG // 2) as i:
                        for par in range(2):
                            item = item0 + IT_B + qb * B_HPG + 2 * i + par
                            for g in range(3):
                                last = stage(item, par, g, pick(m.BQK, 2 * g + i), par * HD, qb)
                            last.then_inc(s.q_staged, 1)
                for qb in range(QB):
                    with pool.Fori(0, C_HEADS // 2) as i:
                        for par in range(2):
                            item = item0 + IT_C + qb * C_HEADS + 2 * i + par
                            stage(item, par, 0, pick(m.CQ, i), par * HD, qb).then_inc(s.q_staged, 1)
            for l in range(DEPTH):
                with pool.Fori(0, 3) as hg:
                    hold(pool, s.acc_free, tiles2(l)["hg"] - FREE_OFF + (24 if l == 0 else 20) * (hg + 1) + 4)
                    for n, (qb, j, side) in enumerate(items2(l)):
                        item = item_base2(l) + len(items2(l)) * hg + n
                        hold(pool, s.s2_done, item + 1)
                        c = side * T + qb * P
                        nc.gpsimd.tensor_copy(m.qs2[0:QH, n % 2, :], m.Q4[0:QH, j, c:c + P]).then_inc(s.q2_staged, 1)

        @block.tensor
        def _(pe):
            def slab_split(slab):
                pe.wait_ge(s.hi_ready, slab + 3)
                pe.wait_ge(s.lo_ready, slab + 3)

            def columns_tile(bank, slot, kts, col, rh, rl, k0=0, late=()):
                for n, k in enumerate(kts):
                    for k_late, sem_, value in late:
                        if k == k_late:
                            pe.wait_ge(sem_, value)
                    w_hi = m.whi[:, slot, k * 256 + col:k * 256 + col + P]
                    w_lo = m.wlo[:, slot, k * 256 + col:k * 256 + col + P]
                    pe.matmul(ps[bank][:, :], w_hi, rh[:, k + k0, :], start=n == 0, stop=False)
                    pe.matmul(ps[bank][:, :], w_hi, rl[:, k + k0, :], start=False, stop=False)
                    last = pe.matmul(ps[bank][:, :], w_lo, rh[:, k + k0, :], start=False,
                                     stop=n == len(kts) - 1)
                return last

            def tokens_tile(bank, slot, block_, col, n):
                for k in range(KT):
                    x_hi = m.xh[:, k, block_ * P:(block_ + 1) * P]
                    x_lo = m.xl[:, k, block_ * P:(block_ + 1) * P]
                    w_hi = m.whi[:, slot, k * 256 + col:k * 256 + col + n]
                    w_lo = m.wlo[:, slot, k * 256 + col:k * 256 + col + n]
                    pe.matmul(ps[bank][:, 0:n], x_hi, w_hi, start=k == 0, stop=False)
                    pe.matmul(ps[bank][:, 0:n], x_hi, w_lo, start=False, stop=False)
                    last = pe.matmul(ps[bank][:, 0:n], x_lo, w_hi, start=False, stop=k == KT - 1)
                return last

            def norm_sums(norm):
                hold(pe, s.sq_ready, (norm + 1) * KT)
                pe.matmul(ps[4][:, :], ones, m.sq[:, 1, :], start=True, stop=True).then_inc(s.sq_used, KT)

            class Group:

                def __init__(self, branch, qb, l):
                    first_item, first_soft, heads = ((IT_A, SX_A, A_HEADS), (IT_B, SX_B, B_HPG),
                                                     (IT_C, SX_C, C_HEADS))[branch]
                    self.branch, self.qb, self.l, self.pairs = branch, qb, l, heads // 2
                    self.free0 = l * (ITEMS1 - IT_A) + first_item - IT_A + qb * heads
                    self.item0, self.soft0 = l * ITEMS1 + first_item + qb * heads, l * SOFTS1 + first_soft + qb * heads

                def logits(self, i, par):
                    item = self.item0 + 2 * i + par
                    opens = isinstance(i, int) and i == par == self.qb == 0
                    pe.wait_ge(s.q_staged, item + 1)
                    pe.wait_ge(s.s_free, self.free0 + 2 * i + par + (2 if opens else 1))
                    for bank, _, n, g, keys in self.segs(par, i):
                        if self.branch == 1:
                            pe.wait_ge(s.part_free, 3 * (self.l * QB * B_HPG + self.qb * B_HPG + 2 * i + par) + g + 1)
                        last = pe.matmul(ps[bank][:, 0:n], m.qs[:, par, g, :], keys, start=True, stop=True)
                    last.then_inc(s.s_done, 1)

                def turn(self, i, par):
                    n = self.soft0 + 2 * i + par
                    bank = 3 if self.branch == 1 else 3 + par
                    strict = self.branch == 1 or (isinstance(i, int) and i == par == self.qb == 0)
                    pe.wait_ge(s.exp_ready, n + 1)
                    pe.wait_ge(s.t_copied, n + (2 if strict else 1))
                    blocks = [c0 + P * b for _, c0, w, _, _ in self.segs(par, i) for b in range(w // P)]
                    for b, c in enumerate(blocks):
                        last = pe.transpose(ps[bank + b // 4][:, (b % 4) * P:(b % 4 + 1) * P],
                                            m.S[:, par, c:c + P], ident)
                    last.then_inc(s.t_done, 1)

                def weighted(self, i, par):
                    n, group = self.soft0 + 2 * i + par, self.branch * QB + self.qb
                    if isinstance(i, int) and i == par == 0:
                        pe.wait_ge(s.o_ready, self.l * GROUPS1 + group + 1)
                    pe.wait_ge(s.t_copied, n + 3)
                    vs = self.values(par, i)
                    for b, v in enumerate(vs):
                        last = pe.matmul(ps[6 + group % 2][:, bass.ds(self.out(par, i), HD)],
                                         m.PT[:, par, b * P:(b + 1) * P], v, start=b == 0, stop=b == len(vs) - 1)
                    last.then_inc(s.pv_done, 1)

                def segs(self, par, i):
                    n = (self.qb + 1) * P
                    k0, near = max(self.qb - 1, 0) * P, min(self.qb + 1, 2) * P
                    if self.branch == 0:
                        return [(par, 0, n, 0, m.AK[:, 0:n])]
                    if self.branch == 2:
                        return [(par, 0, near, 0, m.CK[:, k0:k0 + near])]
                    return [(0, 0, near, 0, m.BQK[:, bass.ds(6 + i, 1), k0:k0 + near].rearrange("p a n -> p (a n)")),
                            (1, near, n, 1, kslice(m.BQK, 8 + i, n)), (2, near + n, n, 2, kslice(m.BQK, 10 + i, n))]

                def values(self, par, i):
                    k0, near = max(self.qb - 1, 0), min(self.qb + 1, 2)
                    if self.branch == 0:
                        return [m.VA[:, b, :] for b in range(self.qb + 1)]
                    if self.branch == 2:
                        return [m.VC[:, k0 + b, par * HD:(par + 1) * HD] for b in range(near)]
                    head = lambda g: (g * B_HPG + 2 * i + par) * HD
                    return ([vslice(m.VB, k0 + b, head(0)) for b in range(near)]
                            + [vslice(m.VB, b, head(g)) for g in (1, 2) for b in range(self.qb + 1)])

                def out(self, par, i):
                    return (4 * par + i if self.branch == 2 else 2 * i + par) * HD

            def kslice(buf, i, n):
                return buf[:, bass.ds(i, 1), 0:n].rearrange("p a n -> p (a n)")

            def vslice(buf, blk, c):
                return buf[:, blk, bass.ds(c, HD)]

            pe.wait_ge(s.consts_in, 32)
            pe.sem_inc(s.sq_used, 2)
            pe.sem_inc(s.s_done, 2)
            pe.sem_inc(s.t_done, 2)
            pe.sem_inc(s.pv_done, 2)
            with pe.Fori(0, DEPTH) as l:
                slab0, tile0, free0 = l * SLABS1, l * TILES1, l * FREES1

                def done(mm):
                    mm.then_inc(s.acc_ready, 1)

                def bank_free(v):
                    pe.wait_ge(s.acc_free, free0 + v + 1)

                norm_sums(l * NORMS1)
                v = FR_A
                for sl in range(5):
                    slab_split(slab0 + SL_A + sl)
                    for t in range(1 if sl == 4 else 2):
                        bank_free(v)
                        late = [(k, s.x_ready, l * NORMS1 * KT + k + 1) for k in range(KT)] if v == FR_A else ()
                        done(columns_tile(v % 4, (SL_A + sl) % 2, range(KT), t * P, m.xh, m.xl, late=late))
                        v += 1
                bank_free(v)
                hold(pe, s.vt_ready, 2 * l + 1)
                for j in range(2):
                    for b in range(QB):
                        c = (QB * j + b) * HD
                        last = pe.transpose(ps[v % 4][:, c:c + HD], m.vT[HD:P, j, b * P:(b + 1) * P],
                                            m.cst[HD:P, HD:P])
                last.then_inc(s.acc_ready, 8)
                with pe.Fori(0, 3) as i:
                    for sl in range(2):
                        slab_split(slab0 + SL_B + 2 * i + sl)
                        for t in range(2):
                            bank_free(FR_B + 4 * i + 2 * sl + t)
                            done(columns_tile((FR_B + 2 * sl + t) % 4, (SL_B + sl) % 2, range(KT), t * P,
                                              m.xh, m.xl))
                hold(pe, s.ik_sq, l + 1)
                pe.matmul(ps[4][0:HD, :], m.cst[0:HD, P:P + HD], m.iknorm[0:HD, :], start=True, stop=True
                          ).then_inc(s.ik_stat, 1)
                for sl in range(3):
                    slab_split(slab0 + SL_BV + sl)
                    for b in range(QB):
                        v = FR_BV + 4 * sl + b
                        bank_free(v)
                        done(tokens_tile(v % 4, (SL_BV + sl) % 2, b, 0, 256))
                for sl in range(2):
                    slab_split(slab0 + SL_C + sl)
                    for t in range(2):
                        v = FR_C + 2 * sl + t
                        bank_free(v)
                        done(columns_tile(v % 4, (SL_C + sl) % 2, range(KT), t * P, m.xh, m.xl))
                slab_split(slab0 + SL_C + 2)
                v = FR_C + 4
                bank_free(v)
                done(columns_tile(v % 4, (SL_C + 2) % 2, range(KT), 0, m.xh, m.xl))
                slab_split(slab0 + SL_C + 3)
                v = FR_C + 5
                bank_free(v)
                done(columns_tile(v % 4, (SL_C + 3) % 2, range(KT), 0, m.xh, m.xl))
                v += 1
                bank_free(v)
                pe.wait_ge(s.vt_ready, 2 * l + 2)
                for b in range(QB):
                    last = pe.transpose(ps[v % 4][:, b * P:(b + 1) * P], m.vT[:, 0, b * P:(b + 1) * P], ident)
                last.then_inc(s.acc_ready, 3)
                pe.wait_ge(s.rope_done, l * ROPES1 + ROPES1 + 2)
                hold(pe, s.acc_free, free0 + FR_C + 9 + 4)
                for qb in range(1, QB):
                    with pe.Fori(0, IDX_HEADS // 2) as i:
                        for par in range(2):
                            item = l * ITEMS1 + IT_IDX + (qb - 1) * IDX_HEADS + 2 * i + par
                            pe.wait_ge(s.q_staged, item + 1)
                            pe.wait_ge(s.r_ready, l * IT_A + IT_IDX + (qb - 1) * IDX_HEADS + 2 * i + par + 1)
                            n = (qb + 1) * P
                            pe.matmul(ps[par][:, 0:n], m.qs[:, par, 0, :], m.IK[:, 0:n], start=True, stop=True
                                      ).then_inc(s.s_done, 1)
                def rows_of(i, slot):
                    pe.wait_ge(s.loaded[slot], 16 * ((l * SLABS1 + SL_ADA) // 2 + i + 1))
                    for k in range(KT):
                        last = pe.matmul(ps[5 + slot][0:2, 0:256], m.cs[:, k, :], m.wst[:, slot, k * 256:(k + 1) * 256],
                                         start=k == 0, stop=k == KT - 1)
                    last.then_inc(s.ada_used, 1)

                def columns_of(i, slot):
                    pe.wait_ge(s.row_copied, l * ADA_SLABS + 2 * i + slot + 1)
                    for t in range(2):
                        last = pe.matmul(ps[7][:, bass.ds(8 * i + 4 * slot + 2 * t, 2)],
                                         m.rows[0:2, slot, t * P:(t + 1) * P], m.cst[0:2, 0:2], start=True, stop=True)
                    last.then_inc(s.ada_turned, 1)

                pe.wait_ge(s.cs_ready, 1)
                hold(pe, s.gate_free, l * 24 + 4)
                rows_of(0, 0)
                with pe.Fori(0, ADA_SLABS // 2 - 1) as i:
                    rows_of(i, 1)
                    columns_of(i, 0)
                    rows_of(i + 1, 0)
                    columns_of(i, 1)
                rows_of(ADA_SLABS // 2 - 1, 1)
                columns_of(ADA_SLABS // 2 - 1, 0)
                columns_of(ADA_SLABS // 2 - 1, 1)
                groups = [Group(branch, qb, l) for branch in range(3) for qb in range(QB)]
                pe.wait_ge(s.r_ready, (l + 1) * IT_A + 2)
                groups[0].logits(0, 0)
                for n, g in enumerate(groups):
                    def item(i, par, g=g, before=groups[n - 1], after=(groups + [None])[n + 1], n=n):
                        if par == 0:
                            g.logits(i, 1)
                        elif not isinstance(i, int) or i + 1 < g.pairs:
                            g.logits(i + 1, 0)
                        elif after is not None:
                            after.logits(0, 0)
                        g.turn(i, par)
                        if par:
                            g.weighted(i, 0)
                        elif not isinstance(i, int) or i:
                            g.weighted(i - 1, 1)
                        elif n:
                            before.weighted(before.pairs - 1, 1)

                    for par in range(2):
                        item(0, par)
                    if g.pairs > 2:
                        with pe.Fori(1, g.pairs - 1) as i:
                            for par in range(2):
                                item(i, par)
                    for par in range(2):
                        item(g.pairs - 1, par)
                groups[-1].weighted(groups[-1].pairs - 1, 1)
                pe.wait_ge(s.o_ready, (l + 1) * GROUPS1 + 2)
                for j in range(9):
                    src, c = (m.OA, j) if j < 3 else (m.OB, j - 3) if j < 5 else (m.OC, j - 5)
                    pe.wait_ge(s.of_ready, l * 9 + j + 1)
                    for b in range(QB):
                        last = pe.transpose(ps[4 + j % 2][:, b * P:(b + 1) * P], src[:, b, c * P:(c + 1) * P], ident)
                    last.then_inc(s.ot_done, 1)
                hold(pe, s.of_ready, (l + 1) * 9 + 2)
                with pe.Fori(0, 2) as jp:
                    for half in range(2):
                        for g in range(3):
                            c = SL_MERGE + 5 * half + g
                            slab_split(slab0 + c + 10 * jp)
                            for t in range(2):
                                u = 6 * half + 2 * g + t
                                pe.wait_ge(s.gate_free, l * 24 + 12 * jp + u + 1)
                                done(columns_tile(4 + u % 4, c % 2, range(KT), t * P, m.xh, m.xl))
                        c = SL_MERGE + 5 * half + 3
                        pe.wait_ge(s.ol_ready, (l + 1) * 9)
                        slab_split(slab0 + c + 10 * jp)
                        for b, (kts, k0) in enumerate((((0, 1, 2), 0), ((3, 4), 0), ((0, 1, 2, 3), 5))):
                            if b == 2:
                                c += 1
                                slab_split(slab0 + c + 10 * jp)
                            for t in range(2):
                                v = FR_MERGE + 6 * half + 2 * b + t
                                bank_free(v + 12 * jp)
                                done(columns_tile(v % 4, c % 2, kts, t * P, m.oh, m.ol, k0))
                hold(pe, s.m_ready, (l + 1) * KT - 2)
                with pe.Fori(0, 2) as i:
                    for sl in range(2):
                        slab_split(slab0 + SL_WO + 2 * i + sl)
                        for t in range(2):
                            v = FR_WO + 2 * sl + t
                            bank_free(v + 4 * i)
                            done(columns_tile(v % 4, (SL_WO + sl) % 2, range(KT), t * P, m.mh, m.ml,
                                              late=[(KT - 2, s.m_ready, (l + 1) * KT)] if t == 0 else ()))
                norm_sums(l * NORMS1 + 1)
                with pe.Fori(0, 4) as q:
                    for down in range(2):
                        xa, xb = (m.uh, m.ul) if down else (m.xh, m.xl)
                        with pe.Fori(0, 2) as i:
                            for sl in range(2):
                                if down:
                                    pe.wait_ge(s.acc_free, free0 + FR_MLP + 16 * q + 7 + 4)
                                    late = [(KT - 1, s.acc_free, free0 + FR_MLP + 16 * q + 8 + 4)]
                                else:
                                    late = [(k, s.x_ready, (l * NORMS1 + 1) * KT + k + 2) for k in range(0, KT, 2)]
                                slab_split(slab0 + SL_MLP + 8 * q + 4 * down + 2 * i + sl)
                                for t in range(2):
                                    v = FR_MLP + 8 * down + 2 * sl + t
                                    bank_free(v + 16 * q + 4 * i)
                                    done(columns_tile(v % 4, (SL_MLP + sl) % 2, range(KT), t * P, xa, xb,
                                                      late=late if t == 0 else ()))
            norm_sums(DEPTH * NORMS1)
            def done2(mm, skip=0):
                mm.then_inc(s.acc_ready, 1 + skip)

            def bank2(tile, i=0):
                pe.wait_ge(s.acc_free, tile - FREE_OFF + 1 + i)
                return tile % 4

            def columns2(bank, slot, kts, col, step, rh, rl, n, k0=0, late=()):
                for a, k in enumerate(kts):
                    for k_late, sem_, value in late:
                        if k == k_late:
                            pe.wait_ge(sem_, value)
                    w_hi = m.whi[:, slot, k * step + col:k * step + col + P]
                    w_lo = m.wlo[:, slot, k * step + col:k * step + col + P]
                    h, t = rh(k + k0), rl(k + k0)
                    pe.matmul(ps[bank][:, 0:n], w_hi, h, start=a == 0, stop=False)
                    pe.matmul(ps[bank][:, 0:n], w_hi, t, start=False, stop=False)
                    last = pe.matmul(ps[bank][:, 0:n], w_lo, h, start=False, stop=a == len(kts) - 1)
                return last

            def sums2(name, kt, n):
                k0 = NORMS2[name][0]
                if summed(name):
                    c0 = T if name[-1] == "1" else 0
                    pe.wait_ge(s.sq_ready, k0 + kt)
                    pe.matmul(ps[4][:, 0:n], ones, m.sum2[:, c0:c0 + n], start=True, stop=True).then_inc(s.sq_used, kt)
                    return
                for k in range(kt):
                    pe.wait_ge(s.sq_ready, k0 + k + 1)
                    pe.matmul(ps[4][:, 0:n], ones, m.sq2[:, (k0 + k) % 2, 0:n], start=k == 0, stop=k == kt - 1
                              ).then_inc(s.sq_used, 1)

            def x_of(side):
                return ((lambda k: m.xch[:, k, :], lambda k: m.xcl[:, k, :]) if side else
                        (lambda k: m.xh[:, k, :], lambda k: m.xl[:, k, :]))

            pe.sem_inc(s.s2_done, 2)
            pe.sem_inc(s.t2_done, 2)
            pe.sem_inc(s.pv2_done, 2)
            for l in range(DEPTH):
                tl = tiles2(l)
                lat_con = pieces(l)

                def slabw(c, i=0, step=0):
                    number, slot, _ = slab2(l, c, i, step)
                    slab_split(number)
                    return slot

                for step in win_steps(l):
                    if step[0] == "slab":
                        slot = slabw(S2_WIN + step[1])
                    elif step[0] == "norm":
                        sums2(step[1], step[2], step[3])
                    elif step[0] == "tile":
                        _, t, c, side, n, _ = step
                        x0 = NORMS2[f"mix{l}{side}"][0] - X_OFF
                        first = c == 0 or (l > 0 and side == 1 and c == 3)
                        late = [(k, s.x_ready, x0 + k + 1) for k in range(KT)] if first else ()
                        b = bank2(t)
                        done2(columns2(b, slot, range(KT), (c % 2) * P, 256, *x_of(side), n, late=late))
                hold(pe, s.x_ready, NORMS2[f"kv{l}1"][0] + 1 - X_OFF)
                items = items2(l)
                with pe.Fori(0, 3) as hg:
                    per = 24 if l == 0 else 20
                    tile = tl["hg"]
                    slot = slabw(S2_HG, hg, 2)
                    for j in range(HG):
                        for side, n, c0 in lat_con:
                            b = bank2(tile, per * hg)
                            done2(columns2(b, slot, range(3), j * P, 512, lambda k: m.cqh[:, k, c0:c0 + n],
                                           lambda k: m.cql[:, k, c0:c0 + n], n))
                            tile += 1
                    slot = slabw(S2_HG + 1, hg, 2)
                    for j in range(HG):
                        for side, n, c0 in pieces(l, True):
                            b = bank2(tile, per * hg)
                            done2(columns2(b, slot, range(1), j * P, 512, lambda k: m.ckvh[:, c0:c0 + n],
                                           lambda k: m.ckvl[:, c0:c0 + n], n))
                            tile += 1
                    for blk in range(6):
                        b = bank2(tile, per * hg)
                        o = ps[b][:, 0:HG * VH]
                        wv = [w[:, slot, 0:512].rearrange("p (h d) -> p h d", h=HG)[:, :, VH:2 * VH]
                              for w in (m.whi, m.wlo)]
                        xa, xb = (x[:, blk * P:(blk + 1) * P] for x in (m.ckvh, m.ckvl))
                        pe.matmul(o, xa, wv[0], start=True, stop=False)
                        pe.matmul(o, xa, wv[1], start=False, stop=False)
                        last = pe.matmul(o, xb, wv[0], start=False, stop=True)
                        done2(last, 2 if blk == 5 else 0)
                        tile += 1
                    pe.wait_ge(s.acc_free, tl["hg"] - FREE_OFF + per * (hg + 1) + 4)

                    tails = QB * HG * (3 * l + hg)

                    def logits(n):
                        qb, j, side = items[n]
                        item = item_base2(l) + len(items) * hg + n
                        pe.wait_ge(s.q2_staged, item + 1)
                        pe.wait_ge(s.exp2_ready, item + 1)
                        for c, w in (((0, 512), (512, 256)) if side == 0 else ((0, 256),)):
                            last = pe.matmul(ps[2 * (n % 2) + c // 512][:, 0:w], m.qs2[0:QH, n % 2, :],
                                             m.K4[0:QH, j, side * T + c:side * T + c + w], start=True, stop=True)
                        last.then_inc(s.s2_done, 1)

                    def turn(n):
                        item = item_base2(l) + len(items) * hg + n
                        pe.wait_ge(s.exp2_ready, item + 3)
                        pe.wait_ge(s.t2_copied, item + 1)
                        if items[n][2] == 0:
                            pe.wait_ge(s.t2_tail, tails + n + 1)
                        for b in range(6 if items[n][2] == 0 else 2):
                            last = pe.transpose(ps[4 + b // 4][:, (b % 4) * P:(b % 4 + 1) * P],
                                                m.P2[:, n % 2, b * P:(b + 1) * P], ident)
                        last.then_inc(s.t2_done, 1)

                    def weighted(n):
                        qb, j, side = items[n]
                        item = item_base2(l) + len(items) * hg + n
                        pe.wait_ge(s.t2_copied, item + 2)
                        if side == 0:
                            pe.wait_ge(s.t2_tail, tails + n + 2)
                        if j == 0:
                            pe.wait_ge(s.o2_ready, group_base2(l) + len(items) // HG * hg + n // HG + 1)
                        blocks = range(6) if side == 0 else range(4, 6)
                        for b, blk in enumerate(blocks):
                            last = pe.matmul(ps[6 + n // HG % 2][:, j * VH:(j + 1) * VH],
                                             m.PT2[:, n % 2, b * P:(b + 1) * P], m.V4[:, blk, j * VH:(j + 1) * VH],
                                             start=b == 0, stop=b == len(blocks) - 1)
                        last.then_inc(s.pv2_done, 1)

                    logits(0)
                    for n in range(len(items)):
                        if n + 1 < len(items):
                            logits(n + 1)
                        turn(n)
                        if n:
                            weighted(n - 1)
                    weighted(len(items) - 1)
                hold(pe, s.o2_ready, group_base2(l) + 3 * len(items) // HG + 2)
                n = 12 * l
                for j in range(6):
                    for side, w, _ in lat_con:
                        pe.wait_ge(s.ot2_copied, n + 1)
                        for b in range(w // P):
                            last = pe.transpose(ps[6 + n % 2][:, b * P:(b + 1) * P],
                                                m.O2[:, 4 * side + b, j * P:(j + 1) * P], ident)
                        last.then_inc(s.ot2_done, 1)
                        n += 1
                pe.wait_ge(s.dft_in, 16 * (l + 1))
                pe.wait_ge(s.mixed, 12 if l == 0 else 22)
                n = 0 if l == 0 else 12
                for side, w, c0 in lat_con:
                    if side == 1:
                        pe.wait_ge(s.f2_copied, 2)
                    for b in range(w // P):
                        for c in range(2):
                            bank = 4 + n % 2
                            pe.wait_ge(s.ab_copied, n + 1)
                            pe.matmul(ps[bank][:, 0:2 * P], m.fT[:, c, c0 + b * P:c0 + (b + 1) * P], m.dft[:, 0:2 * P],
                                      start=True, stop=True).then_inc(s.ab_done, 1)
                            n += 1
                    pe.wait_ge(s.ab_copied, n + 2)
                    for c in range(2):
                        nb, off = w // P, 2 * P + side * QB * 2 * T
                        for b in range(nb):
                            for h in range(2):
                                at = off + (2 * b + h) * w
                                last = pe.matmul(ps[6 + c][:, 0:w], m.AB[:, b, c, h * P:(h + 1) * P], m.dft[:, at:at + w],
                                                 start=b == 0 and h == 0, stop=b == nb - 1 and h == 1)
                        last.then_inc(s.f2_done, 1)
                hold(pe, s.f2_split, 4 if l == 0 else 6)
                t = tl["four"]
                for c in range(2):
                    slot = slabw(S2_FOUR + c)
                    for side, n, c0 in lat_con:
                        b = bank2(t)
                        done2(columns2(b, slot, range(2), 0, 256, lambda k: m.f2h[:, k, c0:c0 + n],
                                       lambda k: m.f2l[:, k, c0:c0 + n], n))
                        t += 1
                pe.wait_ge(s.mixed, 16 if l == 0 else 24)
                t = tl["wout"]
                for sl in range(4):
                    slot = slabw(S2_WOUT + sl)
                    for h in range(2):
                        for side, n, _ in lat_con:
                            b = bank2(t)
                            done2(columns2(b, slot, range(KT), h * P, 256, *x_of(side), n))
                            t += 1
                sums2(f"ffn{l}0", KT, T)
                for c, (_, pairs, first) in enumerate(FFN_CHUNKS):
                    ns = len(lat_con)

                    def up(i):
                        for sl in range(2):
                            slot = slabw(first + sl, i, 2)
                            for side, n, _ in lat_con:
                                if side == 1 and c == 0 and sl == 0 and isinstance(i, int):
                                    sums2(f"ffn{l}1", KT, n)
                                for g in range(2):
                                    t = tl[f"up{c}"] + sl * 2 * ns + 2 * side + g
                                    b = bank2(t, 4 * ns * i)
                                    x0 = NORMS2[f"ffn{l}{side}"][0] - X_OFF
                                    late = [(k, s.x_ready, x0 + k + 2) for k in range(0, KT, 2)]
                                    done2(columns2(b, slot, range(KT), g * P, 256, *x_of(side), n,
                                                   late=late if g == 0 and sl == 0 and c == 0 and isinstance(i, int)
                                                   else ()))

                    up(0)
                    with pe.Fori(1, pairs // 2) as i:
                        up(i)
                    hold(pe, s.gl_ready, GL_BASE[l] + (8 * c + pairs - 1) * ns)
                    with pe.Fori(0, 2) as i:
                        for sl in range(2):
                            slot = slabw(first + pairs + sl, i, 2)
                            for g in range(2):
                                for side, n, c0 in lat_con:
                                    t = tl[f"down{c}"] + sl * 2 * ns + g * ns + side
                                    b = bank2(t, 4 * ns * i)
                                    done2(columns2(b, slot, range(pairs), g * P, 256,
                                                   lambda k: m.gh[:, k, c0:c0 + n], lambda k: m.gl[:, k, c0:c0 + n], n,
                                                   late=[(pairs - 1, s.gl_ready, GL_BASE[l] + (8 * c + pairs) * ns)]))
            sums2("final", KT, T)

        @block.scalar
        def _(act):
            def split(slab, slot, turn, tiles):
                act.wait_ge(s.loaded[slot], 16 * (turn + 1))
                if tiles is not None:
                    act.wait_ge(s.acc_ready, tiles)
                act.activation(m.whi[:, slot, :], m.wst[:, slot, :], ACT.Copy).then_inc(s.hi_ready, 1)

            def swap_halves(rope, tile_count, src, rows=P):
                if tile_count is not None:
                    act.wait_ge(s.acc_ready, tile_count)
                act.wait_ge(s.rope_done, rope[0] + 1)
                for a in range(0, rows, 64):
                    act.activation(m.xs[a:a + 32, rope[1], :], src[a + 32:a + 64, :], ACT.Copy)
                    last = act.activation(m.xs[a + 32:a + 64, rope[1], :], src[a:a + 32, :], ACT.Copy)
                last.then_inc(s.swap_ready, 1)

            def norm(n):
                act.wait_ge(s.var_ready, n + 1)
                act.activation(m.rstd[:, :], m.rstd[:, :], ACT.Sqrt).then_inc(s.std_ready, 1)

            def norm_heads(n):
                with act.Fori(0, KT // 2) as kk:
                    for par in range(2):
                        act.wait_ge(s.xn_ready, n * KT + 2 * kk + par + 1)
                        act.activation(m.xh[:, bass.ds(2 * kk + par, 1), :].rearrange("p a n -> p (a n)"),
                                       m.xn[:, par, :], ACT.Copy).then_inc(s.xh_ready, 1)

            def exponentials(group, i, par):
                branch, qb = group
                soft0, width, _ = soft_of(branch, qb)
                col = 4 * par + i if branch == 2 else 2 * i + par
                act.wait_ge(s.max_ready, group_l(soft0) + 2 * i + par + 1)
                act.activation(m.S[:, par, 0:width], m.S[:, par, 0:width], ACT.Exp, bias=m.nmax[:, par:par + 1],
                               scale=-1.0, accum_out=m.den[:, (branch * QB + qb) % 2, bass.ds(col, 1)]
                               ).then_inc(s.exp_ready, 1)

            def copies(group, i, par):
                branch, qb = group
                soft0, _, nb = soft_of(branch, qb)
                n = group_l(soft0) + 2 * i + par
                bank = 3 if branch == 1 else 3 + par
                act.wait_ge(s.t_done, n + 3)
                act.wait_ge(s.pv_done, n + 1)
                for b in range(0, nb, 4):
                    w = min(4, nb - b) * P
                    last = act.activation(m.PT[:, par, b * P:b * P + w], ps[bank + b // 4][:, 0:w], ACT.Copy)
                last.then_inc(s.t_copied, 1)

            def soft_of(branch, qb):
                n, near = (qb + 1) * P, P if qb == 0 else 2 * P
                if branch == 0:
                    return SX_A + qb * A_HEADS, n, n // P
                if branch == 1:
                    return SX_B + qb * B_HPG, near + 2 * n, (near + 2 * n) // P
                return SX_C + qb * C_HEADS, near + 1, near // P

            def mlp_slab(l, c, q, i):
                return l * SLABS1 + c + 8 * q + 2 * i, c % 2, l * (SLABS1 // 2) + c // 2 + 4 * q + i

            act.sem_inc(s.hi_ready, 2)
            act.sem_inc(s.gate_free, 4)
            act.sem_inc(s.of_ready, 2)
            act.sem_inc(s.t_copied, 2)
            act.sem_inc(s.r_ready, 2)
            act.sem_inc(s.t2_tail, 1)
            act.sem_inc(s.mh_ready, 1)
            for slot in range(2):
                split(slot, slot, 0, None)
            act.wait_ge(s.h_in, 16)
            for k in range(KT):
                act.activation(m.BQK[:, k, :], m.hT[:, k, :], ACT.Square).then_inc(s.h_squared, 1)
            act.wait_ge(s.consts_in, 32)
            act.activation(m.cs[:, :, :], m.sm1[:, 58:74].rearrange("p (k s) -> p k s", s=2), ACT.Silu
                           ).then_inc(s.cs_ready, 1)
            act.wait_ge(s.angles, 1)
            act.activation(m.cosT[:, :], m.red[:, :], ACT.Sin).then_inc(s.tables, 1)
            act.wait_ge(s.angles, 2)
            act.activation(m.sinT[:, :], m.ang[:, :], ACT.Sin).then_inc(s.tables, 1)
            with act.Fori(0, DEPTH) as l:
                tile0, rope0 = l * TILES1, l * ROPES1

                def next_split(c, tiles, i=0, step=0):
                    split(*slab_of(c + 2, l, SLABS1, i, step), tile0 + tiles)

                norm(l * NORMS1)
                norm_heads(l * NORMS1)
                r = RP_A
                for sl, tiles, count in ((0, (0, 1), 2), (1, (2, 3), 4), (2, (4, 5), 6), (3, (6, 7), 8), (4, (), 9)):
                    for t in tiles:
                        if t == 3:
                            act.wait_ge(s.acc_ready, tile0 + t + 1)
                            act.activation(m.vT[HD:P, 0, :], ps[(FR_A + t) % 4][HD:P, :], ACT.Copy)
                        swap_halves((rope0 + r, r % 2), tile0 + t + 1, ps[(FR_A + t) % 4])
                        r += 1
                    next_split(SL_A + sl, count)
                with act.Fori(0, 3) as i:
                    for sl in range(2):
                        for t in range(2):
                            j = 2 * sl + t
                            swap_halves((rope0 + RP_B + 4 * i + j, (RP_B + j) % 2), tile0 + TL_B + 4 * i + j + 1,
                                        ps[(FR_B + j) % 4])
                        next_split(SL_B + sl, TL_B + 2 * sl + 2 + 4 * i, i, 2)
                act.wait_ge(s.ik_var, l + 1)
                act.activation(m.rstd[0:HD, :], m.rstd[0:HD, :], ACT.Sqrt).then_inc(s.ik_std, 1)
                act.wait_ge(s.ik_norm, l + 1)
                swap_halves((rope0 + RP_IK, RP_IK % 2), None, m.iknorm, HD)
                for sl in range(3):
                    next_split(SL_BV + sl, TL_BV + 4 * sl + 4)
                for t in range(4):
                    r = RP_C + t
                    swap_halves((rope0 + r, r % 2), tile0 + TL_C + t + 1, ps[(FR_C + t) % 4])
                    if t % 2:
                        next_split(SL_C + t // 2, TL_C + t + 1)
                swap_halves((rope0 + RP_C + 4, (RP_C + 4) % 2), tile0 + TL_C + 5, ps[(FR_C + 4) % 4])
                for qb in range(1, QB):
                    with act.Fori(0, IDX_HEADS // 2) as i:
                        for par in range(2):
                            item = IT_IDX + (qb - 1) * IDX_HEADS + 2 * i + par
                            act.wait_ge(s.r_used, l * IT_A + item + 1)
                            act.wait_ge(s.s_done, l * ITEMS1 + item + 3)
                            n = (qb + 1) * P
                            act.activation(m.R[:, par, 0:n], ps[par][:, 0:n], ACT.Relu, scale=float(HD ** -0.5)
                                           ).then_inc(s.r_ready, 1)
                with act.Fori(0, ADA_SLABS // 2) as i:
                    for slot in range(2):
                        act.wait_ge(s.ada_used, l * ADA_SLABS + 2 * i + slot + 1)
                        act.sem_inc(s.hi_ready, 1)
                        act.sem_inc(s.lo_ready, 1)
                        act.activation(m.rows[0:2, slot, :], ps[5 + slot][0:2, 0:256], ACT.Copy
                                       ).then_inc(s.row_copied, 1)
                for sl in range(2):
                    split(*slab_of(SL_MERGE + sl, l, SLABS1), tile0 + TL_C + 9)
                group_l = lambda soft: l * SOFTS1 + soft
                groups = [(branch, qb) for branch in range(3) for qb in range(QB)]
                pairs_of = lambda group: (A_HEADS, B_HPG, C_HEADS)[group[0]] // 2
                for n, g in enumerate(groups):
                    act.wait_ge(s.o_ready, l * GROUPS1 + n + 1)
                    exponentials(g, 0, 0)
                    if n:
                        copies(groups[n - 1], pairs_of(groups[n - 1]) - 1, 1)
                    exponentials(g, 0, 1)
                    copies(g, 0, 0)
                    with act.Fori(1, pairs_of(g)) as i:
                        exponentials(g, i, 0)
                        copies(g, i - 1, 1)
                        exponentials(g, i, 1)
                        copies(g, i, 0)
                copies(groups[-1], pairs_of(groups[-1]) - 1, 1)
                for j in range(9):
                    act.wait_ge(s.ot_done, l * 9 + j + 1)
                    act.wait_ge(s.ol_ready, l * 9 + j - 1) if j >= 2 else None
                    act.activation(m.of[:, j % 2, :], ps[4 + j % 2][:, :], ACT.Copy).then_inc(s.of_ready, 1)
                    act.drain()
                    act.activation(m.oh[:, j, :], m.of[:, j % 2, :], ACT.Copy).then_inc(s.oh_ready, 1)
                with act.Fori(0, 2) as jp:
                    for half in range(2):
                        t0 = TL_MERGE + 12 * half
                        for g in range(3):
                            for t in range(2):
                                u = 6 * half + 2 * g + t
                                act.wait_ge(s.acc_ready, tile0 + t0 + 2 * g + t + 1 + 24 * jp)
                                if g == 0 and t == 0:
                                    act.wait_ge(s.mt_ready, l * 8 + 4 * jp + 2 * half + 1)
                                if g == 2 and t == 0 and half == 0:
                                    act.wait_ge(s.ol_ready, (l + 1) * 9)
                                act.activation(m.sg[:, 2 * g + t, :], ps[4 + u % 4][:, :], ACT.Sigmoid
                                               ).then_inc(s.gate_free, 1)
                            next_split(SL_MERGE + 5 * half + g, t0 + 2 * g + 2 + 24 * jp, jp, 10)
                        next_split(SL_MERGE + 5 * half + 3, t0 + 10 + 24 * jp, jp, 10)
                        next_split(SL_MERGE + 5 * half + 4, t0 + 12 + 24 * jp, jp, 10)
                        for t in range(2):
                            act.wait_ge(s.mt_ready, l * 8 + 4 * jp + 2 * half + t + 2)
                            act.activation(m.mh[:, bass.ds(4 * jp + 2 * half + t, 1), :].rearrange("p a n -> p (a n)"),
                                           m.mt[:, t, :], ACT.Copy).then_inc(s.mh_ready, 1)
                with act.Fori(0, 2) as i:
                    for sl in range(2):
                        next_split(SL_WO + sl, TL_WO + 2 * sl + 2 + 4 * i, i, 2)
                norm(l * NORMS1 + 1)
                norm_heads(l * NORMS1 + 1)
                with act.Fori(0, 4) as q:
                    with act.Fori(0, 2) as i:
                        for sl in range(2):
                            for t in range(2):
                                n = l * 32 + 8 * q + 4 * i + 2 * sl + t
                                act.wait_ge(s.acc_ready, tile0 + TL_MLP + 16 * q + 4 * i + 2 * sl + t + 1)
                                act.wait_ge(s.us_ready, n + 1)
                                act.activation(m.ur[:, t, :], ps[(FR_MLP + 2 * sl + t) % 4][:, :], ACT.Relu
                                               ).then_inc(s.relu_ready, 1)
                                act.wait_ge(s.us_ready, n + 3)
                                act.activation(m.uh[:, bass.ds(4 * i + 2 * sl + t, 1), :].rearrange("p a n -> p (a n)"),
                                               m.us[:, t, :], ACT.Copy).then_inc(s.uh_ready, 1)
                            split(*mlp_slab(l, SL_MLP + sl + 2, q, i), tile0 + TL_MLP + 2 * sl + 2 + 16 * q + 4 * i)
                    with act.Fori(0, 2) as i:
                        for sl in range(2):
                            c = SL_MLP + 4 + sl + 2
                            tiles = tile0 + TL_MLP + 8 + 2 * sl + 2 + 16 * q + 4 * i
                            split(*mlp_slab(l, c, q, i), tiles)
            norm(DEPTH * NORMS1)
            def norm2(name):
                n0, n = NORMS2[name][1], T if name[-1] == "0" or name == "final" else TC
                act.wait_ge(s.var_ready, n0 + 1)
                act.activation(m.rstd2[:, 0:n], m.rstd2[:, 0:n], ACT.Sqrt).then_inc(s.std_ready, 1)

            def heads2(name, kt, n, dst, shift=None):
                k0 = NORMS2[name][0]
                for k in range(kt):
                    act.wait_ge(s.xn_ready, k0 + k + 1 - X_OFF)
                    src = m.xn2[:, (k0 + k) % 2, 0:n]
                    if shift is None:
                        ins = act.activation(dst(k), src, ACT.Copy)
                    else:
                        ins = act.activation(dst(k), src, ACT.Identity, bias=shift(k))
                    ins.then_inc(s.xh_ready, 1)

            def x_dst(side):
                return (lambda k: m.xch[:, k, :]) if side else (lambda k: m.xh[:, k, :])

            act.wait_ge(s.sq_ready, (DEPTH * NORMS1 + 1) * KT)
            act.dma_start(m.sm2[:, :], io["small_2"]).then_inc(s.sm2_in, 16)
            act.dma_start(m.cT[:, :, :], io["ctx_t"]).then_inc(s.ctx_in, 16)
            act.dma_start(m.ropes[:, :, :].rearrange("p a n -> p (a n)"), io["c_ropes"]).then_inc(s.ctx_in, 16)
            act.wait_ge(s.sm2_in, 16)
            act.sem_inc(s.exp2_ready, 2)
            act.sem_inc(s.ot2_copied, 2)
            act.sem_inc(s.ab_copied, 2)
            for l in range(DEPTH):
                tl = tiles2(l)
                lat_con = pieces(l)
                ns = len(lat_con)

                def next2(c, tiles, i=0, step=0):
                    if l == DEPTH - 1 and isinstance(i, int) and c + 2 >= SLABS2:
                        return
                    split(*slab2(l, c + 2, i, step), tiles)

                act.wait_ge(s.mod_ready, l + 1)
                t = tl["win"]
                for step in win_steps(l):
                    if step[0] == "tile":
                        t = step[1] + 1
                    elif step[0] == "split":
                        next2(S2_WIN + step[1], t)
                    elif step[0] == "norm":
                        _, name, kt, n, c0 = step
                        side = int(name[-1])
                        norm2(name)
                        if kt == KT:
                            heads2(name, kt, n, x_dst(side), lambda k: m.mod[:, 0, k, side:side + 1])
                        elif kt == 3:
                            heads2(name, kt, n, lambda k: m.cqh[:, k, c0:c0 + n])
                        else:
                            heads2(name, kt, n, lambda k: m.ckvh[:, c0:c0 + n])
                act.wait_ge(s.kr_ready, l + 1)
                for j in range(HG):
                    act.activation(m.K4[64:96, j, :], m.krr[64:96, 0, :], ACT.Copy)
                items = items2(l)
                per = 24 if l == 0 else 20
                with act.Fori(0, 3) as hg:
                    tile = tl["hg"] + per * hg
                    for j in range(HG):
                        act.wait_ge(s.acc_ready, tile + j * ns + 1)
                        act.activation(m.Q4[0:64, j, 0:T], ps[(tl["hg"] + j * ns) % 4][0:64, :], ACT.Copy, scale=SM
                                       ).then_inc(s.q4_part, 1)
                    next2(S2_HG, tile + HG * ns, hg, 2)
                    next2(S2_HG + 1, tile + per, hg, 2)
                    def tail_copied(n):
                        item = item_base2(l) + len(items) * hg + n
                        if items[n][2] == 0:
                            act.wait_ge(s.pv2_done, item + 1)
                            act.wait_ge(s.t2_done, item + 3)
                            act.activation(m.PT2[:, n % 2, 512:TA], ps[5][:, 0:256], ACT.Copy
                                           ).then_inc(s.t2_tail, 1)

                    for n, (qb, j, side) in enumerate(items):
                        item = item_base2(l) + len(items) * hg + n
                        w = TA if side == 0 else TC
                        if j == 0:
                            act.wait_ge(s.o2_ready, group_base2(l) + len(items) // HG * hg + n // HG + 1)
                        act.wait_ge(s.t2_done, item + 1)
                        act.wait_ge(s.max2_ready, item + 1)
                        act.activation(m.P2[:, n % 2, 0:w], psum[:, 1024 * (n % 2):1024 * (n % 2) + w], ACT.Exp,
                                       bias=m.nmax2[:, n % 2:n % 2 + 1],
                                       accum_out=m.den2[:, n // HG % 2, j:j + 1]).then_inc(s.exp2_ready, 1)
                        if n:
                            tail_copied(n - 1)
                    tail_copied(len(items) - 1)
                act.wait_ge(s.o2_ready, group_base2(l) + 3 * len(items) // HG + 2)
                act.dma_start(m.dft[:, :], io["c_dft"]).then_inc(s.dft_in, 16)
                n = 12 * l
                for j in range(6):
                    for side, w, _ in lat_con:
                        act.wait_ge(s.ot2_done, n + 1)
                        if n - 12 * l >= 2:
                            act.wait_ge(s.mixed, n - 1 + 4 * l)
                        act.activation(m.ot2[:, n % 2, 0:w], ps[6 + n % 2][:, 0:w], ACT.Copy).then_inc(s.ot2_copied, 1)
                        act.drain()
                        act.activation(x_dst(side)(2 + j), m.ot2[:, n % 2, 0:w], ACT.Copy).then_inc(s.oth_ready, 1)
                        n += 1
                n, f = (0, 0) if l == 0 else (12, 4)
                for side, w, c0 in lat_con:
                    for b in range(w // P):
                        for c in range(2):
                            act.wait_ge(s.ab_done, n + 1)
                            act.activation(m.AB[:, b, c, :], ps[4 + n % 2][:, 0:2 * P], ACT.Copy
                                           ).then_inc(s.ab_copied, 1)
                            n += 1
                    for c in range(2):
                        act.wait_ge(s.f2_done, f + 1)
                        if side:
                            act.wait_ge(s.f2_split, f - 1)
                        act.activation(m.f2[:, c, 0:w], ps[6 + c][:, 0:w], ACT.Copy).then_inc(s.f2_copied, 1)
                        act.drain()
                        act.activation(m.f2h[:, c, c0:c0 + w], m.f2[:, c, 0:w], ACT.Copy).then_inc(s.f2h_ready, 1)
                        f += 1
                t = tl["four"]
                for c in range(2):
                    for side, n, _ in lat_con:
                        act.wait_ge(s.acc_ready, t + 1)
                        bf = m.sm2[:, C2["b_f"] + 2 * l + c:C2["b_f"] + 2 * l + c + 1]
                        act.activation(x_dst(side)(c), ps[t % 4][:, 0:n], ACT.Identity, bias=bf
                                       ).then_inc(s.oth_ready, 1)
                        t += 1
                    next2(S2_FOUR + c, t)
                for sl in range(4):
                    next2(S2_WOUT + sl, tl["wout"] + (sl + 1) * 2 * ns)
                for side, n, _ in lat_con:
                    norm2(f"ffn{l}{side}")
                    heads2(f"ffn{l}{side}", KT, n, x_dst(side), lambda k, side=side: m.mod[:, 3, k, side:side + 1])
                for c, (pair0, pairs, first) in enumerate(FFN_CHUNKS):
                    with act.Fori(0, pairs // 2) as i:
                        for sl in range(2):
                            for side, n, c0 in lat_con:
                                u = 2 * i + sl
                                for g, buf in ((0, m.cg), (1, m.cv)):
                                    col = 44 * 3 * l + 44 + 22 * g + pair0 + u
                                    bcol = 44 * l + 22 * g + pair0 + u
                                    t = tl[f"up{c}"] + sl * 2 * ns + 2 * side + g
                                    act.wait_ge(s.acc_ready, t + 1 + 4 * ns * i)
                                    hold(act, s.gu_ready, GL_BASE[l] + (8 * c + u) * ns + side + 1)
                                    act.activation(buf[:, 0:n], ps[t % 4][:, 0:n], ACT.Identity,
                                                   bias=m.sm2[:, bass.ds(C2["b_dw"] + bcol, 1)],
                                                   scale=m.sm2[:, bass.ds(C2["w_dw"] + col, 1)]
                                                   ).then_inc(s.mid_ready, 1)
                                if side == ns - 1:
                                    next2(first + sl, tl[f"up{c}"] + (sl + 1) * 2 * ns + 4 * ns * i, i, 2)
                                at = GL_BASE[l] + (8 * c + u) * ns + side
                                t = tl[f"up{c}"] + sl * 2 * ns + 2 * side
                                act.wait_ge(s.acc_free, t + 5 - FREE_OFF + 4 * ns * i)
                                act.activation(m.sgl[:, 0:n], m.cg[:, 0:n], ACT.Silu).then_inc(s.silu_ready, 1)
                                hold(act, s.gu_ready, at + 2)
                                act.activation(m.gh[:, bass.ds(u, 1), c0:c0 + n].rearrange("p a n -> p (a n)"),
                                               m.gu[:, 0:n], ACT.Copy).then_inc(s.gh_ready, 1)
                    down = first + pairs
                    for sl in range(4):
                        next2(down + sl, tl[f"down{c}"] + (sl + 1) * 2 * ns)
            norm2("final")

        @block.vector
        def _(dve):
            STT, TT, TS = nc.vector.scalar_tensor_tensor, nc.vector.tensor_tensor, nc.vector.tensor_scalar

            def split(slab, slot):
                dve.wait_ge(s.hi_ready, slab + 3)
                TT(m.wlo[:, slot, :], m.wst[:, slot, :], m.whi[:, slot, :].bitcast(F32), ALU.subtract
                   ).then_inc(s.lo_ready, 1)

            def rotate(rope, src, dests, rows=P, frees=None):
                dve.drain()
                dve.wait_ge(s.swap_ready, rope[0] + 1)
                xs = m.xs[0:rows, rope[1], :]
                ins = TT(m.xc[0:rows, :], src[0:rows, :], m.cosT[0:rows, :], ALU.mult)
                if frees:
                    ins.then_inc(s.acc_free, frees)
                TT(xs, xs, m.sinT[0:rows, :], ALU.mult)
                dve.drain()
                for r0, r1, dst in dests:
                    ins = TT(dst, m.xc[r0:r1, :], m.xs[r0:r1, rope[1], :], ALU.add)
                ins.then_inc(s.rope_done, 1)

            def col(buf, i):
                return buf[:, bass.ds(i, 1), :].rearrange("p a n -> p (a n)")

            def squares(h):
                dve.drain()
                TT(m.sq[:, 0, :], h, h, ALU.mult)
                dve.drain()
                TT(m.sq[:, 1, :], m.sq[:, 1, :], m.sq[:, 0, :], ALU.add)

            def norm(n, gain, split_it, split_between=None):
                dve.sem_inc(s.sq_ready, KT)
                if split_between is not None:
                    split(*split_between)
                dve.wait_ge(s.sq_used, (n + 1) * KT + 2)
                TS(m.rstd[:, :], ps[4][:, :], 1.0 / D, EPS, ALU.mult, ALU.add).then_inc(s.var_ready, 1)
                dve.wait_ge(s.std_ready, n + 1)
                nc.vector.reciprocal(m.rstd[:, :], m.rstd[:, :])
                dve.drain()
                def normed(k, dst):
                    return STT(dst, m.hT[:, k, :], m.sm1[:, bass.ds(gain + k, 1)], m.rstd[:, :], ALU.mult, ALU.mult)

                for k in range(KT):
                    if not split_it:
                        ins = normed(k, m.hT[:, k, :])
                        continue
                    if k == 0:
                        normed(0, m.xn[:, 0, :]).then_inc(s.xn_ready, 1)
                    if k + 1 < KT:
                        if k:
                            hold(dve, s.x_ready, n * KT + k)
                        normed(k + 1, m.xn[:, (k + 1) % 2, :]).then_inc(s.xn_ready, 1)
                    dve.wait_ge(s.xh_ready, n * KT + k + 1)
                    ins = TT(m.xl[:, k, :], m.xn[:, k % 2, :], m.xh[:, k, :].bitcast(F32), ALU.subtract)
                    ins.then_inc(s.x_ready, 1)
                if not split_it:
                    dve.drain()
                return ins

            def attention(item0, soft0, pairs, segs, width, parts, normalize_before, sink=None):
                def item(i, par):
                    n = soft0 + 2 * i + par
                    dve.wait_ge(s.t_done, n + 1)
                    least = -TAKEN
                    nmax = m.nmax[:, par:par + 1]
                    hold(dve, s.s_done, item0 + 2 * i + par + 3)
                    if sink is not None:
                        least = m.S[:, par, width - 1:width]
                        nc.vector.tensor_copy(least, sink(par, i))
                        dve.drain()
                    for bank, c0, w, mask in segs(par):
                        ins = nc.vector.tensor_tensor_reduce(
                            m.S[:, par, c0:c0 + w], ps[bank][:, 0:w], mask, -(HD ** -0.5), least, ALU.add, ALU.min,
                            nmax)
                        least = nmax
                        if parts:
                            ins.then_inc(s.part_free, 1)
                            dve.drain()
                    if parts:
                        dve.sem_inc(s.max_ready, 1)
                    else:
                        ins.then_inc(s.max_ready, 1)
                        dve.drain()
                    dve.sem_inc(s.s_free, 1)

                for par in range(2):
                    item(0, par)
                normalize_before()
                with dve.Fori(1, pairs) as i:
                    for par in range(2):
                        item(i, par)

            def normalize(group, soft_end, heads, dst):
                dve.wait_ge(s.pv_done, soft_end + 2)
                nc.vector.reciprocal(m.rden[:, 0:heads], m.den[:, group % 2, 0:heads])
                dve.drain()
                TT(dst.rearrange("p (h d) -> p h d", d=HD),
                   ps[6 + group % 2][:, 0:heads * HD].rearrange("p (h d) -> p h d", d=HD),
                   m.rden[:, 0:heads].unsqueeze(2).broadcast_to([P, heads, HD]), ALU.mult).then_inc(s.o_ready, 1)
                dve.drain()

            dve.sem_inc(s.lo_ready, 2)
            dve.sem_inc(s.acc_free, 4)
            dve.sem_inc(s.rope_done, 2)
            dve.sem_inc(s.us_ready, 2)
            dve.sem_inc(s.o_ready, 2)
            dve.sem_inc(s.s_free, 2)
            dve.sem_inc(s.part_free, 3)
            dve.sem_inc(s.r_used, 2)
            dve.sem_inc(s.mt_ready, 1)
            dve.sem_inc(s.t2_copied, 1)
            dve.sem_inc(s.gu_ready, 1)
            dve.wait_ge(s.pos_in, 16)
            dve.wait_ge(s.consts_in, 32)
            c1 = 6.28125
            c2 = float(np.float32(np.round((TWO_PI - c1) * 2 ** 19) / 2 ** 19))
            c3 = float(np.float32(TWO_PI - c1 - c2))
            nc.vector.tensor_copy(m.ang[:, :], m.posi[:, :])
            dve.drain()
            TS(m.ang[:, :], m.ang[:, :], inv, None, ALU.mult)
            for which, dst in ((0, m.red), (1, m.ang)):
                dve.drain()
                TS(m.turns[:, :], m.ang[:, :], 1.0 / TWO_PI, 0.25 if which == 0 else 0.0, ALU.mult, ALU.add)
                dve.drain()
                TS(m.turns[:, :], m.turns[:, :], ROUND, -ROUND, ALU.add, ALU.add)
                dve.drain()
                STT(dst[:, :], m.turns[:, :], -c1, m.ang[:, :], ALU.mult, ALU.add)
                dve.drain()
                STT(dst[:, :], m.turns[:, :], -c2, dst[:, :], ALU.mult, ALU.add)
                dve.drain()
                STT(dst[:, :], m.turns[:, :], -c3, dst[:, :], ALU.mult, ALU.add)
                dve.drain()
                if which == 0:
                    TS(dst[:, :], dst[:, :], float(np.pi / 2), None, ALU.add)
                    dve.drain()
                TS(dst[:, :], dst[:, :], 3.1415925, -3.1415925, ALU.min, ALU.max).then_inc(s.angles, 1)
            TS(m.nsink[:, :], m.sm1[:, 42:58], -1.0, None, ALU.mult)
            split(0, 0)
            split(1, 1)
            dve.wait_ge(s.h_squared, KT)
            half = KT // 2
            while half > 1:
                TT(m.BQK[:, 0:half, :], m.BQK[:, 0:half, :], m.BQK[:, half:2 * half, :], ALU.add)
                dve.drain()
                half //= 2
            TT(m.sq[:, 1, :], m.BQK[:, 0, :], m.BQK[:, 1, :], ALU.add)
            dve.wait_ge(s.tables, 2)
            TS(m.sinT[:, :], m.sinT[:, :], sign, None, ALU.mult)
            dve.wait_ge(s.h_in, 16)
            dve.drain()
            with dve.Fori(0, DEPTH) as l:
                slab0, tile0, rope0 = l * SLABS1, l * TILES1, l * ROPES1
                norm(l * NORMS1, l * 8, True)

                def next_split(c, i=0, step=0):
                    split(slab0 + c + 2 + i * step, c % 2)

                def whole(ap):
                    return [(0, P, ap)]

                r = RP_A
                for sl in range(5):
                    if sl < 4:
                        for t in range(2):
                            tile = r
                            src = ps[(FR_A + tile) % 4]
                            if tile < 3:
                                dst = whole(m.AQ[:, tile, :])
                            elif tile == 3:
                                dst = [(0, HD, m.AK[0:HD, :]), (0, HD, m.AK[HD:P, :])]
                            else:
                                dst = whole(m.IQ[:, tile - 4, :])
                            rotate((rope0 + r, r % 2), src, dst, frees=1)
                            r += 1
                    if sl == 4:
                        dve.wait_ge(s.acc_ready, tile0 + 9)
                        nc.vector.tensor_copy(m.vT[HD:P, 1, :], ps[(FR_A + 8) % 4][HD:P, :]).then_inc(s.vt_ready, 1)
                        nc.vector.tensor_copy(m.ikraw[0:HD, :], ps[(FR_A + 8) % 4][0:HD, :]).then_inc(s.acc_free, 1)
                        dve.drain()
                        TT(m.iknorm[0:HD, :], m.ikraw[0:HD, :], m.ikraw[0:HD, :], ALU.mult).then_inc(s.ik_sq, 1)
                        dve.wait_ge(s.acc_ready, tile0 + 17)
                        turned = ps[(FR_A + 9) % 4][:, :].rearrange("p (j b d) -> p j b d", j=2, b=QB)
                        nc.vector.tensor_copy(m.VA[:, :, :], turned[:, 0, :, :])
                        TS(m.IW[:, :, :], turned[:, 1, :, 0:IDX_HEADS], float(np.float32(IDX_HEADS ** -0.5)), None,
                           ALU.mult).then_inc(s.acc_free, 8)
                    next_split(SL_A + sl)
                with dve.Fori(0, 3) as i:
                    for sl in range(2):
                        for t in range(2):
                            j = 2 * sl + t
                            rotate((rope0 + RP_B + 4 * i + j, (RP_B + j) % 2), ps[(FR_B + j) % 4],
                                   whole(col(m.BQK, 4 * i + j)), frees=1)
                        next_split(SL_B + sl, i, 2)
                dve.wait_ge(s.ik_stat, l + 1)
                TS(m.rstd[0:HD, :], ps[4][0:HD, :], 1.0 / HD, EPS, ALU.mult, ALU.add).then_inc(s.ik_var, 1)
                dve.wait_ge(s.ik_std, l + 1)
                nc.vector.reciprocal(m.rstd[0:HD, :], m.rstd[0:HD, :])
                dve.drain()
                STT(m.iknorm[0:HD, :], m.ikraw[0:HD, :], m.sm1[0:HD, bass.ds(40 + l, 1)], m.rstd[0:HD, :],
                    ALU.mult, ALU.mult).then_inc(s.ik_norm, 1)
                rotate((rope0 + RP_IK, RP_IK % 2), m.iknorm, [(0, HD, m.IK[0:HD, :]), (0, HD, m.IK[HD:P, :])], HD)
                for sl in range(3):
                    for b in range(QB):
                        t = 4 * sl + b
                        dve.wait_ge(s.acc_ready, tile0 + TL_BV + t + 1)
                        nc.vector.tensor_copy(m.VB[:, b, sl * 256:(sl + 1) * 256], ps[(FR_BV + t) % 4][:, 0:256]
                                              ).then_inc(s.acc_free, 1)
                    next_split(SL_BV + sl)
                for t in range(4):
                    r = RP_C + t
                    rotate((rope0 + r, r % 2), ps[(FR_C + t) % 4], whole(m.CQ[:, t, :]), frees=1)
                    if t % 2:
                        next_split(SL_C + t // 2)
                rotate((rope0 + RP_C + 4, (RP_C + 4) % 2), ps[(FR_C + 4) % 4], whole(m.CK[:, :]), frees=1)
                dve.wait_ge(s.acc_ready, tile0 + TL_C + 6)
                nc.vector.tensor_copy(m.vT[:, 0, :], ps[(FR_C + 5) % 4][:, :]).then_inc(s.vt_ready, 1)
                dve.wait_ge(s.vt_ready, 2 * l + 2)
                dve.sem_inc(s.acc_free, 1)
                dve.wait_ge(s.acc_ready, tile0 + TL_C + 9)
                nc.vector.tensor_copy(m.VC[:, :, :].rearrange("p b n -> p (b n)"), ps[(FR_C + 6) % 4][:, :]
                                      ).then_inc(s.acc_free, 3)
                offs = {1: 0, 2: 256, 3: 640}
                dve.wait_ge(s.masks_in, 16)
                for qb in range(1, QB):
                    n = (qb + 1) * P
                    acc = m.MA[:, offs[qb]:offs[qb] + n]
                    nc.vector.tensor_copy(acc, m.masks[:, M_CAUSAL + 512 - n:M_CAUSAL + 512])
                    with dve.Fori(0, IDX_HEADS // 2) as i:
                        for par in range(2):
                            dve.drain()
                            dve.wait_ge(s.r_ready, l * IT_A + IT_IDX + (qb - 1) * IDX_HEADS + 2 * i + par + 3)
                            STT(acc, m.R[:, par, 0:n], m.IW[:, qb, bass.ds(2 * i + par, 1)], acc,
                                ALU.mult, ALU.add).then_inc(s.r_used, 1)
                for qb in range(1, QB):
                    n = (qb + 1) * P
                    acc = m.MA[:, offs[qb]:offs[qb] + n]
                    dve.drain()
                    with dve.Fori(0, TOPK // 8) as _i:
                        nc.vector.max(m.top8[:, :], acc)
                        dve.drain()
                        nc.vector.match_replace(acc, m.top8[:, :], acc, TAKEN)
                        dve.drain()
                    TS(acc, acc, 0.5 * TAKEN, NEG, ALU.is_gt, ALU.mult)
                hold(dve, s.ada_turned, (l + 1) * ADA_SLABS)
                nc.vector.tensor_copy(m.mods[:, bass.ds(l, 1), :].rearrange("p a n -> p (a n)"),
                                      ps[7][:, 0:6 * KT * 2])
                for sl in range(2):
                    split(slab0 + SL_MERGE + sl, sl)
                last_group = None
                for branch in range(3):
                    for qb in range(QB):
                        n = (qb + 1) * P
                        near = P if qb == 0 else 2 * P
                        mk = lambda base, size, w: m.masks[:, base + size - w:base + size]
                        it0, sx0, heads, dst = ((IT_A, SX_A, A_HEADS, m.OA), (IT_B, SX_B, B_HPG, m.OB),
                                                (IT_C, SX_C, C_HEADS, m.OC))[branch]
                        sink, width = None, n
                        if branch == 0:
                            mask = mk(M_CAUSAL, 512, n) if qb == 0 else m.MA[:, offs[qb]:offs[qb] + n]
                            segs = lambda par: [(par, 0, n, mask)]
                        elif branch == 1:
                            width = near + 2 * n
                            segs = lambda par: [(0, 0, near, mk(M_B0, 256, near)), (1, near, n, mk(M_B1, 512, n)),
                                                (2, near + n, n, mk(M_B2, 512, n))]
                        else:
                            width = near + 1
                            segs = lambda par: [(par, 0, near, mk(M_C, 256, near))]
                            sink = lambda par, i: m.nsink[:, bass.ds(l * 8 + 4 * par + i, 1)]
                        before = (lambda args=last_group: normalize(*args)) if last_group else (lambda: None)
                        soft0 = l * SOFTS1 + sx0 + qb * heads
                        attention(l * ITEMS1 + it0 + qb * heads, soft0, heads // 2, segs, width, branch == 1, before,
                                  sink)
                        last_group = (branch * QB + qb, soft0 + heads, heads, dst[:, qb, :])
                normalize(*last_group)
                for j in range(9):
                    dve.wait_ge(s.oh_ready, l * 9 + j + 1)
                    TT(m.ol[:, j, :], m.of[:, j % 2, :], m.oh[:, j, :].bitcast(F32), ALU.subtract
                       ).then_inc(s.ol_ready, 1)
                with dve.Fori(0, 2) as jp:
                    for half in range(2):
                        for g in range(3):
                            next_split(SL_MERGE + 5 * half + g, jp, 10)
                        for b in range(3):
                            for t in range(2):
                                v = FR_MERGE + 6 * half + 2 * b + t
                                dve.drain()
                                dve.wait_ge(s.acc_ready, tile0 + TL_MERGE + 12 * half + 6 + 2 * b + t + 1 + 24 * jp)
                                if b == 0 and t == 0:
                                    dve.wait_ge(s.gate_free, l * 24 + 12 * jp + 6 * half + 6 + 4)
                                if b == 0:
                                    dve.wait_ge(s.mh_ready, l * 8 + 4 * jp + 2 * half + 1)
                                    TT(m.mt[:, t, :], ps[v % 4][:, :], m.sg[:, t, :], ALU.mult).then_inc(s.acc_free, 1)
                                    continue
                                TT(m.mtmp[:, :], ps[v % 4][:, :], m.sg[:, 2 * b + t, :], ALU.mult
                                   ).then_inc(s.acc_free, 1)
                                dve.drain()
                                ins = TT(m.mt[:, t, :], m.mt[:, t, :], m.mtmp[:, :], ALU.add)
                                if b == 2:
                                    ins.then_inc(s.mt_ready, 1)
                            if b == 1:
                                next_split(SL_MERGE + 5 * half + 3, jp, 10)
                        next_split(SL_MERGE + 5 * half + 4, jp, 10)
                        for t in range(2):
                            k = 4 * jp + 2 * half + t
                            dve.wait_ge(s.mh_ready, l * 8 + k + 2)
                            TT(col(m.ml, k), m.mt[:, t, :], col(m.mh, k).bitcast(F32), ALU.subtract
                               ).then_inc(s.m_ready, 1)
                dve.drain()
                nc.vector.memset(m.sq[:, 1, :], 0.0)
                for sl in range(4):
                    for t in range(2):
                        j = 2 * sl + t
                        dve.wait_ge(s.acc_ready, tile0 + TL_WO + j + 1)
                        TT(m.hT[:, j, :], m.hT[:, j, :], ps[(FR_WO + j) % 4][:, :], ALU.add).then_inc(s.acc_free, 1)
                        squares(m.hT[:, j, :])
                    if sl < 3:
                        next_split(SL_WO + sl)
                dve.drain()
                norm(l * NORMS1 + 1, 16 + l * 8, True, (slab0 + SL_WO + 3 + 2, (SL_WO + 3) % 2))
                with dve.Fori(0, 4) as q:
                    with dve.Fori(0, 2) as i:
                        for sl in range(2):
                            for t in range(2):
                                n = l * 32 + 8 * q + 4 * i + 2 * sl + t
                                dve.wait_ge(s.relu_ready, n + 1)
                                TT(m.us[:, t, :], m.ur[:, t, :], m.ur[:, t, :], ALU.mult).then_inc(s.us_ready, 1)
                                dve.wait_ge(s.uh_ready, n + 1)
                                k = 4 * i + 2 * sl + t
                                TT(col(m.ul, k), m.us[:, t, :], col(m.uh, k).bitcast(F32), ALU.subtract
                                   ).then_inc(s.acc_free, 1)
                            next_split(SL_MLP + sl, 8 * q + 2 * i, 1)
                    dve.drain()
                    nc.vector.memset(m.sq[:, 1, :], 0.0)
                    with dve.Fori(0, 2) as i:
                        for sl in range(2):
                            for t in range(2):
                                j = 2 * sl + t
                                dve.wait_ge(s.acc_ready, tile0 + TL_MLP + 8 + 16 * q + 4 * i + j + 1)
                                h = col(m.hT, 4 * i + j)
                                TT(h, h, ps[(FR_MLP + j) % 4][:, :], ALU.add).then_inc(s.acc_free, 1)
                                squares(h)
                            next_split(SL_MLP + 4 + sl, 8 * q + 2 * i, 1)
                dve.drain()
                dve.sem_inc(s.acc_free, 2)
            norm(DEPTH * NORMS1, 32, False)
            def norm2(name, kt, n, src, gain, shift=None, dst=None, width=D):
                k0, n0 = NORMS2[name]
                if summed(name):
                    dve.drain()
                    dve.sem_inc(s.sq_ready, kt)
                while later:
                    split(*later.pop())
                for k in range(0 if summed(name) else kt):
                    dve.wait_ge(s.sq_used, k0 + k + 1)
                    h = src(k)
                    TT(m.sq2[:, (k0 + k) % 2, 0:n], h, h, ALU.mult).then_inc(s.sq_ready, 1)
                dve.wait_ge(s.sq_used, k0 + kt + 2)
                TS(m.rstd2[:, 0:n], ps[4][:, 0:n], 1.0 / width, EPS, ALU.mult, ALU.add).then_inc(s.var_ready, 1)
                dve.wait_ge(s.std_ready, n0 + 1)
                nc.vector.reciprocal(m.rstd2[:, 0:n], m.rstd2[:, 0:n])
                dve.drain()
                def normed(k):
                    xn = m.xn2[:, (k0 + k) % 2, 0:n]
                    STT(xn, src(k), gain(k), m.rstd2[:, 0:n], ALU.mult, ALU.mult).then_inc(s.xn_ready, 1)

                for k in range(kt):
                    if dst is None:
                        last = STT(src(k), src(k), gain(k), m.rstd2[:, 0:n], ALU.mult, ALU.mult)
                        continue
                    if k == 0:
                        normed(0)
                    if k + 1 < kt:
                        if k:
                            dve.wait_ge(s.x_ready, k0 + k - X_OFF)
                        normed(k + 1)
                    head, tail = dst
                    xn = m.xn2[:, (k0 + k) % 2, 0:n]
                    dve.wait_ge(s.xh_ready, k0 + k + 1 - X_OFF)
                    if shift is None:
                        last = TT(tail(k), xn, head(k).bitcast(F32), ALU.subtract)
                    else:
                        last = STT(tail(k), xn, shift(k), head(k).bitcast(F32), ALU.add, ALU.subtract)
                    last.then_inc(s.x_ready, 1)
                return last

            def x_pair(side):
                a, b = (m.xch, m.xcl) if side else (m.xh, m.xl)
                return (lambda k: a[:, k, :]), (lambda k: b[:, k, :])

            dve.sem_inc(s.o2_ready, 2)
            dve.wait_ge(s.sm2_in, 16)
            later = []
            for l in range(DEPTH):
                tl = tiles2(l)
                lat_con = pieces(l)
                ns = len(lat_con)

                def next2(c, i=0, step=0):
                    if l == DEPTH - 1 and isinstance(i, int) and c + 2 >= SLABS2:
                        return
                    number, slot, _ = slab2(l, c + 2, i, step)
                    if c in (S2_FOUR + 5, SLABS2 - 1):
                        later.append((number, slot))
                    else:
                        split(number, slot)

                def ready(tile):
                    dve.wait_ge(s.acc_ready, tile + 1)

                mod = m.mod[:, :, :, :].rearrange("p a k s -> p (a k s)")
                TT(mod, m.mods[:, l, :], m.sm2[:, C2["b_ada"] + 96 * l:C2["b_ada"] + 96 * (l + 1)], ALU.add)
                dve.drain()
                for a, (part, name) in enumerate(((1, "g_mix"), (4, "g_ffn"))):
                    g = m.sm2[:, C2[name] + 16 * l:C2[name] + 16 * l + 16].rearrange("p (k s) -> p k s", s=2)
                    ins = STT(m.G[:, a, :, :], m.mod[:, part, :, :], 1.0, g, ALU.add, ALU.mult)
                ins.then_inc(s.mod_ready, 1)
                dve.drain()

                def residual(side):
                    return (lambda k: m.cT[:, k, :]) if side else (lambda k: m.hT[:, k, :])

                def modulated(which, name, sides):
                    for side, n, _ in sides:
                        norm2(f"{name}{l}{side}", KT, n, residual(side),
                              lambda k: m.G[:, which, k, side:side + 1],
                              lambda k: m.mod[:, 3 * which, k, side:side + 1], x_pair(side))

                for step in win_steps(l):
                    if step[0] == "split":
                        next2(S2_WIN + step[1])
                    elif step[0] == "norm":
                        _, name, kt, n, c0 = step
                        side = int(name[-1])
                        dve.drain()
                        if name == "mix01":
                            dve.wait_ge(s.ctx_in, 32)
                        if kt == KT:
                            modulated(0, "mix", [(side, n, c0)])
                        elif kt == 3:
                            norm2(name, 3, n, lambda k: m.cqr[:, k, c0:c0 + n],
                                  lambda k: m.sm2[:, C2["g_q"] + 3 * l + k:C2["g_q"] + 3 * l + k + 1], None,
                                  ((lambda k: m.cqh[:, k, c0:c0 + n]), (lambda k: m.cql[:, k, c0:c0 + n])), FQ)
                        else:
                            norm2(name, 1, n, lambda k: m.ckvr[:, c0:c0 + n],
                                  lambda k: m.sm2[:, C2["g_kv"] + l:C2["g_kv"] + l + 1], None,
                                  ((lambda k: m.ckvh[:, c0:c0 + n]), (lambda k: m.ckvl[:, c0:c0 + n])), FKV)
                    elif step[0] == "tile":
                        _, t, c, side, n, c0 = step
                        ready(t)
                        bank = ps[t % 4]
                        if c < 6:
                            dst = m.cqr[:, c, c0:c0 + n] if c < 3 else (
                                m.ckvr[:, c0:c0 + n] if c == 3 else m.fT[:, c - 4, c0:c0 + n])
                            nc.vector.tensor_copy(dst, bank[:, 0:n]).then_inc(s.acc_free, 1)
                        elif side == 0:
                            TT(m.krr[64:96, 0, 0:T], bank[64:96, :], m.ropes[64:96, 1, :], ALU.mult)
                            TT(m.krr[64:96, 1, 0:T], bank[96:128, :], m.ropes[96:128, 1, :], ALU.mult
                               ).then_inc(s.acc_free, 1)
                            dve.drain()
                            TT(m.krr[64:96, 0, 0:T], m.krr[64:96, 0, 0:T], m.krr[64:96, 1, 0:T], ALU.add)
                        else:
                            nc.vector.tensor_copy(m.krr[64:96, 0, T:TA], bank[64:96, 0:n]).then_inc(s.acc_free, 1)
                            dve.drain()
                            dve.sem_inc(s.kr_ready, 1)
                items = items2(l)
                per = 24 if l == 0 else 20
                with dve.Fori(0, 3) as hg:
                    tile = tl["hg"]
                    for j in range(HG):
                        for side, n, c0 in lat_con:
                            bank = ps[tile % 4]
                            if side == 0:
                                dve.drain()
                            ready(tile + per * hg)
                            if side == 0:
                                TT(m.rt[64:96, 0, :], bank[64:96, :], m.ropes[64:96, 0, :], ALU.mult)
                                TT(m.rt[64:96, 1, :], bank[96:128, :], m.ropes[96:128, 0, :], ALU.mult)
                                dve.drain()
                                dve.wait_ge(s.q4_part, 4 * (3 * l + hg) + j + 1)
                                TT(m.Q4[64:96, j, 0:T], m.rt[64:96, 0, :], m.rt[64:96, 1, :], ALU.add
                                   ).then_inc(s.acc_free, 1)
                            else:
                                TS(m.Q4[0:QH, j, T:TA], bank[0:QH, 0:n], SM, None, ALU.mult).then_inc(s.acc_free, 1)
                            tile += 1
                    next2(S2_HG, hg, 2)
                    for j in range(HG):
                        for side, n, c0 in pieces(l, True):
                            ready(tile + per * hg)
                            nc.vector.tensor_copy(m.K4[0:64, j, c0:c0 + n], ps[tile % 4][0:64, 0:n]
                                                  ).then_inc(s.acc_free, 1)
                            tile += 1
                    for blk in range(6):
                        ready(tile + per * hg)
                        nc.vector.tensor_copy(m.V4[:, blk, :], ps[tile % 4][:, 0:HG * VH]
                                              ).then_inc(s.acc_free, 3 if blk == 5 else 1)
                        tile += 1
                    next2(S2_HG + 1, hg, 2)

                    def item(n):
                        return item_base2(l) + len(items) * hg + n

                    def maximum(n):
                        w = TA if items[n][2] == 0 else TC
                        dve.wait_ge(s.s2_done, item(n) + 3)
                        nc.vector.tensor_reduce(m.nmax2[:, n % 2:n % 2 + 1], psum[:, 1024 * (n % 2):1024 * (n % 2) + w],
                                                AX.X, ALU.max, negate=True).then_inc(s.max2_ready, 1)

                    def copied(n):
                        w = 512 if items[n][2] == 0 else TC
                        dve.wait_ge(s.pv2_done, item(n) + 1)
                        dve.wait_ge(s.t2_done, item(n) + 3)
                        nc.vector.tensor_copy(m.PT2[:, n % 2, 0:w], psum[:, 2048:2048 + w]).then_inc(s.t2_copied, 1)

                    def normalized(n):
                        qb, _, side = items[n]
                        par = n // HG % 2
                        dve.drain()
                        dve.wait_ge(s.pv2_done, item(n) + 3)
                        nc.vector.reciprocal(m.rden2[:, :], m.den2[:, par, :])
                        dve.drain()
                        TT(m.O2[:, 4 * side + qb, bass.ds(hg * (HG * VH), HG * VH)].rearrange("p (h d) -> p h d", d=VH),
                           ps[6 + par][:, 0:HG * VH].rearrange("p (h d) -> p h d", d=VH),
                           m.rden2[:, :].unsqueeze(2).broadcast_to([P, HG, VH]), ALU.mult).then_inc(s.o2_ready, 1)

                    maximum(0)
                    for n in range(len(items)):
                        if n + 1 < len(items):
                            maximum(n + 1)
                        copied(n)
                        if n > HG - 1 and n % HG == 0:
                            normalized(n - 1)
                    normalized(len(items) - 1)
                n, at_ = 12 * l, 16 * l
                for j in range(6):
                    for side, w, _ in lat_con:
                        head, tail = x_pair(side)
                        dve.wait_ge(s.oth_ready, at_ + 1)
                        TT(tail(2 + j), m.ot2[:, n % 2, 0:w], head(2 + j).bitcast(F32), ALU.subtract
                           ).then_inc(s.mixed, 1)
                        n += 1
                        at_ += 1
                f = 4 * l
                for side, w, c0 in lat_con:
                    for c in range(2):
                        dve.wait_ge(s.f2h_ready, f + 1)
                        TT(m.f2l[:, c, c0:c0 + w], m.f2[:, c, 0:w], m.f2h[:, c, c0:c0 + w].bitcast(F32), ALU.subtract
                           ).then_inc(s.f2_split, 1)
                        f += 1
                t = tl["four"]
                for c in range(2):
                    bf = m.sm2[:, C2["b_f"] + 2 * l + c:C2["b_f"] + 2 * l + c + 1]
                    for side, n, _ in lat_con:
                        head, tail = x_pair(side)
                        dve.wait_ge(s.oth_ready, at_ + 1)
                        STT(tail(c), ps[t % 4][:, 0:n], bf, head(c).bitcast(F32), ALU.add, ALU.subtract
                            ).then_inc(s.acc_free, 1)
                        t += 1
                        at_ += 1
                    next2(S2_FOUR + c)
                dve.drain()
                dve.sem_inc(s.mixed, 2 * ns)

                def gated_residual(t, gate, col, side, n, with_squares):
                    h, g = residual(side)(col), m.mod[:, gate, col, side:side + 1]
                    STT(h, ps[t % 4][:, 0:n], g, h, ALU.mult, ALU.add).then_inc(s.acc_free, 1)
                    if with_squares:
                        c0 = T if side else 0
                        total = m.sum2[:, c0:c0 + n]
                        dve.drain()
                        if col == 0:
                            TT(total, h, h, ALU.mult)
                        else:
                            TT(m.sq2[:, 0, 0:n], h, h, ALU.mult)
                            dve.drain()
                            TT(total, total, m.sq2[:, 0, 0:n], ALU.add)

                t = tl["wout"]
                for sl in range(4):
                    for h in range(2):
                        for side, n, _ in lat_con:
                            ready(t)
                            gated_residual(t, 2, 2 * sl + h, side, n, True)
                            t += 1
                    next2(S2_WOUT + sl)
                dve.drain()
                modulated(1, "ffn", lat_con)
                for c, (pair0, pairs, first) in enumerate(FFN_CHUNKS):
                    with dve.Fori(0, pairs // 2) as i:
                        for sl in range(2):
                            for side, n, c0 in lat_con:
                                u = 2 * i + sl
                                at_ = GL_BASE[l] + (8 * c + u) * ns + side
                                for g, buf in ((0, m.cg), (1, m.cv)):
                                    t = tl[f"up{c}"] + sl * 2 * ns + 2 * side + g
                                    bank = ps[t % 4]
                                    tap = lambda k: m.sm2[:, bass.ds(C2["w_dw"] + 132 * l + 44 * k + 22 * g + pair0 + u,
                                                                     1)]
                                    dve.wait_ge(s.mid_ready, 2 * at_ + g + 1)
                                    STT(buf[:, 1:n], bank[:, 0:n - 1], tap(0), buf[:, 1:n], ALU.mult, ALU.add)
                                    dve.drain()
                                    STT(buf[:, 0:n - 1], bank[:, 1:n], tap(2), buf[:, 0:n - 1], ALU.mult, ALU.add
                                        ).then_inc(s.acc_free, 1)
                                if side == ns - 1:
                                    next2(first + sl, i, 2)
                                dve.drain()
                                dve.wait_ge(s.silu_ready, at_ + 1)
                                TT(m.gu[:, 0:n], m.sgl[:, 0:n], m.cv[:, 0:n], ALU.mult).then_inc(s.gu_ready, 1)
                                dve.wait_ge(s.gh_ready, at_ + 1)
                                TT(m.gl[:, bass.ds(u, 1), c0:c0 + n].rearrange("p a n -> p (a n)"), m.gu[:, 0:n],
                                   m.gh[:, bass.ds(u, 1), c0:c0 + n].rearrange("p a n -> p (a n)").bitcast(F32),
                                   ALU.subtract).then_inc(s.gl_ready, 1)
                    for sl in range(4):
                        for g in range(2):
                            for side, n, c0 in lat_con:
                                t = tl[f"down{c}"] + sl * 2 * ns + g * ns + side
                                ready(t)
                                gated_residual(t, 5, 2 * sl + g, side, n, c == len(FFN_CHUNKS) - 1)
                        next2(first + pairs + sl)
                dve.drain()
            last = norm2("final", KT, T, lambda k: m.hT[:, k, :],
                         lambda k: m.sm2[:, C2["g_final"] + k:C2["g_final"] + k + 1])
            last.then_inc(s.final_ready, 1)



def _slab(w):
    kt, n = w.shape[0] // P, w.shape[1]
    out = np.zeros((P, KT, 256), w.dtype)
    out[:, :kt, :n] = w.reshape(kt, P, n).transpose(1, 0, 2)
    return out.reshape(P, SLAB)


def _columns(v):
    return v.reshape(-1, P).T


def _features(x):
    return np.ascontiguousarray(x.T.reshape(-1, P, x.shape[0]).transpose(1, 0, 2))


def _stream_1(w_in, w_a, w_b, w_c, w_o, w_up, w_down, w_ada):
    slabs = []
    for l in range(DEPTH):
        w = w_in[l]
        slabs += [_slab(w[:, c:c + 256]) for c in range(0, 1280, 256)]
        slabs += [_slab(w[:, c:c + 256]) for c in range(COL_BQ, COL_BV + 768, 256)]
        cq = w[:, COL_CQ:COL_CK].reshape(D, 2, 4, HD).transpose(0, 2, 1, 3).reshape(D, 8 * HD)
        slabs += [_slab(cq[:, 0:256]), _slab(cq[:, 256:512]),
                  _slab(w[:, COL_CK:COL_CK + P]), _slab(w[:, COL_CV:COL_CV + P])]
        slabs += [_slab(w_ada[l][:, c:c + 256]) for c in range(0, 6 * D, 256)]
        for c in range(0, D, 256):
            slabs += [_slab(w[:, COL_G + g * D + c:COL_G + g * D + c + 256]) for g in range(3)]
            slabs += [_slab(np.concatenate([w_a[l][:, c:c + 256], w_b[l][:, c:c + 256]])), _slab(w_c[l][:, c:c + 256])]
        slabs += [_slab(w_o[l][:, c:c + 256]) for c in range(0, D, 256)]
        for q in range(0, D_FF, D):
            slabs += [_slab(w_up[l][:, q + c:q + c + 256]) for c in range(0, D, 256)]
            slabs += [_slab(w_down[l][q:q + D, c:c + 256]) for c in range(0, D, 256)]
    return slabs


def _arrays_1(x, positions, attn_norm, w_in, idx_k_norm, sinks, w_a, w_b, w_c, w_o, mlp_norm, w_up, w_down,
              final_norm, c, c_ctx):
    small = np.zeros((P, 74), np.float32)
    small[:, 0:16] = _columns(attn_norm)
    small[:, 16:32] = _columns(mlp_norm)
    small[:, 32:40] = _columns(final_norm)
    small[:HD, 40:42] = idx_k_norm.T
    small[:, 42:58] = sinks.reshape(1, -1)
    small[:, 58:74] = np.stack([_columns(c), _columns(c_ctx)], axis=2).reshape(P, 16)
    return {
        "x_t": _features(x[0]), "pos": np.ascontiguousarray(np.broadcast_to(positions[0], (P, T))),
        "small_1": small, **shape_constants(),
    }


def _stream_2(w_in, w_fourier, w_q_b, w_kv_b, w_out, w_up, w_down):
    slabs = []
    for l in range(DEPTH):
        w = w_in[l]
        kr = np.zeros((D, P), w.dtype)
        kr[:, 64:96] = w[:, 768:800]
        kr[:, 96:112], kr[:, 112:128] = w[:, 784:800], w[:, 768:784]
        slabs += [_slab(w[:, c:c + 256]) for c in (256, 512, 0)] + [_slab(kr)]
        q = w_q_b[l].reshape(FQ, KH, QH)
        q = np.concatenate([q, q[:, :, 80:96], q[:, :, 64:80]], axis=2)
        kv = w_kv_b[l].reshape(FKV, KH, P)
        for h in range(0, KH, HG):
            a = np.zeros((P, SLAB), w.dtype)
            a[:, :3 * 512] = q[:, h:h + HG].reshape(3, P, 512).transpose(1, 0, 2).reshape(P, 3 * 512)
            b = np.zeros((P, SLAB), w.dtype)
            b[:, :512] = kv[:, h:h + HG].reshape(P, 512)
            slabs += [a, b]
        slabs += [_slab(w_fourier[l][:, c:c + P]) for c in (0, P)]
        slabs += [_slab(w_out[l][:, c:c + 256]) for c in range(0, D, 256)]
        for pair0, pairs, _ in FFN_CHUNKS:
            for u in range(pair0, pair0 + pairs):
                slabs.append(_slab(np.concatenate([w_up[l][:, u * P:(u + 1) * P],
                                                   w_up[l][:, FF2 + u * P:FF2 + (u + 1) * P]], axis=1)))
            rows = w_down[l][pair0 * P:(pair0 + pairs) * P]
            slabs += [_slab(rows[:, c:c + 256]) for c in range(0, D, 256)]
    return slabs


def _arrays_2(ctx, b_ada, g_mix, b_fourier, g_q_a, g_kv_a, g_ffn, w_dw, b_dw, g_final):
    twice = lambda v: np.repeat(_columns(v), 2, axis=1)
    parts = {
        "b_ada": twice(b_ada), "g_mix": twice(g_mix), "g_ffn": twice(g_ffn), "g_final": _columns(g_final),
        "b_f": _columns(b_fourier), "g_q": _columns(g_q_a), "g_kv": _columns(g_kv_a), "w_dw": _columns(w_dw),
        "b_dw": _columns(b_dw),
    }
    small = np.concatenate([parts[name] for name in C2], axis=1)
    assert small.shape[1] == SMALL2
    return {"small_2": small, "ctx_t": _features(ctx[0]), **shape_constants_2()}


def kernel(**inputs):
    import concourse.bacc as bacc
    from concourse.bass_utils import run_bass_kernel_spmd

    a = {k: np.asarray(v) for k, v in inputs.items()}
    arrays = _arrays_1(*[a[k] for k in ("x", "positions", "attn_norm", "w_in", "idx_k_norm", "sinks", "w_a", "w_b",
                                        "w_c", "w_o", "mlp_norm", "w_up", "w_down", "final_norm", "c_2",
                                        "c_ctx_2")])
    arrays.update(_arrays_2(*[a[k + "_2"] for k in ("ctx", "b_ada", "g_mix", "b_fourier", "g_q_a",
                                                    "g_kv_a", "g_ffn", "w_dw", "b_dw", "g_final")]))
    slabs = _stream_1(*[a[k] for k in ("w_in", "w_a", "w_b", "w_c", "w_o", "w_up", "w_down", "w_ada_2")])
    slabs += _stream_2(*[a[k + "_2"] for k in ("w_in", "w_fourier", "w_q_b", "w_kv_b", "w_out", "w_up",
                                               "w_down")])
    assert len(slabs) == SLABS_ALL
    arrays["weights"] = np.stack(slabs)
    nc = bacc.Bacc("TRN2", target_bir_lowering=False, num_devices=1)
    io = {}
    for name, v in arrays.items():
        io[name] = nc.dram_tensor(name, v.shape, mybir.dt.from_np(v.dtype), kind="ExternalInput").ap()
    out = nc.dram_tensor("out", (P, KT, T), F32, kind="ExternalOutput").ap()
    two_stacks(nc, io, out)
    r = run_bass_kernel_spmd(nc, [arrays], core_ids=[0])
    return np.ascontiguousarray(r.results[0]["out"].transpose(2, 1, 0)).reshape(1, T, D)
```
